# Optimizing a Trainium2 kernel written in Bass

```python
import jax, jax.numpy as jnp
from jax import lax
import numpy as np

D_MODEL = 1024
BATCH = 1
SEQ = 512
DEPTH = 1
DEC_BATCH = 8
DEC_SEQ = 1
PAST_LEN = 2048
PAGE_SIZE = 128

HEAD_DIM = 64
GDN_HEADS = 8
FOX_HEADS = 8
GDN_WIDTH = GDN_HEADS * HEAD_DIM
FOX_WIDTH = FOX_HEADS * HEAD_DIM
MIX_WIDTH = GDN_WIDTH + FOX_WIDTH
CONV_WIDTH = 4
GDN_CHUNK = 64
FOX_BLOCK = 128
PROJ_SPLITS = (GDN_WIDTH, GDN_WIDTH, GDN_WIDTH, GDN_WIDTH, GDN_HEADS, GDN_HEADS, FOX_WIDTH, FOX_WIDTH, FOX_WIDTH, FOX_HEADS)
PROJ_WIDTH = 4 * GDN_WIDTH + 2 * GDN_HEADS + 3 * FOX_WIDTH + FOX_HEADS
PEER_HEADS = 8
N_KEYS = 128
N_EXPERTS = N_KEYS * N_KEYS
PEER_TOPK = 16
PEER_DK_HALF = 128
PEER_BLOCK = 256
N_MOD = 6
EPS = 1e-6

kernel_name = 'hymba_gdn_fox_peer_adaln_step'

def rms(x):
    xf = x.astype(jnp.float32)
    return xf * lax.rsqrt(jnp.mean(xf * xf, axis=-1, keepdims=True) + EPS)

def modulate(x, shift, scale):
    y = rms(x) * (1.0 + scale[:, None, :].astype(jnp.float32)) + shift[:, None, :].astype(jnp.float32)
    return y.astype(x.dtype)

def l2norm(x):
    return x * lax.rsqrt(jnp.sum(x * x, axis=-1, keepdims=True) + 1e-6)

def causal_conv(u, buf, w):
    xp = jnp.concatenate([buf.astype(u.dtype), u], axis=1)
    out = lax.conv_general_dilated(xp, w[:, None, :].astype(u.dtype), window_strides=(1,), padding='VALID',
                                   dimension_numbers=('NWC', 'WIO', 'NWC'), feature_group_count=u.shape[-1])
    return out, xp[:, xp.shape[1] - (CONV_WIDTH - 1):]

def gated_delta_chunked(q, k, v, g, beta, s0):
    B, L, H, _ = q.shape
    DV = v.shape[-1]
    C = GDN_CHUNK if L >= GDN_CHUNK else L
    Lp = -(-L // C) * C
    pad = Lp - L

    def to_chunks(t):
        t = jnp.pad(t, [(0, 0), (0, pad)] + [(0, 0)] * (t.ndim - 2))
        t = t.reshape((B, Lp // C, C) + t.shape[2:])
        return jnp.moveaxis(jnp.moveaxis(t, 1, 0), 3, 2)

    qc, kc, vc, gc, bc = to_chunks(q), to_chunks(k), to_chunks(v), to_chunks(g), to_chunks(beta)
    G = jnp.cumsum(gc, axis=-1)
    causal = jnp.tril(jnp.ones((C, C), dtype=bool))
    strict = jnp.tril(jnp.ones((C, C), dtype=bool), k=-1)
    decay = jnp.exp(jnp.where(causal, G[..., :, None] - G[..., None, :], -jnp.inf))
    A = jnp.where(strict, bc[..., :, None] * jnp.einsum('nbhcd,nbhed->nbhce', kc, kc) * decay, 0.0)
    rhs = jnp.concatenate([vc * bc[..., None], kc * (bc * jnp.exp(G))[..., None]], axis=-1)
    sol = lax.linalg.triangular_solve(A, rhs, left_side=True, lower=True, unit_diagonal=True)
    Uc, Wc = sol[..., :DV], sol[..., DV:]
    Aqk = jnp.einsum('nbhcd,nbhed->nbhce', qc, kc) * decay
    qG = qc * jnp.exp(G)[..., None]
    kG = kc * jnp.exp(G[..., -1:] - G)[..., None]
    gl = jnp.exp(G[..., -1])

    def step(S, xs):
        Ui, Wi, Ai, qi, ki, gi = xs
        vn = Ui - jnp.einsum('bhcd,bhde->bhce', Wi, S)
        o = jnp.einsum('bhcd,bhde->bhce', qi, S) + jnp.einsum('bhcs,bhse->bhce', Ai, vn)
        S = S * gi[..., None, None] + jnp.einsum('bhcd,bhce->bhde', ki, vn)
        return S, o

    S, o = lax.scan(step, s0, (Uc, Wc, Aqk, qG, kG, gl))
    o = jnp.moveaxis(jnp.moveaxis(o, 2, 3), 0, 1).reshape(B, Lp, H, DV)[:, :L]
    return o, S

def fox_attend(q, k, v, Fq, Fk, q_pos, k_pos):
    s = jnp.einsum('bqhd,bkhd->bhqk', q, k).astype(jnp.float32) * (HEAD_DIM ** -0.5)
    s = s + jnp.swapaxes(Fq, 1, 2)[..., :, None] - jnp.swapaxes(Fk, 1, 2)[..., None, :]
    s = jnp.where(k_pos[None, :] <= q_pos[:, None], s, -jnp.inf)
    p = jax.nn.softmax(s, axis=-1)
    return jnp.einsum('bhqk,bkhd->bqhd', p.astype(v.dtype), v)

def fox_prompt(q, k, v, F):
    B, L, H, Dh = q.shape
    nb = L // FOX_BLOCK
    qb = jnp.swapaxes(q.reshape(B, nb, FOX_BLOCK, H, Dh), 0, 1)
    Fb = jnp.swapaxes(F.reshape(B, nb, FOX_BLOCK, H), 0, 1)
    starts = jnp.arange(nb) * FOX_BLOCK
    k_pos = jnp.arange(L)

    def one(args):
        qi, Fi, st = args
        return fox_attend(qi, k, v, Fi, F, st + jnp.arange(FOX_BLOCK), k_pos)

    o = lax.map(one, (qb, Fb, starts))
    return jnp.swapaxes(o, 0, 1).reshape(B, L, H, Dh)

def token_mixers(h, w_in, conv_w, a_log, dt_bias, gdn_norm_w, fox_fb, w_out, conv_buf, s0, past):
    B, L, _ = h.shape
    proj = h @ w_in
    gq, gk, gv, gz, ga, gb, fq, fk, fv, ff = jnp.split(proj, np.cumsum(PROJ_SPLITS)[:-1].tolist(), axis=-1)
    qkv, new_buf = causal_conv(jnp.concatenate([gq, gk, gv], axis=-1), conv_buf, conv_w)
    cq, ck, cv = jnp.split(jax.nn.silu(qkv), 3, axis=-1)
    q = l2norm(cq.reshape(B, L, GDN_HEADS, HEAD_DIM).astype(jnp.float32)) * (HEAD_DIM ** -0.5)
    k = l2norm(ck.reshape(B, L, GDN_HEADS, HEAD_DIM).astype(jnp.float32))
    v = cv.reshape(B, L, GDN_HEADS, HEAD_DIM).astype(jnp.float32)
    beta = jax.nn.sigmoid(gb.astype(jnp.float32))
    g = -jnp.exp(a_log.astype(jnp.float32)) * jax.nn.softplus(ga.astype(jnp.float32) + dt_bias.astype(jnp.float32))
    o, S = gated_delta_chunked(q, k, v, g, beta, s0.astype(jnp.float32))
    o = rms(o) * gdn_norm_w.astype(jnp.float32) * jax.nn.silu(gz.reshape(B, L, GDN_HEADS, HEAD_DIM).astype(jnp.float32))
    o_gdn = o.reshape(B, L, GDN_WIDTH).astype(h.dtype)
    fq = fq.reshape(B, L, FOX_HEADS, HEAD_DIM)
    fk = fk.reshape(B, L, FOX_HEADS, HEAD_DIM)
    fv = fv.reshape(B, L, FOX_HEADS, HEAD_DIM)
    logf = jax.nn.log_sigmoid((ff + fox_fb).astype(jnp.float32))
    if past is None:
        o_fox = fox_prompt(fq, fk, fv, jnp.cumsum(logf, axis=1))
    else:
        k_past, v_past, logf_past = past
        P = k_past.shape[1]
        k_all = jnp.concatenate([k_past.astype(fk.dtype), fk], axis=1)
        v_all = jnp.concatenate([v_past.astype(fv.dtype), fv], axis=1)
        F = jnp.cumsum(jnp.concatenate([logf_past.astype(jnp.float32), logf], axis=1), axis=1)
        o_fox = fox_attend(fq, k_all, v_all, F[:, P:], F, P + jnp.arange(L), jnp.arange(P + L))
    y = jnp.concatenate([o_gdn, o_fox.reshape(B, L, FOX_WIDTH).astype(h.dtype)], axis=-1) @ w_out
    dt = h.dtype
    return y, (fk.astype(dt), fv.astype(dt), logf.astype(dt), new_buf.astype(dt), S.astype(dt))

def peer(h, wq, subkeys, pu, pv):
    B, L, D = h.shape
    n = B * L
    blk = min(PEER_BLOCK, n)
    nb = -(-n // blk)
    xs = jnp.pad(h.reshape(n, D), ((0, nb * blk - n), (0, 0))).reshape(nb, blk, D)

    def one(xb):
        q = (xb @ wq).reshape(blk, PEER_HEADS, 2, PEER_DK_HALF)
        s = jnp.einsum('thpc,hpnc->thpn', q, subkeys).astype(jnp.float32)
        sv, si = lax.top_k(s, PEER_TOPK)
        cand = (sv[:, :, 0, :, None] + sv[:, :, 1, None, :]).reshape(blk, PEER_HEADS, PEER_TOPK * PEER_TOPK)
        cidx = (si[:, :, 0, :, None] * N_KEYS + si[:, :, 1, None, :]).reshape(blk, PEER_HEADS, PEER_TOPK * PEER_TOPK)
        fv, fi = lax.top_k(cand, PEER_TOPK)
        eidx = jnp.take_along_axis(cidx, fi, axis=-1)
        gate = jax.nn.softmax(fv, axis=-1)
        act = jax.nn.gelu(jnp.einsum('thkd,td->thk', pu[eidx], xb).astype(jnp.float32), approximate=False) * gate
        return jnp.einsum('thk,thkd->td', act.astype(xb.dtype), pv[eidx])

    out = lax.map(one, xs)
    return out.reshape(nb * blk, D)[:n].reshape(B, L, D)

def layer(x, c, w_mod, b_mod, w_in, conv_w, a_log, dt_bias, gdn_norm_w, fox_fb, w_out,
          peer_wq, peer_subkeys, peer_u, peer_v, conv_buf, s0, past):
    mod = jax.nn.silu(c) @ w_mod + b_mod
    sh1, sc1, g1, sh2, sc2, g2 = jnp.split(mod, N_MOD, axis=-1)
    m, st = token_mixers(modulate(x, sh1, sc1), w_in, conv_w, a_log, dt_bias, gdn_norm_w, fox_fb, w_out,
                         conv_buf, s0, past)
    x = x + g1[:, None, :] * m
    x = x + g2[:, None, :] * peer(modulate(x, sh2, sc2), peer_wq, peer_subkeys, peer_u, peer_v)
    return x, st

def setup_inputs(seed: int = 0) -> dict:
    key = jax.random.key(seed)
    ks = jax.random.split(key, 24)
    n_pages = PAST_LEN // PAGE_SIZE
    n_used = DEC_BATCH * n_pages
    n_pool = (n_used * 5) // 4
    nrm = jax.random.normal
    page_table = jax.random.permutation(ks[0], n_pool)[:n_used].reshape(DEC_BATCH, n_pages).astype(jnp.int32)
    dt = jnp.exp(jax.random.uniform(ks[1], (DEPTH, GDN_HEADS), minval=np.log(1e-3), maxval=np.log(1e-1)))
    return {
        'x_prompt': nrm(ks[2], (BATCH, SEQ, D_MODEL), jnp.float32),
        'x_sample': nrm(ks[3], (DEC_BATCH, DEC_SEQ, D_MODEL), jnp.float32),
        'cache_k': nrm(ks[4], (DEPTH, n_pool, PAGE_SIZE, FOX_HEADS, HEAD_DIM), jnp.float32),
        'cache_v': nrm(ks[5], (DEPTH, n_pool, PAGE_SIZE, FOX_HEADS, HEAD_DIM), jnp.float32),
        'cache_logf': jax.nn.log_sigmoid(3.0 + 0.5 * nrm(ks[6], (DEPTH, n_pool, PAGE_SIZE, FOX_HEADS), jnp.float32)),
        'state_conv': nrm(ks[7], (DEPTH, DEC_BATCH, CONV_WIDTH - 1, 3 * GDN_WIDTH), jnp.float32),
        'state_delta': 0.1 * nrm(ks[8], (DEPTH, DEC_BATCH, GDN_HEADS, HEAD_DIM, HEAD_DIM), jnp.float32),
        'page_table': page_table,
        'c_prompt': nrm(ks[9], (BATCH, D_MODEL), jnp.float32),
        'c_sample': nrm(ks[10], (DEC_BATCH, D_MODEL), jnp.float32),
        'w_mod': nrm(ks[11], (DEPTH, D_MODEL, N_MOD * D_MODEL), jnp.float32) * D_MODEL ** -0.5,
        'b_mod': 0.02 * nrm(ks[12], (DEPTH, N_MOD * D_MODEL), jnp.float32),
        'w_in': nrm(ks[13], (DEPTH, D_MODEL, PROJ_WIDTH), jnp.float32) * D_MODEL ** -0.5,
        'conv_w': 0.5 * nrm(ks[14], (DEPTH, CONV_WIDTH, 3 * GDN_WIDTH), jnp.float32),
        'a_log': jnp.log(jax.random.uniform(ks[15], (DEPTH, GDN_HEADS), minval=1.0, maxval=16.0)),
        'dt_bias': dt + jnp.log(-jnp.expm1(-dt)),
        'gdn_norm_w': 1.0 + 0.02 * nrm(ks[16], (DEPTH, HEAD_DIM), jnp.float32),
        'fox_fb': 2.0 + 0.5 * nrm(ks[17], (DEPTH, FOX_HEADS), jnp.float32),
        'w_out': nrm(ks[18], (DEPTH, MIX_WIDTH, D_MODEL), jnp.float32) * MIX_WIDTH ** -0.5,
        'peer_wq': nrm(ks[19], (DEPTH, D_MODEL, PEER_HEADS * 2 * PEER_DK_HALF), jnp.float32) * D_MODEL ** -0.5,
        'peer_subkeys': nrm(ks[20], (DEPTH, PEER_HEADS, 2, N_KEYS, PEER_DK_HALF), jnp.float32) * PEER_DK_HALF ** -0.5,
        'peer_u': nrm(ks[21], (DEPTH, N_EXPERTS, D_MODEL), jnp.float32) * D_MODEL ** -0.5,
        'peer_v': nrm(ks[22], (DEPTH, N_EXPERTS, D_MODEL), jnp.float32) * PEER_HEADS ** -0.5,
        'final_norm_w': 1.0 + 0.02 * nrm(ks[23], (D_MODEL,), jnp.float32),
    }

def reference(x_prompt, x_sample, cache_k, cache_v, cache_logf, state_conv, state_delta, page_table,
              c_prompt, c_sample, w_mod, b_mod, w_in, conv_w, a_log, dt_bias, gdn_norm_w, fox_fb, w_out,
              peer_wq, peer_subkeys, peer_u, peer_v, final_norm_w):
    Bp = x_prompt.shape[0]
    Bs = x_sample.shape[0]
    n_pages = page_table.shape[1]
    xp, xs = x_prompt, x_sample
    st_p, st_s = [], []
    for l in range(DEPTH):
        lw = (w_mod[l], b_mod[l], w_in[l], conv_w[l], a_log[l], dt_bias[l], gdn_norm_w[l], fox_fb[l], w_out[l],
              peer_wq[l], peer_subkeys[l], peer_u[l], peer_v[l])
        buf0 = jnp.zeros((Bp, CONV_WIDTH - 1, 3 * GDN_WIDTH), x_prompt.dtype)
        s00 = jnp.zeros((Bp, GDN_HEADS, HEAD_DIM, HEAD_DIM), jnp.float32)
        xp, sp = layer(xp, c_prompt, *lw, buf0, s00, None)
        st_p.append(sp)
        k_past = cache_k[l][page_table].reshape(Bs, n_pages * PAGE_SIZE, FOX_HEADS, HEAD_DIM)
        v_past = cache_v[l][page_table].reshape(Bs, n_pages * PAGE_SIZE, FOX_HEADS, HEAD_DIM)
        f_past = cache_logf[l][page_table].reshape(Bs, n_pages * PAGE_SIZE, FOX_HEADS)
        xs, ss = layer(xs, c_sample, *lw, state_conv[l], state_delta[l], (k_past, v_past, f_past))
        st_s.append(ss)
    fw = final_norm_w.astype(jnp.float32)
    y_prompt = (rms(xp) * fw).astype(x_prompt.dtype)
    y_sample = (rms(xs) * fw).astype(x_sample.dtype)
    k_prompt = jnp.stack([s[0] for s in st_p])
    v_prompt = jnp.stack([s[1] for s in st_p])
    logf_prompt = jnp.stack([s[2] for s in st_p])
    conv_prompt = jnp.stack([s[3] for s in st_p])
    delta_prompt = jnp.stack([s[4] for s in st_p])
    k_sample = jnp.stack([s[0] for s in st_s])
    v_sample = jnp.stack([s[1] for s in st_s])
    logf_sample = jnp.stack([s[2] for s in st_s])
    conv_sample = jnp.stack([s[3] for s in st_s])
    delta_sample = jnp.stack([s[4] for s in st_s])
    return (y_prompt, y_sample, k_prompt, v_prompt, logf_prompt, conv_prompt, delta_prompt,
            k_sample, v_sample, logf_sample, conv_sample, delta_sample)


_drawn_inputs = setup_inputs


def setup_inputs(seed=0):
    import zlib

    import numpy as np

    out = dict(_drawn_inputs(seed))
    spreads = {}
    factors = {'cache_logf': 15.725, 'gdn_norm_w': 11.929, 'final_norm_w': 8.364}
    for name, (base, spread) in spreads.items():
        noise = np.random.default_rng([zlib.crc32(name.encode()), seed]).standard_normal(out[name].shape)
        drawn = base * np.exp(spread * noise) if base else spread * noise
        out[name] = __import__('jax').numpy.asarray(drawn.astype(out[name].dtype))
    for name, factor in factors.items():
        out[name] = (out[name] * factor).astype(out[name].dtype)
    return out
```

```python
from contextlib import ExitStack

import concourse.bass as bass
from concourse import mybir

F32 = mybir.dt.float32
U32 = mybir.dt.uint32
I32 = mybir.dt.int32
ALU = mybir.AluOpType
ACT = mybir.ActivationFunctionType
AXX = mybir.AxisListType.X

P = 128
D_MODEL, SEQ, NB = 1024, 512, 8
HEADS, HD = 8, 64
WID = HEADS * HD
PAGES = 16
KT = D_MODEL // P
TILES = SEQ // P
TOK = SEQ + NB
CONV = 3 * WID
TAPS = 4
NEXP, NKEY, TOPK, PH = 16384, 128, 16, 8
NEG = -1.0e30
EPS = 1e-6
LOOP_STEPS = 142
COL_Q, COL_K, COL_V, COL_Z, COL_AB, COL_FQ, COL_FK, COL_FV = 0, 512, 1024, 1536, 2048, 2064, 2576, 3088
PROJ = 3608
SLOTW = 528


def hybrid_decoder_step(nc, a, o):
    ctx = ExitStack()
    with ctx:
        sems = {}

        def S(name):
            if name not in sems:
                sems[name] = ctx.enter_context(nc.semaphore(name))
            return sems[name]

        def sb(name, shape, dt=F32):
            return ctx.enter_context(nc.sbuf_tensor(name, shape, dt))

        def dram(name, shape):
            return nc.dram_tensor(name, shape, F32, kind="Internal").ap()

        ident = sb("ident", [P, P])
        ones = sb("ones", [P, P])
        upper = sb("upper", [P, P])
        lower = sb("lower", [P, P])
        hide_q = sb("hide_q", [P, P])
        hide_e = sb("hide_e", [P, P])
        level = sb("level", [P, 7, P])
        small = sb("small", [P, 1024])
        RING = sb("RING", [P, 3, KT * SLOTW])
        HT = sb("HT", [P, KT, TOK])
        MV = sb("MV", [P, 4, D_MODEL])
        RQ64 = sb("RQ64", [P, 328])
        R1 = sb("R1", [P, 14336])
        R2 = sb("R2", [P, 14700])
        banks = [ctx.enter_context(nc.psum_tensor(f"bank{i}", [P, 512], F32)) for i in range(8)]

        def part(_t, _at, _n, /, **dims):
            v = _t[:, _at:_at + _n]
            if not dims:
                return v
            names = list(dims)
            return v.rearrange(f"row ({' '.join(names)}) -> row {' '.join(names)}", **{k: dims[k] for k in names[1:]})

        GT = part(R1, 0, 6144, t=TILES, c=CONV)
        GZ = part(R1, 6144, 2048, t=TILES, c=WID)
        VT = part(R1, 8192, 2048, t=TILES, c=WID)
        FQ = part(R1, 10240, 2048, j=4, t=SEQ)
        FK = part(R1, 12288, 2048, j=4, t=SEQ)

        C9 = R2[:, 0:1024]
        SC9 = R2[:, 1024:2048]
        KO = part(R2, 0, 1024, n=2, c=512)
        XR = part(R2, 2048, 2048, n=2, c=1024)
        HJ = part(R2, 4096, 2048, n=2, c=1024)
        PS = R2[:, 2048:2048 + PROJ]
        RAW = part(R2, 6144, 1032, n=2, c=516)
        CACC = part(R2, 7176, 1024, n=2, c=512)
        CACT = part(R2, 8200, 1024, n=2, c=512)
        ints = R2[:, 7176:7688].bitcast(I32).rearrange("p (n c) -> p n c", n=4)
        SCW = part(R2, 0, 2048, n=4, c=512)
        SST = part(R2, 6144, 1536, n=3, c=512)
        STMP = R2[:, 7680:8192]
        PSC = R2[:, 9224:9224 + CONV]
        TAILO = R2[:, 10760:10760 + CONV]
        FA = part(R2, 0, 1024, n=2, c=512)
        FB = part(R2, 1024, 1024, n=2, c=512)
        PR = part(R2, 2048, 1024, n=2, c=512)
        PT = part(R2, 3072, 1024, n=2, c=512)
        SS0 = part(R2, 4096, 4096, k=HD, v=HD)
        SSP = part(R2, 8192, 4096, k=HD, v=HD)
        SV = part(R2, 12288, 320, n=5, c=HD)
        QGT_, KB_, KBG_, KG_ = (R2[:, i * 512:(i + 1) * 512] for i in range(4))
        SQ = R2[:, 0:1024]
        TQ, TK, TKB, TQG = (part(R2, 2048 + i * 512, 512, j=4, c=P) for i in range(4))
        BATCH = [[part(R2, 4096 + b * 3584 + i * 512, 512, m=4, c=P) for i in range(7)] for b in range(2)]
        WT = part(MV[:, 0, :], 0, 512, j=4, c=P)
        VN = part(R2, 11628, 512, h=8, d=HD)
        ST = part(R2, 12652 - 512, 512, j=4, d=P)
        EX = MV[:, 3, 0:512]
        KG4 = [R1[:, 8192:10240].rearrange("p (g c) -> p g c", g=4), R1[:, 12288:14336].rearrange("p (g c) -> p g c", g=4)]
        SLOT2 = RING[:, 2, :]
        SC = part(SLOT2, 0, 1088, h=HEADS, b=NB, g=17)
        LG = SLOT2[:, 1088:2112]
        LP = part(SLOT2, 2112, 1024, h=HEADS, b=NB, g=PAGES)
        QB = part(SLOT2, 3136, 1024, n=2, c=512)
        VNEW = MV[0:1, 2, :]
        X1 = part(R2, 0, 5120, t=5, d=D_MODEL)
        TMPX = part(R2, 5120, 1024, n=2, c=512)
        H2 = part(R2, 6144, 5120, t=5, d=D_MODEL)
        QT = part(R1, 0, 16 * TOK, b=16, t=TOK)
        KEYT = part(R1, 8320, 2048, b=16, n=P)
        MVS2 = part(R1, 12288, 2048, n=2, d=D_MODEL)
        SCS = R1[:, 12288:14336]
        KN = part(SLOT2, 0, 2048, b=16, c=P)
        FLAT = RING[:, :, :].rearrange("p s n -> p (s n)")
        UR = part(FLAT, 0, 4096, n=4, d=D_MODEL)
        VR = part(FLAT, 4096, 8192, n=8, d=D_MODEL)
        ACC = HT[:, :, :].rearrange("p k t -> p (k t)")[:, 0:4096].rearrange("p (t d) -> p t d", t=TILES)
        SX = part(R1, 10368, 256, p=2, n=P)
        CAND = R1[:, 10624:10880]
        V16 = part(R1, 10880, 32, p=2, n=16)
        I16 = R1[:, 10912:10944].bitcast(U32).rearrange("q (p n) -> q p n", p=2)
        IF = part(R1, 10944, 32, p=2, n=16)
        FI = R1[:, 10976:10992].bitcast(U32)
        IJ = R1[:, 10992:11024].bitcast(U32).rearrange("q (p n) -> q p n", p=2)
        IJF = part(R1, 11024, 32, p=2, n=16)
        R01 = part(R1, 11056, 32, p=2, n=16)
        OH = part(R1, 11088, 512, p=2, k=16, n=16)
        FVT = R1[:, 11600:11616]
        EIX = R2[:, 11264:11328].bitcast(U32).rearrange("q (t n) -> q t n", t=4)
        FVS = part(R2, 11328, 64, t=4, n=16)
        DOT = part(R2, 11392, 64, t=4, n=16)
        AG = part(R2, 11456, 64, t=4, n=16)
        GAT = part(R2, 11520, 64, t=4, n=16)
        SUMG = R2[:, 11584:11588]
        NMX = R2[:, 11588:11592]
        DG = part(R2, 11628, 512, n=4, c=P)
        EISF = R2[:, 12652:12780]
        FVSS = R2[:, 12780:12908]
        IXT = R2[:, 12908:12916].bitcast(U32)
        GTT = R2[:, 12916:12924]
        DOTS = R2[:, 12924:12932]
        AM = R2[:, 12932:12996]
        H2B = part(R1, 12288, 2048, n=2, d=D_MODEL)
        IOTA16 = small[:, 847:863]
        IOTAI = small[:, 863:879].bitcast(I32)
        BMR = part(R2, 12652, 1024, n=2, c=512)
        MR = part(R2, 13676, 1024, n=2, c=512)

        CT = part(small, 0, 72, k=KT, n=9)
        CW = part(small, 72, 48, j=TAPS, b=12)
        BIAS = part(small, 120, 24, n=3, h=8)
        GATE = part(small, 144, 120, t=5, n=24)
        TAILI = part(small, 264, 36, b=12, n=3)
        BETA = part(small, 300, 40, t=5, h=8)
        G = part(small, 340, 40, t=5, h=8)
        LOGF = part(small, 380, 40, t=5, h=8)
        GW = part(small, 420, 120, t=5, n=24)
        SS = small[:, 540:560]
        FR = MV[:, 2, 0:512]
        NFR = MV[:, 2, 512:1024]
        RS = small[:, 562:594]
        NM = small[:, 594:626]
        RI = small[:, 626:658]
        GC = part(small, 658, 32, t=4, h=8)
        EG = part(small, 690, 32, t=4, h=8)
        GL = part(small, 722, 32, t=4, h=8)
        EKG = part(small, 754, 32, t=4, h=8)
        NBG = part(small, 786, 32, t=4, h=8)
        RQ = small[:, 818:834]
        TDG = small[:, 896:960]
        SRCP = small[:, 960:1024]
        SMX = small[:, 846:847]
        PTI = small[:, 834:835].bitcast(U32)
        SSM = small[:, 836:846]
        LNB = RQ64[:, 0:64]
        M64 = RQ64[:, 64:128]
        SN = RQ64[:, 128:136]
        OGS = MV[0:NB, 3, 512:1024]
        NW = RQ64[:, 136:200]
        PTB = RQ64[0:1, 200:328].bitcast(I32)
        CWN = small[0:48, 896:1024]
        EPSB = small[:, 561:562]

        def SRAW(g):
            return PS[0:NB, g * 512:(g + 1) * 512]

        def SCONV(g):
            return PSC[0:NB, g * 512:(g + 1) * 512]

        def wide(v, n):
            return v.rearrange("p (m o) -> p m o", o=1).to_broadcast([v.shape[0], v.shape[1], n])

        def FOUR(m):
            return m[:, :].rearrange("p (o c) -> p o c", o=1).to_broadcast([P, 4, P])

        def fox_out(j):
            return (EX if j == 0 else FQ[:, j - 1, :]).rearrange("p (t c) -> p t c", t=TILES)

        samp_d = dram("samp_d", [NB, 6, 512])
        sgate_d = dram("sgate_d", [3, NB, 8])
        frow_d = dram("frow_d", [2, 8, SEQ])
        h2s_d = dram("h2s_d", [NB, D_MODEL])
        mod_d = dram("mod_d", [9, 6 * D_MODEL])
        drams = {}

        pools = {"A": [0, 1, 2, 3], "D": [4, 5, 6, 7]}
        taken = {"A": 0, "D": 0}
        job_of = {}
        newest = [None]
        last_job = []

        def take_bank(job, pool):
            n = taken[pool]
            taken[pool] += 1
            b = pools[pool][n % 4]
            if n >= 4:
                nc.tensor.wait_ge(S(f"bank{b}_free"), n // 4)
            job_of[job] = (b, n // 4 + 1)
            newest[0] = job
            return banks[b]

        def full_bank(eng, job):
            b, use = job_of[job]
            eng.wait_ge(S(f"bank{b}_full"), use)
            return banks[b]

        def job_done(eng, job):
            b, use = job_of[job]
            eng.wait_ge(S(f"bank{b}_full"), use)

        def job_read(eng, job):
            b, use = job_of[job]
            eng.wait_ge(S(f"bank{b}_free"), use)

        def full(job):
            return S(f"bank{job_of[job][0]}_full")

        def free(job):
            return S(f"bank{job_of[job][0]}_free")

        w_mod = a["w_mod"][0].rearrange("(k p) n -> p k n", p=P)
        w_in = a["w_in"][0].rearrange("(k p) n -> p k n", p=P)
        w_out = a["w_out"][0].rearrange("(k p) n -> p k n", p=P)
        wq = a["peer_wq"][0].rearrange("(k p) n -> p k n", p=P)
        chunks = [(f"mod{j}", w_mod[:, :, j * 512:(j + 1) * 512]) for j in range(4)]
        chunks += [("fv", w_in[:, :, COL_FV:PROJ]), ("gz", w_in[:, :, COL_Z:COL_FQ]),
                   ("fq", w_in[:, :, COL_FQ:COL_FK]), ("fk", w_in[:, :, COL_FK:COL_FV]),
                   ("gq", w_in[:, :, 0:512]), ("gk", w_in[:, :, 512:1024]), ("gv", w_in[:, :, 1024:1536])]
        chunks += [(f"mod{j}", w_mod[:, :, j * 512:(j + 1) * 512]) for j in range(4, 12)]
        chunks += [(f"wo{j}", w_out[:, :, j * 512:(j + 1) * 512]) for j in range(2)]
        chunks += [(f"wq{j}", wq[:, :, j * 512:(j + 1) * 512]) for j in range(4)]
        slot_of = [n % 3 if n < 11 else (n - 9) % 2 for n in range(len(chunks))]
        before = [next((m for m in range(n - 1, -1, -1) if slot_of[m] == slot_of[n]), None) for n in range(len(chunks))]
        chunk_at = {name: n for n, (name, _) in enumerate(chunks)}

        def slot(name):
            n = chunk_at[name]
            w = chunks[n][1].shape[2]
            return RING[:, slot_of[n], 0:KT * w].rearrange("p (k n) -> p k n", k=KT)

        def ring_ready(eng, name):
            n = chunk_at[name]
            eng.wait_ge(S(f"ring{slot_of[n]}_loaded"), 16 * (slot_of[:n].count(slot_of[n]) + 1))
            return slot(name)

        block = ctx.enter_context(nc.Block())

        @block.tensor
        def _(pe):
            def mm(out, lhsT, rhs, start=True, stop=True, sem=None, **k):
                i = nc.tensor.matmul(out, lhsT, rhs, start=start, stop=stop, **k)
                if sem is not None:
                    i.then_inc(sem, 1)
                return i

            def tr(out, in_, sem=None):
                n = in_.shape[0]
                i = nc.tensor.transpose(out, in_, ident[0:n, 0:n])
                if sem is not None:
                    i.then_inc(sem, 1)

            def project(job, pool, lhs, rhs, cols=0):
                b = take_bank(job, pool)
                l0, r0 = lhs(0), rhs(0)
                m, n = l0.shape[1], r0.shape[1]
                for k in range(KT):
                    mm(b[0:m, cols:cols + n], lhs(k), rhs(k), k == 0, k == KT - 1, full(job) if k == KT - 1 else None)

            pe.wait_ge(S("ident_ready"), 1)
            pe.wait_ge(S("silu_c"), 1)
            b = take_bank("cT", "A")
            for k in range(KT):
                tr(b[:, k * 9:k * 9 + 9], SC9[0:9, k * P:(k + 1) * P], full("cT") if k == KT - 1 else None)
            b = take_bank("cwT", "A")
            pe.wait_ge(S("conv_w_in"), 16)
            tr(b[:, 0:48], CWN, full("cwT"))

            def mod_chunk(j):
                w = ring_ready(pe, f"mod{j}")
                project(("mod", j), "D", lambda k: CT[:, k, :], lambda k: w[:, k, :])
                last_job.append(newest[0])

            pe.wait_ge(S("cT_ready"), 1)
            for j in range(4):
                mod_chunk(j)
            for t in range(5):
                n = P if t < 4 else NB
                pe.wait_ge(S("h_ready"), t + 1)
                for half in range(2):
                    b = take_bank(("hT", t, half), "A")
                    for k in range(4):
                        kk = half * 4 + k
                        tr(b[:, k * n:(k + 1) * n], HJ[0:n, t % 2, kk * P:(kk + 1) * P], full(("hT", t, half)) if k == 3 else None)

            def tokens_out(name, cols, w):
                for t in range(5):
                    n = P if t < 4 else NB
                    pe.wait_ge(S("hT_ready"), 2 * t + 2)
                    project((name, t), "A", lambda k: HT[:, k, t * P:t * P + n], lambda k: w[:, k, cols])

            def narrow_out(name, w, cols, n_cols):
                b = take_bank(name, "D")
                for t in range(5):
                    n = P if t < 4 else NB
                    for k in range(KT):
                        last = t == 4 and k == KT - 1
                        mm(b[0:n, t * n_cols:(t + 1) * n_cols], HT[:, k, t * P:t * P + n], w[:, k, cols],
                           k == 0, k == KT - 1, full(name) if last else None)

            w = ring_ready(pe, "fv")
            tokens_out("fv", slice(0, 512), w)
            narrow_out("ff", w, slice(512, 520), 8)
            last_job.append(newest[0])
            w = ring_ready(pe, "gz")
            tokens_out("gz", slice(0, 512), w)
            narrow_out("gab", w, slice(512, 528), 16)
            last_job.append(newest[0])
            for name in ("fq", "fk"):
                w = ring_ready(pe, name)
                for j in range(4):
                    project((name, j), "A", lambda k: w[:, k, j * P:(j + 1) * P], lambda k: HT[:, k, 0:SEQ])
                project((name, 4), "A", lambda k: HT[:, k, SEQ:TOK], lambda k: w[:, k, :])
                last_job.append(newest[0])
            pe.wait_ge(S("fk_ready"), 4)
            for t in range(TILES):
                b = take_bank(("ktok", t), "D")
                for j in range(4):
                    tr(b[:, j * P:(j + 1) * P], FK[:, j, t * P:(t + 1) * P], full(("ktok", t)) if j == 3 else None)
            def conv_back(cb):
                pe.wait_ge(S("conv_act"), cb + 1)
                b = take_bank(("cvT", cb), "D")
                for t in range(TILES):
                    tr(b[:, t * P:(t + 1) * P], CACT[:, cb % 2, t * P:(t + 1) * P], full(("cvT", cb)) if t == 3 else None)

            for g, name in enumerate(("gq", "gk", "gv")):
                w = ring_ready(pe, name)
                for j in range(4):
                    cb = g * 4 + j
                    project(("cv", cb), "A", lambda k: w[:, k, j * P:(j + 1) * P], lambda k: HT[:, k, 0:SEQ])
                    if cb >= 2:
                        conv_back(cb - 2)
                project((name, 4), "A", lambda k: HT[:, k, SEQ:TOK], lambda k: w[:, k, :])
                last_job.append(newest[0])
            conv_back(10)
            conv_back(11)
            pe.wait_ge(S("tails"), 12)
            for q in range(3):
                b = take_bank(("tail", q), "D")
                for j in range(4):
                    tr(b[0:3, j * P:(j + 1) * P], TAILI[:, q * 4 + j, :], full(("tail", q)) if j == 3 else None)
            pe.wait_ge(S("gates_ready"), 1)
            b = take_bank("frow", "D")
            for i in range(TILES):
                for j in range(i + 1):
                    mm(b[0:8, i * P:(i + 1) * P], LOGF[:, j, :], upper[:, :] if j == i else ones[:, :], j == 0, j == i,
                       full("frow") if i == j == TILES - 1 else None)
            b = take_bank("gsum", "D")
            g32 = small[:, 340:372]
            mm(b[:, 0:32], upper[:, :], g32)
            mm(b[:, 32:64], ones[:, :], g32, sem=full("gsum"))

            def head_of(h):
                return slice((h % 2) * HD, (h % 2) * HD + HD), h // 2

            def fox_scores(u):
                h, i = divmod(u, 4)
                r, j = head_of(h)
                if i == 0:
                    pe.wait_ge(S(f"frow_in{h % 2}"), 32 * (h // 2 + 1))
                b = take_bank(("sc", u), "A")
                w = P * (i + 1)
                mm(b[:, 0:w], FQ[r, j, i * P:(i + 1) * P], FK[r, j, 0:w], True, False)
                mm(b[:, 0:w], FA[0:2, h % 2, i * P:(i + 1) * P], FB[0:2, h % 2, 0:w], False, False)
                mm(b[:, i * P:w], ident[:, :], hide_q[:, :], False, True, full(("sc", u)))

            def fox_turn(u):
                i = u % 4
                job_read(pe, ("sc", u))
                b = take_bank(("pT", u), "D")
                for k in range(i + 1):
                    tr(b[:, k * P:(k + 1) * P], PR[:, u % 2, k * P:(k + 1) * P], full(("pT", u)) if k == i else None)

            def fox_values(u):
                h, i = divmod(u, 4)
                job_read(pe, ("pT", u))
                b = take_bank(("fo", u), "D")
                for k in range(i + 1):
                    mm(b[:, 0:HD], PT[:, u % 2, k * P:(k + 1) * P], VT[:, k, h * HD:(h + 1) * HD], k == 0, k == i,
                       full(("fo", u)) if k == i else None)

            for u in range(34):
                if u < 32:
                    fox_scores(u)
                if 1 <= u < 33:
                    fox_turn(u - 1)
                if u >= 2:
                    fox_values(u - 2)
                if u in (6, 14, 22, 30):
                    mod_chunk(4 + (u - 6) // 8)

            def pair_turns(i):
                pe.wait_ge(S("gdn_tokens"), i + 1)
                for name, src in (("q", GT[:, i, 0:512]), ("k", GT[:, i, 512:1024]), ("kb", KB_), ("qG", QGT_)):
                    b = take_bank(("t" + name, i), "A")
                    for j in range(4):
                        tr(b[:, j * P:(j + 1) * P], src[:, j * P:(j + 1) * P], full(("t" + name, i)) if j == 3 else None)

            def products(i, hb):
                heads = range(hb, HEADS, 2)
                b = take_bank(("dec", i, hb), "D")
                for m, h in enumerate(heads):
                    mm(b[:, m * P:(m + 1) * P], G[:, i, h:h + 1].to_broadcast([P, P]), upper[:, :],
                       sem=full(("dec", i, hb)) if m == 3 else None)
                job_read(pe, ("tk", i))
                job_read(pe, ("tkb", i))
                for name, rhs in (("kk", TKB), ("kq", TQ)):
                    b = take_bank((name, i, hb), "D")
                    for m, h in enumerate(heads):
                        r, j = head_of(h)
                        mm(b[:, m * P:(m + 1) * P], TK[r, j, :], rhs[r, j, :], sem=full((name, i, hb)) if m == 3 else None)

            def solve(i, hb, lv):
                _, AT, AQ, X, Y, M0, M1 = BATCH[hb]
                T = BATCH[hb][0]
                M = (M0, M1)[lv % 2]
                pe.wait_ge(S(f"level{hb}"), 7 * i + lv + 1)
                if lv:
                    job_read(pe, ("Y", i, hb, lv - 1))
                    job_read(pe, ("X", i, hb, lv - 1))
                else:
                    pe.wait_ge(S("eye"), 2 * i + hb + 1)
                b = take_bank(("T", i, hb, lv), "A")
                for m in range(4):
                    mm(b[:, m * P:(m + 1) * P], M[:, m, :], X[:, m, :], sem=full(("T", i, hb, lv)) if m == 3 else None)

            def solve2(i, hb, lv):
                _, AT, AQ, X, Y, M0, M1 = BATCH[hb]
                T = BATCH[hb][0]
                job_read(pe, ("T", i, hb, lv))
                for name, l, r in (("X", Y, T), ("Y", T, Y)):
                    if lv == 6 and name == "X":
                        continue
                    b = take_bank((name, i, hb, lv), "D")
                    for m in range(4):
                        mm(b[:, m * P:(m + 1) * P], l[:, m, :], r[:, m, :], sem=full((name, i, hb, lv)) if m == 3 else None)

            def state(i):
                YH = lambda h: BATCH[h % 2][4][:, h // 2, :]
                AQH = lambda h: BATCH[h % 2][2][:, h // 2, :]
                job_read(pe, ("Y", i, 0, 6))
                job_read(pe, ("Y", i, 1, 6))
                b = take_bank(("wt", i), "A")
                for h in range(HEADS):
                    r, j = head_of(h)
                    mm(b[r, j * P:(j + 1) * P], KBG_[:, h * HD:(h + 1) * HD], YH(h), sem=full(("wt", i)) if h == 7 else None)
                job_read(pe, ("wt", i))
                pe.wait_ge(S("state"), 2 * i + 1)
                b = take_bank(("vn", i), "A")
                for h in range(HEADS):
                    if h % 2 == 0:
                        mm(b[:, h * HD:(h + 2) * HD], WT[:, h // 2, :], ST[:, h // 2, :], True, False)
                    mm(b[:, h * HD:(h + 1) * HD], YH(h), GT[:, i, 1024 + h * HD:1024 + (h + 1) * HD], False, h % 2 == 1,
                       full(("vn", i)) if h == 7 else None)
                job_read(pe, ("vn", i))
                b = take_bank(("o", i), "D")
                for h in range(HEADS):
                    if h % 2 == 0:
                        mm(b[:, h * HD:(h + 2) * HD], TQG[:, h // 2, :], ST[:, h // 2, :], True, False)
                    mm(b[:, h * HD:(h + 1) * HD], AQH(h), VN[:, h, :], False, h % 2 == 1, full(("o", i)) if h == 7 else None)
                b = take_bank(("dS", i), "D")
                for j in range(4):
                    mm(b[:, j * P:(j + 1) * P], KG_[:, j * P:(j + 1) * P], VN[:, 2 * j:2 * j + 2, :].rearrange("p h d -> p (h d)"),
                       sem=full(("dS", i)) if j == 3 else None)

            for i in range(TILES):
                pair_turns(i)
                products(i, 0)
                products(i, 1)
                for lv in range(7):
                    solve(i, 0, lv)
                    solve(i, 1, lv)
                    solve2(i, 0, lv)
                    solve2(i, 1, lv)
                state(i)
                mod_chunk(8 + i)

            pe.wait_ge(S("logf_pages"), 16)
            for half in range(2):
                b = take_bank(("lp", half), "D")
                for m in range(4):
                    h = half * 4 + m
                    tr(b[:, m * P:(m + 1) * P], LG.rearrange("p (n h) -> p h n", h=HEADS)[:, h, :], full(("lp", half)) if m == 3 else None)
            job_read(pe, ("lp", 1))
            for half in range(2):
                rhs = SLOT2[:, 2112 + half * 512:2112 + half * 512 + 512]
                b = take_bank(("lsum", half), "D")
                mm(b[:, :], lower[:, :], rhs, sem=full(("lsum", half)))
                b = take_bank(("ltot", half), "D")
                mm(b[:, :], ones[:, :], rhs, sem=full(("ltot", half)))
            pe.wait_ge(S("smax"), 1)
            b = take_bank("smT", "D")
            tr(b[0:64, 0:P], M64, full("smT"))
            pe.wait_ge(S("smax"), 2)
            b = take_bank("smB", "D")
            mm(b[:, 0:64], ones[0:64, :], TDG[0:64, :], sem=full("smB"))
            pe.wait_ge(S("ssums"), 1)
            b = take_bank("ssum", "D")
            mm(b[:, 0:64], ones[:, :], M64, sem=full("ssum"))
            pe.wait_ge(S("probs"), 1)
            for bb in range(NB):
                b = take_bank(("pv", bb), "D")
                for q in range(4):
                    n = bb * 4 + q
                    pe.wait_ge(S(f"kv_in{n % 2}"), 64 * (16 + n // 2 + 1))
                    for g in range(4):
                        for j in range(4):
                            mm(b[:, 2 * j:2 * j + 2], KG4[n % 2][:, g, j * P:(j + 1) * P], SC[:, 2 * j:2 * j + 2, bb, q * 4 + g],
                               q == g == j == 0, False, S("kv_used") if g == j == 3 else None, skip_group_check=True)
                pe.wait_ge(S(f"vnew_in{bb % 2}"), 16 * (bb // 2 + 1))
                for j in range(4):
                    mm(b[:, 2 * j:2 * j + 2], VNEW[:, (bb % 2) * 512 + j * P:(bb % 2) * 512 + (j + 1) * P], SC[0:1, 2 * j:2 * j + 2, bb, 16], False, j == 3,
                       full(("pv", bb)) if j == 3 else None, skip_group_check=True)

            for i in range(5):
                n = P if i < 4 else NB
                if i < 4:
                    pe.wait_ge(S("gdn_out"), i + 1)
                else:
                    pe.wait_ge(S("ogs_in"), 16)
                for half in range(2 if i < 4 else 1):
                    job = ("oT", i, half)
                    b = take_bank(job, "A")
                    for j in range(4):
                        src = fox_out(j)[:, i, :] if half else (GT[:, i, j * P:(j + 1) * P] if i < 4 else OGS[:, j * P:(j + 1) * P])
                        tr(b[:, j * n:(j + 1) * n], src, full(job) if j == 3 else None)
            job_read(pe, ("oT", 4, 0))
            job_read(pe, ("oT", 3, 0))
            job_read(pe, ("oT", 3, 1))
            job_read(pe, ("oT", 2, 1))
            job_read(pe, ("pv", 7))
            for c in range(2):
                w = ring_ready(pe, f"wo{c}")
                for t in range(5):
                    n = P if t < 4 else NB
                    project(("wo", c, t), "D", lambda k: HT[:, k, t * P:t * P + n], lambda k: w[:, k, :])
                last_job.append(newest[0])
            pe.wait_ge(S("keys_in"), 16)
            for q in range(4):
                b = take_bank(("key", q), "A")
                for j in range(4):
                    tr(b[:, j * P:(j + 1) * P], KN[:, q * 4 + j, :], full(("key", q)) if j == 3 else None)
            for t in range(5):
                n = P if t < 4 else NB
                pe.wait_ge(S("h_ready"), 5 + t + 1)
                for half in range(2):
                    job = ("h2T", t, half)
                    b = take_bank(job, "A")
                    for k in range(4):
                        tr(b[:, k * n:(k + 1) * n], H2[0:n, t, (half * 4 + k) * P:(half * 4 + k + 1) * P], full(job) if k == 3 else None)
            for t in range(5):
                job_read(pe, ("h2T", t, 0))
                job_read(pe, ("h2T", t, 1))
            for c in range(4):
                w = ring_ready(pe, f"wq{c}")
                for j in range(4):
                    project(("qT", c * 4 + j), "A", lambda k: w[:, k, j * P:(j + 1) * P], lambda k: HT[:, k, 0:SEQ])
                b = take_bank(("qTs", c), "A")
                for j in range(4):
                    for k in range(KT):
                        mm(b[:, j * NB:(j + 1) * NB], w[:, k, j * P:(j + 1) * P], HT[:, k, SEQ:TOK], k == 0, k == KT - 1,
                           full(("qTs", c)) if j == 3 and k == KT - 1 else None)
                last_job.append(newest[0])
            for t in range(5):
                n = P if t < 4 else NB
                for q in range(4):
                    if t == 0:
                        for j in range(4):
                            job_read(pe, ("qT", q * 4 + j))
                        job_read(pe, ("key", q))
                        job_read(pe, ("qTs", q))
                    b = take_bank(("score", t, q), "A")
                    for j in range(4):
                        mm(b[0:n, j * P:(j + 1) * P], QT[:, q * 4 + j, t * P:t * P + n], KEYT[:, q * 4 + j, :],
                           sem=full(("score", t, q)) if j == 3 else None)

            for t in range(5):
                for q in range(4):
                    job_read(pe, ("score", t, q))

            def peer_values(h, t):
                n_ = h * 4 + t
                lo, hi = banks[(t % 2) * 2], banks[(t % 2) * 2 + 1]
                pe.wait_ge(S("sums_free"), n_ + 1)
                for s_ in range(16):
                    pe.wait_ge(S(f"v_in{s_ % 8}"), n_ * 32 + 16 * (s_ // 8 + 1))
                    pe.wait_ge(S("diagonal"), n_ * 16 + s_ + 1)
                    mm(lo[:, :], DG[:, s_ % 4, :], VR[:, s_ % 8, 0:512], s_ == 0, s_ == 15)
                    mm(hi[:, :], DG[:, s_ % 4, :], VR[:, s_ % 8, 512:1024], s_ == 0, s_ == 15, S("v_used"))

            with pe.Fori(0, PH - 1) as h:
                for t in range(TILES):
                    peer_values(h, t)
            for t in range(TILES):
                peer_values(PH - 1, t)
            pe.wait_ge(S("sample_picks"), 1)
            b = take_bank("ixT", "D")
            tr(b[:, 0:8], EISF[0:NB, :])
            pe.wait_ge(S("sample_picks"), 2)
            tr(b[:, 8:16], FVSS[0:NB, :], full("ixT"))
            pe.wait_ge(S("sums_free"), 34)
            pe.wait_ge(S("sample_gates"), 1)
            for t in range(NB):
                pe.wait_ge(S(f"v_in{t}"), 16 * (64 + 1))
                for half in range(2):
                    mm(banks[half][0:NB, :], AM[:, t * 8:t * 8 + 8], VR[:, t, half * 512:(half + 1) * 512], t == 0, t == NB - 1,
                       S("v_used") if half else None)

        @block.scalar
        def _(act):
            A = nc.scalar.activation
            act.wait_ge(S("c_in"), 32)
            A(SC9[0:9, :], C9[0:9, :], ACT.Silu).then_inc(S("silu_c"), 1)
            b = full_bank(act, "cT")
            A(small[:, 0:72], b[:, 0:72], ACT.Copy).then_inc(S("cT_ready"), 1)
            act.wait_ge(S("cT_ready"), 1)
            nc.scalar.sem_inc(free("cT"), 1)
            b = full_bank(act, "cwT")
            A(small[:, 72:120], b[:, 0:48], ACT.Copy).then_inc(free("cwT"), 1)
            for t in range(5):
                n = P if t < 4 else NB
                act.wait_ge(S("sumsq"), t + 1)
                A(SS[0:n, 5 + t:6 + t], SS[0:n, t:t + 1], ACT.Sqrt, scale=1.0 / D_MODEL, bias=EPSB[0:n, :]).then_inc(S("root"), 1)
                for half in range(2):
                    b = full_bank(act, ("hT", t, half))
                    A(HT[:, half * 4:half * 4 + 4, t * P:t * P + n], b[:, 0:4 * n].rearrange("p (k n) -> p k n", k=4),
                      ACT.Copy).then_inc(S("hT_ready"), 1)
                    act.wait_ge(S("hT_ready"), 2 * t + half + 1)
                    act.sem_inc(free(("hT", t, half)), 1)
            for t in range(4):
                b = full_bank(act, ("fv", t))
                A(VT[:, t, :], b[:, :], ACT.Copy).then_inc(free(("fv", t)), 1)
            b = full_bank(act, ("fv", 4))
            A(PS[0:NB, COL_FV:COL_FV + 512], b[0:NB, :], ACT.Copy).then_inc(free(("fv", 4)), 1)
            for t in range(4):
                b = full_bank(act, ("gz", t))
                A(GZ[:, t, :], b[:, :], ACT.Silu).then_inc(free(("gz", t)), 1)
            b = full_bank(act, ("gz", 4))
            A(PS[0:NB, COL_Z:COL_Z + 512], b[0:NB, :], ACT.Silu).then_inc(free(("gz", 4)), 1)
            for name, dst, scale, col in (("fq", FQ, HD ** -0.5, COL_FQ), ("fk", FK, 1.0, COL_FK)):
                for j in range(4):
                    b = full_bank(act, (name, j))
                    A(dst[:, j, :], b[:, :], ACT.Copy, scale=scale).then_inc(S(name + "_ready"), 1)
                    act.wait_ge(S(name + "_ready"), j + 1)
                    act.sem_inc(free((name, j)), 1)
                b = full_bank(act, (name, 4))
                A(PS[0:NB, col:col + 512], b[0:NB, :], ACT.Copy, scale=scale).then_inc(free((name, 4)), 1)

            def conv_silu(cb):
                act.wait_ge(S("conv_sum"), cb + 1)
                if cb >= 2:
                    job_done(act, ("cvT", cb - 2))
                A(CACT[:, cb % 2, :], CACC[:, cb % 2, :], ACT.Silu).then_inc(S("conv_act"), 1)

            act.wait_ge(S("raw_zero"), 1)
            for g, name in enumerate(("gq", "gk", "gv")):
                for j in range(4):
                    cb = g * 4 + j
                    b = full_bank(act, ("cv", cb))
                    if cb >= 2:
                        act.wait_ge(S("tails"), cb - 1)
                    A(RAW[:, cb % 2, 3:515], b[:, :], ACT.Copy).then_inc(S("raw_ready"), 1)
                    act.wait_ge(S("raw_ready"), cb + 1)
                    act.sem_inc(free(("cv", cb)), 1)
                    if cb >= 1:
                        conv_silu(cb - 1)
                b = full_bank(act, (name, 4))
                A(PS[0:NB, g * 512:(g + 1) * 512], b[0:NB, :], ACT.Copy).then_inc(S("sample_raw"), 1)
                act.wait_ge(S("sample_raw"), g + 1)
                act.sem_inc(free((name, 4)), 1)
            conv_silu(11)
            act.sem_inc(S("sample_ready"), 1)
            act.wait_ge(S("gate_abs"), 1)
            for t0, n, tt in ((0, P, 4), (4, NB, 1)):
                v = GW[0:n, t0:t0 + tt, :]
                A(v, v, ACT.Exp, scale=-1.0).then_inc(S("gate_exp"), 1)
            act.wait_ge(S("gate_exp"), 2)
            for t0, n, tt in ((0, P, 4), (4, NB, 1)):
                v = GW[0:n, t0:t0 + tt, 0:16]
                A(v, v, ACT.Ln, bias=1.0).then_inc(S("gate_ln"), 1)
            A(BIAS[:, 2, :], BIAS[:, 2, :], ACT.Exp).then_inc(S("gate_ln"), 1)
            act.wait_ge(S("sconv_done"), 3)
            A(PSC[0:NB, :], PSC[0:NB, :], ACT.Silu).then_inc(S("sconv_silu"), 1)
            act.wait_ge(S("gsums"), 1)
            A(small[:, 690:722], small[:, 658:690], ACT.Exp).then_inc(S("decays"), 1)
            A(small[:, 754:786], small[:, 754:786], ACT.Exp).then_inc(S("decays"), 1)
            A(small[:, 722:754], small[:, 722:754], ACT.Exp).then_inc(S("decays"), 1)
            act.wait_ge(S("psbuf_free"), 1)
            for u in range(32):
                w = P * (u % 4 + 1)
                b = full_bank(act, ("sc", u))
                act.wait_ge(S("fox_max"), u + 1)
                if u >= 2:
                    job_done(act, ("pT", u - 2))
                A(PR[:, u % 2, 0:w], b[:, 0:w], ACT.Exp, bias=NM[:, u:u + 1], accum_out=RS[:, u:u + 1]).then_inc(free(("sc", u)), 1)
                if u == 9:
                    act.wait_ge(S("srule"), 1)
                    A(SSM[0:64, 4:6], SSM[0:64, 2:4], ACT.Sqrt, bias=EPSB[0:64, :]).then_inc(S("srule_act"), 1)
                    A(SSM[0:64, 6:7], SSM[0:64, 1:2], ACT.Exp).then_inc(S("srule_act"), 1)
            act.wait_ge(S("srule"), 5)
            A(SSM[0:64, 4:5], SSM[0:64, 2:3], ACT.Sqrt, scale=1.0 / HD, bias=EPSB[0:64, :]).then_inc(S("srule_act"), 1)
            for i in range(TILES):
                act.wait_ge(S("sq_free"), i + 1)
                A(SQ, GT[:, i, 0:1024], ACT.Square).then_inc(S("gdn_sq"), 1)
                act.wait_ge(S("gdn_ss"), i + 1)
                A(RQ, RQ, ACT.Sqrt, bias=EPSB).then_inc(S("gdn_root"), 1)
                for name, dst in (("q", TQ), ("k", TK), ("kb", TKB), ("qG", TQG)):
                    b = full_bank(act, ("t" + name, i))
                    A(dst, b[:, :].rearrange("p (j c) -> p j c", j=4), ACT.Copy).then_inc(free(("t" + name, i)), 1)
                for hb in range(2):
                    act.wait_ge(S("exponents"), 2 * i + hb + 1)
                    A(BATCH[hb][0], BATCH[hb][0], ACT.Exp).then_inc(S("decay_matrix"), 1)
                for lv in range(7):
                    for hb in range(2):
                        b = full_bank(act, ("T", i, hb, lv))
                        if lv == 0:
                            act.wait_ge(S("decay_used"), 2 * i + hb + 1)
                        A(BATCH[hb][0], b[:, :].rearrange("p (m c) -> p m c", m=4), ACT.Copy).then_inc(free(("T", i, hb, lv)), 1)
                b = full_bank(act, ("wt", i))
                A(WT, b[:, :].rearrange("p (j c) -> p j c", j=4), ACT.Copy).then_inc(free(("wt", i)), 1)
                b = full_bank(act, ("vn", i))
                A(VN, b[:, :].rearrange("p (h d) -> p h d", h=8), ACT.Copy).then_inc(free(("vn", i)), 1)
                act.wait_ge(S("o_ss"), i + 1)
                A(RQ[:, 0:8], RQ[:, 0:8], ACT.Sqrt, scale=1.0 / HD, bias=EPSB).then_inc(S("o_root"), 1)
            act.wait_ge(S("sshift"), 1)
            A(SLOT2[:, 0:1088], SLOT2[:, 0:1088], ACT.Exp).then_inc(S("sexp"), 1)
            for i in range(5):
                n = P if i < 4 else NB
                for half in range(2 if i < 4 else 1):
                    b = full_bank(act, ("oT", i, half))
                    A(HT[:, half * 4:half * 4 + 4, i * P:i * P + n], b[:, 0:4 * n].rearrange("p (k n) -> p k n", k=4),
                      ACT.Copy).then_inc(free(("oT", i, half)), 1)
            for q in range(4):
                b = full_bank(act, ("key", q))
                A(KEYT[:, q * 4:q * 4 + 4, :], b[:, :].rearrange("p (b n) -> p b n", b=4), ACT.Copy).then_inc(free(("key", q)), 1)
            job_done(act, ("wo", 1, 4))
            for t in range(5):
                n = P if t < 4 else NB
                act.wait_ge(S("sumsq"), 5 + t + 1)
                A(SS[0:n, 5 + t:6 + t], SS[0:n, t:t + 1], ACT.Sqrt, scale=1.0 / D_MODEL, bias=EPSB[0:n, :]).then_inc(S("root"), 1)
                for half in range(2):
                    b = full_bank(act, ("h2T", t, half))
                    A(HT[:, half * 4:half * 4 + 4, t * P:t * P + n], b[:, 0:4 * n].rearrange("p (k n) -> p k n", k=4),
                      ACT.Copy).then_inc(free(("h2T", t, half)), 1)
            for c in range(4):
                for j in range(4):
                    b = full_bank(act, ("qT", c * 4 + j))
                    A(QT[:, c * 4 + j, 0:SEQ], b[:, :], ACT.Copy).then_inc(free(("qT", c * 4 + j)), 1)
                b = full_bank(act, ("qTs", c))
                A(QT[:, c * 4:c * 4 + 4, SEQ:TOK], b[:, 0:32].rearrange("p (b n) -> p b n", b=4), ACT.Copy).then_inc(free(("qTs", c)), 1)
            for t in range(5):
                n = P if t < 4 else NB
                for q in range(4):
                    b = full_bank(act, ("score", t, q))
                    dst = QT[:, q * 4:q * 4 + 4, t * P:(t + 1) * P] if t < 4 else SCS[0:NB, q * 512:(q + 1) * 512].rearrange("p (b n) -> p b n", b=4)
                    A(dst, b[0:n, :].rearrange("p (b n) -> p b n", b=4), ACT.Copy).then_inc(free(("score", t, q)), 1)

            def gates(n_, t):
                act.wait_ge(S("picked"), n_ + 1)
                A(GAT[:, t, :], FVS[:, t, :], ACT.Exp, bias=NMX[:, t:t + 1], accum_out=SUMG[:, t:t + 1]).then_inc(S("gate_raw"), 1)

            def gelu(n_, t):
                act.wait_ge(S("dots"), n_ * 16 + 16)
                A(AG[:, t, :], DOT[:, t, :], ACT.Gelu).then_inc(S("gelu"), 1)

            def peer_scalar(h, last):
                for t in range(TILES):
                    n_ = h * 4 + t
                    act.wait_ge(S("weights"), n_ + 1)
                    for s_ in range(16):
                        act.wait_ge(S("v_used"), n_ * 16 + s_ + 5)
                        A(DG[:, s_ % 4, :], ident[:, :], ACT.Copy, scale=AG[:, t, s_:s_ + 1]).then_inc(S("diagonal"), 1)
                        if s_ == 8 and not (last and t >= 2):
                            gates(n_ + 2, (t + 2) % 4)
                    if not (last and t == 3):
                        gelu(n_ + 1, (t + 1) % 4)

            gates(0, 0)
            gates(1, 1)
            gelu(0, 0)
            with act.Fori(0, PH - 1) as h:
                peer_scalar(h, False)
            peer_scalar(PH - 1, True)
            act.wait_ge(S("sample_shift"), 1)
            A(FVSS[0:NB, :], FVSS[0:NB, :], ACT.Exp).then_inc(S("sample_exp"), 1)
            act.wait_ge(S("sample_dots"), NB)
            A(DOTS, DOTS, ACT.Gelu).then_inc(S("sample_gelu"), 1)
            for t in range(5):
                n = P if t < 4 else NB
                act.wait_ge(S("sumsq"), 10 + t + 1)
                A(SS[0:n, 5 + t:6 + t], SS[0:n, t:t + 1], ACT.Sqrt, scale=1.0 / D_MODEL, bias=EPSB[0:n, :]).then_inc(S("root"), 1)

        @block.vector
        def _(dve):
            V = nc.vector
            count = [0]

            def step(ins):
                count[0] += 1
                ins.then_inc(S("dve_steps"), 1)

            def settle():
                dve.wait_ge(S("dve_steps"), count[0])

            step(V.memset(ones[:, :], 1.0))
            step(V.memset(EPSB[:, :], EPS))
            V.memset(RAW[:, :, 0:3], 0.0).then_inc(S("raw_zero"), 1)
            dve.wait_ge(S("iota"), 2)
            E, C = ints[:, 0, :], ints[:, 1, :]
            V.tensor_tensor(ident[:, :], E, C, ALU.is_equal).then_inc(S("ident_ready"), 1)
            step(V.tensor_tensor(upper[:, :], E, C, ALU.is_le))
            step(V.tensor_tensor(lower[:, :], E, C, ALU.is_gt))
            settle()
            step(V.tensor_scalar(hide_e[:, :], lower[:, :], NEG, None, ALU.mult))
            step(V.tensor_tensor(hide_q[:, :], E, C, ALU.is_lt))
            settle()
            step(V.tensor_scalar(hide_q[:, :], hide_q[:, :], NEG, None, ALU.mult))
            for s in range(7):
                step(V.tensor_scalar(ints[:, 2, :], C, s, 1, ALU.logical_shift_right, ALU.bitwise_xor))
                step(V.tensor_scalar(ints[:, 3, :], E, s, 0, ALU.logical_shift_right, ALU.bitwise_or))
                settle()
                step(V.tensor_tensor(level[:, s, :], ints[:, 2, :], ints[:, 3, :], ALU.is_equal))
                settle()
                step(V.tensor_tensor(level[:, s, :], level[:, s, :], upper[:, :], ALU.mult))
                settle()

            def mod_row(j, nth):
                b = full_bank(dve, ("mod", j))
                dve.wait_ge(S(f"bmod{nth % 2}"), 16 * (nth // 2 + 1))
                if nth >= 2:
                    dve.wait_ge(S(f"mod_out{nth % 2}"), 16 * (nth // 2))
                plus = 1.0 if j in (2, 3, 8, 9) else 0.0
                V.scalar_tensor_tensor(MR[0:9, nth % 2, :], b[0:9, :], plus, BMR[0:9, nth % 2, :], ALU.add, ALU.add)\
                    .then_inc(S("mod_row"), 1)
                dve.wait_ge(S("mod_row"), nth + 1)
                dve.sem_inc(free(("mod", j)), 1)

            for j in range(4):
                mod_row(j, j)

            def norm_mod(t, x, out, rows, sh, sc, ss):
                V.scalar_tensor_tensor(out, x, 1.0, x, ALU.mult, ALU.mult, accum_out=ss[0]).then_inc(S("sumsq"), 1)
                dve.wait_ge(S("root"), t + 1)
                step(V.reciprocal(ss[1], ss[1]))
                settle()
                step(V.scalar_tensor_tensor(out, x, ss[1], sc, ALU.mult, ALU.mult))
                settle()
                V.tensor_tensor(out, out, sh, ALU.add).then_inc(S("h_ready"), 1)

            for t in range(5):
                n, mv = (P, 0) if t < 4 else (NB, 2)
                dve.wait_ge(S(f"x_in{t % 2}"), 16 * (t // 2 + 1))
                if t >= 2:
                    full_bank(dve, ("hT", t - 2, 1))
                if t == 0:
                    dve.wait_ge(S("mv_prompt"), 32)
                if t == 4:
                    dve.wait_ge(S("mv_sample"), 32)
                norm_mod(t, XR[0:n, t % 2, :], HJ[0:n, t % 2, :], n, MV[0:n, mv, :], MV[0:n, mv + 1, :],
                         (SS[0:n, t:t + 1], SS[0:n, 5 + t:6 + t]))
            b = full_bank(dve, "ff")
            step(V.tensor_copy(GATE[:, 0:4, 16:24], b[:, 0:32].rearrange("p (t h) -> p t h", h=8)))
            V.tensor_copy(GATE[0:NB, 4, 16:24], b[0:NB, 32:40]).then_inc(free("ff"), 1)
            b = full_bank(dve, "gab")
            step(V.tensor_copy(GATE[:, 0:4, 0:16], b[:, 0:64].rearrange("p (t h) -> p t h", h=16)))
            V.tensor_copy(GATE[0:NB, 4, 0:16], b[0:NB, 64:80]).then_inc(free("gab"), 1)
            job_read(dve, "gab")
            dve.wait_ge(S("bias_in"), 48)
            settle()
            both = ((0, P, 4), (4, NB, 1))
            for t0, n, tt in both:
                step(V.tensor_tensor(GATE[0:n, t0:t0 + tt, 0:8], GATE[0:n, t0:t0 + tt, 0:8],
                                     BIAS[0:n, 0:1, :].to_broadcast([n, tt, 8]), ALU.add))
                step(V.tensor_tensor(GATE[0:n, t0:t0 + tt, 16:24], GATE[0:n, t0:t0 + tt, 16:24],
                                     BIAS[0:n, 1:2, :].to_broadcast([n, tt, 8]), ALU.add))
            settle()
            for t0, n, tt in both:
                for at, frm in ((0, 0), (8, 16)):
                    v = GATE[0:n, t0:t0 + tt, frm:frm + 8]
                    step(V.scalar_tensor_tensor(GW[0:n, t0:t0 + tt, at:at + 8], v, -1.0, v, ALU.mult, ALU.max))
                step(V.tensor_copy(GW[0:n, t0:t0 + tt, 16:24], GATE[0:n, t0:t0 + tt, 8:16]))
            settle()
            dve.sem_inc(S("gate_abs"), 1)
            for t in range(TILES):
                b = full_bank(dve, ("ktok", t))
                if t >= 2:
                    dve.wait_ge(S(f"k_out{t % 2}"), 16 * (t // 2))
                V.tensor_copy(KO[:, t % 2, :], b[:, :]).then_inc(S("ktok_copied"), 1)
                dve.wait_ge(S("ktok_copied"), t + 1)
                dve.sem_inc(free(("ktok", t)), 1)

            def conv_block(cb):
                dve.wait_ge(S("raw_ready"), cb + 1)
                r, acc = RAW[:, cb % 2, :], CACC[:, cb % 2, :]
                if cb >= 2:
                    dve.wait_ge(S("conv_act"), cb - 1)
                V.tensor_copy(TAILI[:, cb, :], r[:, 512:515]).then_inc(S("tails_early"), 1)
                step(V.tensor_scalar(acc, r[:, 0:512], CW[:, 0, cb:cb + 1], None, ALU.mult))
                for j in range(1, 3):
                    settle()
                    step(V.scalar_tensor_tensor(acc, r[:, j:j + 512], CW[:, j, cb:cb + 1], acc, ALU.mult, ALU.add))
                settle()
                V.scalar_tensor_tensor(acc, r[:, 3:515], CW[:, 3, cb:cb + 1], acc, ALU.mult, ALU.add)\
                    .then_inc(S("conv_sum"), 1)
                dve.wait_ge(S("conv_sum"), cb + 1)
                dve.wait_ge(S("tails_early"), cb + 1)
                dve.sem_inc(S("tails"), 1)

            def conv_tokens(cb):
                b = full_bank(dve, ("cvT", cb))
                V.tensor_copy(GT[:, :, cb * P:(cb + 1) * P], b[:, :].rearrange("p (t c) -> p t c", t=TILES))\
                    .then_inc(free(("cvT", cb)), 1)

            dve.wait_ge(S("raw_zero"), 1)
            for cb in range(12):
                conv_block(cb)
                if cb >= 2:
                    conv_tokens(cb - 2)
            conv_tokens(10)
            conv_tokens(11)
            for q in range(3):
                b = full_bank(dve, ("tail", q))
                V.tensor_copy(TAILO[0:3, q * 512:(q + 1) * 512], b[0:3, :]).then_inc(S("tail_out"), 1)
                dve.wait_ge(S("tail_out"), q + 1)
                dve.sem_inc(free(("tail", q)), 1)
            dve.wait_ge(S("gate_ln"), 3)
            for t0, n, tt in both:
                step(V.tensor_scalar_add(BETA[0:n, t0:t0 + tt, :], GW[0:n, t0:t0 + tt, 16:24], 1.0))
                step(V.scalar_tensor_tensor(G[0:n, t0:t0 + tt, :], GATE[0:n, t0:t0 + tt, 0:8], 0.0,
                                            GW[0:n, t0:t0 + tt, 0:8], ALU.max, ALU.add))
                step(V.scalar_tensor_tensor(LOGF[0:n, t0:t0 + tt, :], GATE[0:n, t0:t0 + tt, 16:24], 0.0,
                                            GW[0:n, t0:t0 + tt, 8:16], ALU.min, ALU.subtract))
            settle()
            for t0, n, tt in both:
                step(V.reciprocal(BETA[0:n, t0:t0 + tt, :], BETA[0:n, t0:t0 + tt, :]))
                step(V.scalar_tensor_tensor(G[0:n, t0:t0 + tt, :], G[0:n, t0:t0 + tt, :], -1.0,
                                            BIAS[0:n, 2:3, :].to_broadcast([n, tt, 8]), ALU.mult, ALU.mult))
            settle()
            dve.sem_inc(S("gates_ready"), 1)
            dve.wait_ge(S("sample_ready"), 1)
            T8 = MV[0:NB, 3, 0:512]
            step(V.tensor_tensor(T8, PS[0:NB, COL_FQ:COL_FQ + 512], PS[0:NB, COL_FK:COL_FK + 512], ALU.mult))
            settle()
            V.tensor_reduce(SN[0:NB, :], T8.rearrange("p (h d) -> p h d", h=8), AXX, ALU.add).then_inc(S("new_score"), 1)
            b = full_bank(dve, "frow")
            step(V.tensor_copy(FR[0:8, :], b[0:8, :]))
            V.tensor_scalar(NFR[0:8, :], b[0:8, :], -1.0, None, ALU.mult).then_inc(free("frow"), 1)
            b = full_bank(dve, "gsum")
            step(V.tensor_copy(small[:, 658:690], b[:, 0:32]))
            V.tensor_copy(small[:, 722:754], b[:, 32:64]).then_inc(free("gsum"), 1)
            job_read(dve, "gsum")
            job_read(dve, "frow")
            settle()
            dve.sem_inc(S("frows"), 1)
            step(V.tensor_tensor(small[:, 754:786], small[:, 722:754], small[:, 658:690], ALU.subtract))
            settle()
            dve.sem_inc(S("gsums"), 1)
            dve.wait_ge(S("decays"), 3)
            step(V.scalar_tensor_tensor(small[:, 786:818], small[:, 300:332], -1.0, small[:, 690:722], ALU.mult, ALU.mult))

            def fox_max(u):
                w = P * (u % 4 + 1)
                job_done(dve, ("sc", u))
                V.tensor_reduce(NM[:, u:u + 1], banks[job_of[("sc", u)][0]][:, 0:w], AXX, ALU.max, negate=True)\
                    .then_inc(S("fox_max"), 1)

            def fox_turned(u):
                w = P * (u % 4 + 1)
                b = full_bank(dve, ("pT", u))
                if u >= 2:
                    job_done(dve, ("fo", u - 2))
                V.tensor_copy(PT[:, u % 2, 0:w], b[:, 0:w]).then_inc(free(("pT", u)), 1)

            def fox_norm(u):
                h, i = divmod(u, 4)
                job_read(dve, ("sc", u))
                step(V.reciprocal(RI[:, u:u + 1], RS[:, u:u + 1]))
                b = full_bank(dve, ("fo", u))
                settle()
                V.tensor_scalar(fox_out(h // 2)[:, i, (h % 2) * HD:(h % 2) * HD + HD], b[:, 0:HD], RI[:, u:u + 1], None,
                                ALU.mult).then_inc(free(("fo", u)), 1)

            SR = slice(0, 64)

            def srule_norms():
                dve.wait_ge(S("srule_in"), 128)
                t = SSP[SR].rearrange("p k v -> p (k v)")[:, 0:128].rearrange("p (n d) -> p n d", n=2)
                step(V.tensor_tensor(t, SV[SR, 0:2, :], SV[SR, 0:2, :], ALU.mult))
                settle()
                V.tensor_reduce(SSM[SR, 2:4], t, AXX, ALU.add).then_inc(S("srule"), 1)

            def srule_scale():
                dve.wait_ge(S("srule_act"), 2)
                step(V.reciprocal(SSM[SR, 4:6], SSM[SR, 4:6]))
                step(V.scalar_tensor_tensor(SSM[SR, 7:8], SSM[SR, 0:1], -1.0, SSM[SR, 6:7], ALU.mult, ALU.mult))
                step(V.tensor_scalar(SV[SR, 2, :], SV[SR, 2, :], SSM[SR, 0:1], None, ALU.mult))
                settle()
                step(V.tensor_scalar(SV[SR, 0, :], SV[SR, 0, :], SSM[SR, 4:5], HD ** -0.5, ALU.mult, ALU.mult))
                step(V.tensor_scalar(SV[SR, 1, :], SV[SR, 1, :], SSM[SR, 5:6], None, ALU.mult))
                settle()
                dve.sem_inc(S("srule"), 1)

            def srule_new():
                dve.wait_ge(S("srule_pool"), 1)
                step(V.tensor_reduce(SV[SR, 4, :], SSP[SR].rearrange("p k v -> p v k"), AXX, ALU.add))
                settle()
                V.scalar_tensor_tensor(SV[SR, 2, :], SV[SR, 4, :], SSM[SR, 7:8], SV[SR, 2, :], ALU.mult, ALU.add)\
                    .then_inc(S("srule"), 1)

            def srule_state():
                dve.wait_ge(S("srule_pool"), 2)
                V.scalar_tensor_tensor(SS0[SR], SS0[SR], SSM[SR, 6:7], SSP[SR], ALU.mult, ALU.add).then_inc(S("srule"), 1)

            def srule_out():
                dve.wait_ge(S("srule_pool"), 3)
                o_ = SV[SR, 4, :]
                t = SSP[SR, 0, :]
                step(V.tensor_reduce(o_, SSP[SR].rearrange("p k v -> p v k"), AXX, ALU.add))
                settle()
                step(V.tensor_tensor(t, o_, o_, ALU.mult))
                settle()
                V.tensor_reduce(SSM[SR, 2:3], t, AXX, ALU.add).then_inc(S("srule"), 1)

            def srule_gate():
                dve.wait_ge(S("srule_act"), 3)
                o_ = SV[SR, 4, :]
                step(V.reciprocal(SSM[SR, 4:5], SSM[SR, 4:5]))
                settle()
                step(V.scalar_tensor_tensor(o_, o_, SSM[SR, 4:5], NW[SR, :], ALU.mult, ALU.mult))
                settle()
                V.tensor_tensor(o_, o_, SV[SR, 3, :], ALU.mult).then_inc(S("srule"), 1)

            between = {8: srule_norms, 10: srule_scale, 16: srule_new, 21: srule_state, 29: srule_out}
            for u in range(34):
                if u < 32:
                    fox_max(u)
                if 1 <= u < 33:
                    if u == 1:
                        dve.wait_ge(S("psbuf_free"), 1)
                    fox_turned(u - 1)
                if u >= 2:
                    fox_norm(u - 2)
                if u in (6, 14, 22, 30):
                    mod_row(4 + (u - 6) // 8, 4 + (u - 6) // 8)
                if u in between:
                    between[u]()
            srule_gate()
            dve.wait_ge(S("srule"), 6)
            dve.wait_ge(S("srule_stored"), 32)

            step(V.memset(SC[:, :, :, 16], NEG))
            settle()
            dve.sem_inc(S("scores_cleared"), 1)
            kg = [0]

            def key_group():
                n = kg[0]
                if n == 32:
                    return
                kg[0] += 1
                dve.wait_ge(S("kprod"), n + 1)
                V.tensor_reduce(SC[:, :, n // 4, (n % 4) * 4:(n % 4) * 4 + 4].rearrange("p h g -> p g h"),
                                KG4[n % 2].rearrange("p g (h d) -> p g h d", d=HD), AXX, ALU.add).then_inc(S("kred"), 1)

            step(V.memset(ST, 0.0))
            settle()
            dve.sem_inc(S("state"), 1)
            for i in range(TILES):
                dve.wait_ge(S("gates_ready"), 1)
                dve.sem_inc(S("sq_free"), 1)
                q8, k8, v8 = (GT[:, i, n * 512:(n + 1) * 512].rearrange("p (h d) -> p h d", h=8) for n in range(3))
                three = lambda v: v.rearrange("p (h d) -> p h d", h=8)
                dve.wait_ge(S("gdn_sq"), i + 1)
                V.tensor_reduce(RQ, SQ.rearrange("p (n d) -> p n d", d=HD), AXX, ALU.add).then_inc(S("gdn_ss"), 1)
                step(V.tensor_tensor(v8, v8, wide(BETA[:, i, :], HD), ALU.mult))
                dve.wait_ge(S("gdn_root"), i + 1)
                step(V.reciprocal(RQ, RQ))
                settle()
                step(V.tensor_scalar(RQ[:, 0:8], RQ[:, 0:8], HD ** -0.5, None, ALU.mult))
                step(V.tensor_tensor(k8, k8, wide(RQ[:, 8:16], HD), ALU.mult))
                settle()
                step(V.tensor_tensor(q8, q8, wide(RQ[:, 0:8], HD), ALU.mult))
                step(V.tensor_tensor(three(KB_), k8, wide(BETA[:, i, :], HD), ALU.mult))
                step(V.tensor_tensor(three(KBG_), k8, wide(NBG[:, i, :], HD), ALU.mult))
                step(V.tensor_tensor(three(KG_), k8, wide(EKG[:, i, :], HD), ALU.mult))
                settle()
                V.tensor_tensor(three(QGT_), q8, wide(EG[:, i, :], HD), ALU.mult).then_inc(S("gdn_tokens"), 1)
                for hb in range(2):
                    D, AT, AQ, X, Y, M0, M1 = BATCH[hb]
                    step(V.tensor_copy(X, FOUR(ident)))
                    V.tensor_copy(Y, FOUR(ident)).then_inc(S("eye_y"), 1)
                    settle()
                    dve.wait_ge(S("eye_y"), 2 * i + hb + 1)
                    dve.sem_inc(S("eye"), 1)
                    b = full_bank(dve, ("dec", i, hb))
                    V.tensor_tensor(D, b[:, :].rearrange("p (m c) -> p m c", m=4), wide(GC[:, i, hb:8:2], P),
                                    ALU.subtract).then_inc(free(("dec", i, hb)), 1)
                    job_read(dve, ("dec", i, hb))
                    V.tensor_tensor(D, D, FOUR(hide_e), ALU.min).then_inc(S("exponents"), 1)
                    dve.wait_ge(S("decay_matrix"), 2 * i + hb + 1)
                    for name, dst in (("kk", AT), ("kq", AQ)):
                        b = full_bank(dve, (name, i, hb))
                        V.tensor_tensor(dst, b[:, :].rearrange("p (m c) -> p m c", m=4), D, ALU.mult)\
                            .then_inc(free((name, i, hb)), 1)
                    job_read(dve, ("kq", i, hb))
                    job_read(dve, ("kk", i, hb))
                    dve.sem_inc(S("decay_used"), 1)
                for lv in range(7):
                    for hb in range(2):
                        D, AT, AQ, X, Y, M0, M1 = BATCH[hb]
                        for name, dst in (("X", X), ("Y", Y)):
                            if lv == 6 and name == "X":
                                continue
                            b = full_bank(dve, (name, i, hb, lv))
                            V.tensor_tensor(dst, dst, b[:, :].rearrange("p (m c) -> p m c", m=4), ALU.subtract)\
                                .then_inc(free((name, i, hb, lv)), 1)
                    key_group()
                dve.wait_ge(S("decays"), 3)
                b = full_bank(dve, ("o", i))
                O8 = q8
                V.tensor_copy(O8, b[:, :].rearrange("p (h d) -> p h d", h=8)).then_inc(free(("o", i)), 1)
                b = full_bank(dve, ("dS", i))
                for a_ in range(2):
                    r_ = slice(a_ * HD, a_ * HD + HD)
                    own = ST[r_, :, r_]
                    step(V.tensor_tensor(own, own, wide(GL[:, i, :].rearrange("p (j a) -> p a j", a=2)[r_, a_, :], HD), ALU.mult))
                settle()
                for a_ in range(2):
                    r_ = slice(a_ * HD, a_ * HD + HD)
                    ins = V.tensor_tensor(ST[r_, :, r_], ST[r_, :, r_], b[:, :].rearrange("p (j c) -> p j c", j=4)[r_, :, r_], ALU.add)
                    ins.then_inc(free(("dS", i)), 1) if a_ else step(ins)
                settle()
                job_read(dve, ("dS", i))
                dve.sem_inc(S("state"), 2)
                job_read(dve, ("o", i))
                t8 = three(SQ[:, 0:512])
                step(V.tensor_tensor(t8, O8, O8, ALU.mult))
                settle()
                V.tensor_reduce(RQ[:, 0:8], t8, AXX, ALU.add).then_inc(S("o_ss"), 1)
                step(V.tensor_tensor(three(GZ[:, i, :]), three(GZ[:, i, :]), NW.rearrange("p (o d) -> p o d", o=1).to_broadcast([P, 8, HD]), ALU.mult))
                settle()
                step(V.tensor_tensor(O8, O8, three(GZ[:, i, :]), ALU.mult))
                dve.wait_ge(S("o_root"), i + 1)
                step(V.reciprocal(RQ[:, 0:8], RQ[:, 0:8]))
                settle()
                step(V.tensor_tensor(O8, O8, wide(RQ[:, 0:8], HD), ALU.mult))
                settle()
                dve.sem_inc(S("gdn_out"), 1)
                mod_row(8 + i, 8 + i)
            while kg[0] < 32:
                key_group()
            for half in range(2):
                b = full_bank(dve, ("lp", half))
                V.tensor_copy(SLOT2[:, 2112 + half * 512:2624 + half * 512], b[:, :]).then_inc(free(("lp", half)), 1)
            dve.wait_ge(S("kred"), 32)
            TP = LG.rearrange("p (h b g) -> p h b g", h=HEADS, b=NB)
            for half in range(2):
                hs = slice(half * 4, half * 4 + 4)
                as4 = lambda b: b[:, :].rearrange("p (h b g) -> p h b g", h=4, b=NB)
                b = full_bank(dve, ("lsum", half))
                V.tensor_tensor(SC[:, hs, :, 0:16].rearrange("p h b g -> p (h b) g"), SC[:, hs, :, 0:16].rearrange("p h b g -> p (h b) g"),
                                b[:, :].rearrange("p (n g) -> p n g", g=16), ALU.add).then_inc(free(("lsum", half)), 1)
                b = full_bank(dve, ("ltot", half))
                V.tensor_copy(LG[:, half * 512:(half + 1) * 512], b[:, :]).then_inc(free(("ltot", half)), 1)
            job_read(dve, ("lsum", 1))
            job_read(dve, ("ltot", 1))
            for g in range(14, -1, -1):
                step(V.tensor_tensor(TP[:, :, :, g], TP[:, :, :, g], TP[:, :, :, g + 1], ALU.add))
                settle()
            flat = lambda v: v.rearrange("p h b g -> p (h b) g")
            step(V.tensor_tensor(flat(SC[:, :, :, 0:15]), flat(SC[:, :, :, 0:15]), flat(TP[:, :, :, 1:16]), ALU.add))
            dve.wait_ge(S("new_in"), 32)
            settle()
            step(V.tensor_tensor(SC[:, :, :, 0:16], SC[:, :, :, 0:16],
                                 LNB.rearrange("p (b h o) -> p h b o", h=8, o=1).to_broadcast([P, 8, 8, 16]), ALU.add))
            settle()
            V.tensor_reduce(M64, flat(SC), AXX, ALU.max).then_inc(S("smax"), 1)
            b = full_bank(dve, "smT")
            V.tensor_reduce(SMX[0:64, :], b[0:64, 0:P], AXX, ALU.max).then_inc(free("smT"), 1)
            job_read(dve, "smT")
            V.tensor_scalar(TDG[0:64, :], ident[0:64, 0:64], SMX[0:64, :], None, ALU.mult).then_inc(S("smax"), 1)
            b = full_bank(dve, "smB")
            V.tensor_tensor(flat(SC), flat(SC), wide(b[:, 0:64], 17), ALU.subtract).then_inc(free("smB"), 1)
            job_read(dve, "smB")
            dve.sem_inc(S("sshift"), 1)
            dve.wait_ge(S("sexp"), 1)
            V.tensor_reduce(M64, flat(SC), AXX, ALU.add).then_inc(S("ssums"), 1)
            b = full_bank(dve, "ssum")
            V.reciprocal(SRCP, b[:, 0:64]).then_inc(free("ssum"), 1)
            job_read(dve, "ssum")
            V.tensor_tensor(flat(SC), flat(SC), wide(SRCP, 17), ALU.mult).then_inc(S("probs"), 1)
            for bb in range(NB):
                b = full_bank(dve, ("pv", bb))
                step(V.tensor_copy(HT[0:64, 4:8, SEQ + bb], b[0:64, 0:8:2]))
                V.tensor_copy(HT[64:128, 4:8, SEQ + bb], b[64:128, 1:8:2]).then_inc(free(("pv", bb)), 1)
            dve.wait_ge(S("x1_in"), 32)
            dve.wait_ge(S("g1_in"), 32)
            nth = 0
            for c in range(2):
                for t in range(5):
                    n = P if t < 4 else NB
                    cs = slice(c * 512, (c + 1) * 512)
                    b = full_bank(dve, ("wo", c, t))
                    tmp = TMPX[0:n, nth % 2, :]
                    V.tensor_tensor(tmp, b[0:n, :], MV[0:n, 0 if t < 4 else 1, cs], ALU.mult).then_inc(free(("wo", c, t)), 1)
                    job_read(dve, ("wo", c, t))
                    if nth >= 2:
                        dve.wait_ge(S("x1_part"), nth - 1)
                    V.tensor_tensor(X1[0:n, t, cs], X1[0:n, t, cs], tmp, ALU.add).then_inc(S("x1_part"), 1)
                    nth += 1
            dve.wait_ge(S("x1_part"), 10)
            dve.wait_ge(S("mv2_in"), 64)
            for t in range(5):
                n = P if t < 4 else NB
                mv = MV[:, 2:4, :] if t < 4 else MVS2
                norm_mod(5 + t, X1[0:n, t, :], H2[0:n, t, :], n, mv[0:n, 0, :], mv[0:n, 1, :], (SS[0:n, t:t + 1], SS[0:n, 5 + t:6 + t]))
            dve.wait_ge(S("h_ready"), 10)
            dve.wait_ge(S("iota"), 3)
            step(V.tensor_copy(IOTA16, IOTAI))
            job_done(dve, ("qTs", 3))
            step(V.memset(ACC, 0.0))
            settle()
            base = count[0]
            clock = [lambda: count[0]]

            def calm(plain=False):
                dve.wait_ge(S("dve_steps"), clock[0]())
                if plain:
                    dve.sem_inc(S("dve_pace"), 1)

            def top16(rows, n_parts, val, vals16, idx16):
                for rnd in range(2):
                    for p_ in range(n_parts):
                        step(V.max(vals16(p_)[rows, rnd * 8:rnd * 8 + 8], val(p_)[rows]))
                    calm(True)
                    for p_ in range(n_parts):
                        step(V.max_index(idx16(p_)[rows, rnd * 8:rnd * 8 + 8], vals16(p_)[rows, rnd * 8:rnd * 8 + 8], val(p_)[rows]))
                    if rnd == 0:
                        calm(True)
                        for p_ in range(n_parts):
                            step(V.match_replace(val(p_)[rows], vals16(p_)[rows, 0:8], val(p_)[rows], NEG))
                        calm(True)

            def pick(n, src, fv, eix):
                rows = slice(0, n)
                step(V.tensor_copy(SX[rows], src))
                calm(True)
                top16(rows, 2, lambda p_: SX[:, p_, :], lambda p_: V16[:, p_, :], lambda p_: I16[:, p_, :])
                calm()
                step(V.tensor_copy(IF[rows], I16[rows]))
                step(V.tensor_tensor(CAND[rows].rearrange("p (i j) -> p i j", i=16), wide(V16[rows, 0, :], 16),
                                     V16[rows, 1:2, :].to_broadcast([n, 16, 16]), ALU.add))
                calm(True)
                top16(rows, 1, lambda p_: CAND, lambda p_: fv, lambda p_: FI)
                calm()
                step(V.tensor_scalar(IJ[rows, 0, :], FI[rows], 4, 0, ALU.logical_shift_right, ALU.bitwise_or))
                step(V.tensor_scalar(IJ[rows, 1, :], FI[rows], 15, 0, ALU.bitwise_and, ALU.bitwise_or))
                calm()
                step(V.tensor_copy(IJF[rows], IJ[rows]))
                calm()
                iota = IOTA16[rows].rearrange("p (a b n) -> p a b n", a=1, b=1).to_broadcast([n, 2, 16, 16])
                step(V.tensor_tensor(OH[rows], iota, IJF[rows].rearrange("q p (n o) -> q p n o", o=1).to_broadcast([n, 2, 16, 16]), ALU.is_equal))
                calm()
                step(V.tensor_tensor(OH[rows], OH[rows], IF[rows].rearrange("q p (o n) -> q p o n", o=1).to_broadcast([n, 2, 16, 16]), ALU.mult))
                calm()
                step(V.tensor_reduce(R01[rows], OH[rows], AXX, ALU.add))
                calm()
                step(V.scalar_tensor_tensor(eix, R01[rows, 0, :], float(NKEY), R01[rows, 1, :], ALU.mult, ALU.add))

            def pick_prompt(h, t):
                pick(P, QT[:, bass.ds(2 * h, 2), t * P:(t + 1) * P], FVS[:, t, :], EIX[:, t, :])
                step(V.tensor_scalar(NMX[:, t:t + 1], FVS[:, t, 0:1], -1.0, None, ALU.mult))
                calm()
                dve.sem_inc(S("picked"), 1)

            def pick_sample(h):
                pick(NB, SCS[0:NB, bass.ds(h * 256, 256)].rearrange("p (a n) -> p a n", a=2), FVT, EISF[0:NB, bass.ds(h * 16, 16)])
                step(V.tensor_copy(FVSS[0:NB, bass.ds(h * 16, 16)], FVT[0:NB, :]))

            def dots(n_, t, s0, s1):
                for s_ in range(s0, s1):
                    dve.wait_ge(S(f"u_in{s_ % 4}"), n_ * 64 + 16 * (s_ // 4 + 1))
                    g = UR[:, s_ % 4, :]
                    V.scalar_tensor_tensor(g, g, 1.0, H2[:, t, :], ALU.mult, ALU.mult, accum_out=DOT[:, t, s_:s_ + 1]).then_inc(S("dots"), 1)

            def weigh(n_, t):
                dve.wait_ge(S("gate_raw"), n_ + 1)
                step(V.reciprocal(SUMG[:, t:t + 1], SUMG[:, t:t + 1]))
                dve.wait_ge(S("gelu"), n_ + 1)
                calm()
                V.scalar_tensor_tensor(AG[:, t, :], AG[:, t, :], SUMG[:, t:t + 1], GAT[:, t, :], ALU.mult, ALU.mult).then_inc(S("weights"), 1)

            def gather_sums(n_, t):
                dve.wait_ge(S("v_used"), n_ * 16 + 16 + 8)
                for half in range(2):
                    b = banks[(t % 2) * 2 + half]
                    v = ACC[:, t, half * 512:(half + 1) * 512]
                    step(V.tensor_tensor(v, v, b[:, :], ALU.add))
                calm()
                dve.sem_inc(S("sums_free"), 1)

            def peer_vector(h, last):
                for t in range(TILES):
                    n_ = h * 4 + t
                    if not (last and t == 3):
                        dots(n_ + 1, (t + 1) % 4, 0, 8)
                    if not (last and t >= 2):
                        pick_prompt(h + (1 if t >= 2 else 0), (t + 2) % 4)
                    if not (last and t == 3):
                        dots(n_ + 1, (t + 1) % 4, 8, 16)
                        weigh(n_ + 1, (t + 1) % 4)
                    if t == 1:
                        pick_sample(h)
                    gather_sums(n_, t)

            for t in range(5):
                for q in range(4):
                    job_read(dve, ("score", t, q))
            pick_prompt(0, 0)
            pick_prompt(0, 1)
            dots(0, 0, 0, 16)
            weigh(0, 0)
            base = count[0]
            with dve.Fori(0, PH - 1) as h:
                clock[0] = lambda: h * LOOP_STEPS + count[0]
                peer_vector(h, False)
                assert count[0] - base == LOOP_STEPS, (count[0] - base)
            count[0] += (PH - 2) * LOOP_STEPS
            clock[0] = lambda: count[0]
            peer_vector(PH - 1, True)
            settle()
            f3 = FVSS[0:NB, :].rearrange("p (h k) -> p h k", h=PH)
            dve.sem_inc(S("sample_picks"), 1)
            step(V.tensor_copy(OH[0:NB, 0, 0, 0:8], f3[:, :, 0]))
            settle()
            V.tensor_tensor(f3, f3, wide(OH[0:NB, 0, 0, 0:8], 16), ALU.subtract).then_inc(S("sample_shift"), 1)
            dve.wait_ge(S("sample_exp"), 1)
            step(V.tensor_reduce(OH[0:NB, 0, 0, 0:8], f3, AXX, ALU.add))
            settle()
            step(V.reciprocal(OH[0:NB, 0, 0, 0:8], OH[0:NB, 0, 0, 0:8]))
            settle()
            V.tensor_tensor(f3, f3, wide(OH[0:NB, 0, 0, 0:8], 16), ALU.mult).then_inc(S("sample_picks"), 1)
            b = full_bank(dve, "ixT")
            V.tensor_copy(IXT, b[:, 0:8]).then_inc(S("sample_ix"), 1)
            V.tensor_copy(GTT, b[:, 8:16]).then_inc(free("ixT"), 1)
            for t in range(NB):
                dve.wait_ge(S(f"u_in{t % 4}"), 16 * (128 + t // 4 + 1))
                dve.wait_ge(S(f"h2b_in{t % 2}"), 16 * (t // 2 + 1))
                g = UR[:, t % 4, :]
                V.scalar_tensor_tensor(g, g, 1.0, H2B[:, t % 2, :], ALU.mult, ALU.mult, accum_out=DOTS[:, t:t + 1]).then_inc(S("sample_dots"), 1)
            step(V.memset(AM, 0.0))
            dve.wait_ge(S("sample_gelu"), 1)
            job_read(dve, "ixT")
            settle()
            V.tensor_tensor(AM[:, 0:64:9], DOTS, GTT, ALU.mult).then_inc(S("sample_gates"), 1)
            dve.wait_ge(S("g2_in"), 48)

            def finish(t, n, y, mv):
                settle()
                step(V.tensor_tensor(y, y, X1[0:n, t, :], ALU.add))
                settle()
                V.scalar_tensor_tensor(H2[0:n, t, :], y, 1.0, y, ALU.mult, ALU.mult, accum_out=SS[0:n, t:t + 1]).then_inc(S("sumsq"), 1)
                dve.wait_ge(S("root"), 10 + t + 1)
                step(V.reciprocal(SS[0:n, 5 + t:6 + t], SS[0:n, 5 + t:6 + t]))
                settle()
                V.scalar_tensor_tensor(y, y, SS[0:n, 5 + t:6 + t], MV[0:n, 2, :], ALU.mult, ALU.mult).then_inc(S("y_ready"), 1)

            for t in range(TILES):
                step(V.tensor_tensor(ACC[:, t, :], ACC[:, t, :], MV[:, 0, :], ALU.mult))
                finish(t, P, ACC[:, t, :], 0)
            dve.wait_ge(S("v_used"), 32 * 16 + 8 + NB)
            ys = UR[0:NB, 0, :]
            for half in range(2):
                c = slice(half * 512, (half + 1) * 512)
                step(V.tensor_tensor(ys[:, c], banks[half][0:NB, :], MV[0:NB, 1, c], ALU.mult))
            finish(4, NB, ys, 1)

        @block.gpsimd
        def _(pool):
            nc.gpsimd.iota(ints[:, 0, :], [[0, P]], base=0, channel_multiplier=1).then_inc(S("iota"), 1)
            nc.gpsimd.iota(ints[:, 1, :], [[1, P]], base=0, channel_multiplier=0).then_inc(S("iota"), 1)
            T = nc.gpsimd.tensor_tensor
            n = [0]

            def step(ins):
                n[0] += 1
                ins.then_inc(S("pool_steps"), 1)
                pool.wait_ge(S("pool_steps"), n[0])

            for g in range(3):
                pool.wait_ge(S("sconv_in"), 32 * (g + 1))
                pool.wait_ge(S("sample_raw"), g + 1)
                x = SRAW(g)
                step(T(SCONV(g), x, SCW[0:NB, 3, :], ALU.mult))
                for j in range(3):
                    step(T(STMP[0:NB, :], SST[0:NB, j, :], SCW[0:NB, j, :], ALU.mult))
                    step(T(SCONV(g), SCONV(g), STMP[0:NB, :], ALU.add))
                pool.sem_inc(S("sconv_done"), 1)
            pool.wait_ge(S("psbuf_free"), 1)
            nc.gpsimd.memset(FA[0:2, :, :], 1.0).then_inc(S("frow_ones"), 1)
            nc.gpsimd.memset(FB[0:2, :, :], 1.0).then_inc(S("frow_ones"), 1)
            SR = slice(0, 64)
            over_v = lambda v: wide(v, HD)
            over_k = lambda v: v.rearrange("p (o d) -> p o d", o=1).to_broadcast([64, HD, HD])
            pool.wait_ge(S("srule"), 2)
            T(SSP[SR], SS0[SR], over_v(SV[SR, 1, :]), ALU.mult).then_inc(S("srule_pool"), 1)
            pool.wait_ge(S("srule"), 3)
            T(SSP[SR], over_v(SV[SR, 1, :]), over_k(SV[SR, 2, :]), ALU.mult).then_inc(S("srule_pool"), 1)
            pool.wait_ge(S("srule"), 4)
            T(SSP[SR], SS0[SR], over_v(SV[SR, 0, :]), ALU.mult).then_inc(S("srule_pool"), 1)
            pool.wait_ge(S("pages_in"), 16)
            job_done(pool, last_job[8])
            nc.gpsimd.indirect_dma_start(LG, None, a["cache_logf"][0].rearrange("n p h -> n (p h)"),
                                         bass.IndirectOffsetOnAxis(ap=PTI, axis=0)).then_inc(S("logf_pages"), 16)
            def mask(i, lv):
                for hb in range(2):
                    AT, M = BATCH[hb][1], BATCH[hb][5 + lv % 2]
                    if lv == 0:
                        pool.wait_ge(S("decay_used"), 2 * i + hb + 1)
                        if i:
                            job_done(pool, ("T", i - 1, hb, 6))
                    elif lv >= 2:
                        job_done(pool, ("T", i, hb, lv - 2))
                    T(M, AT, level[:, lv:lv + 1, :].to_broadcast([P, 4, P]), ALU.mult).then_inc(S(f"level{hb}"), 1)

            kg = [0]

            def key_group():
                n_ = kg[0]
                if n_ == 32:
                    return
                kg[0] += 1
                pool.wait_ge(S(f"kv_in{n_ % 2}"), 64 * (n_ // 2 + 1))
                pool.wait_ge(S(f"qb_in{n_ // 4 % 2}"), 16 * (n_ // 8 + 1))
                k = KG4[n_ % 2]
                T(k, k, QB[:, n_ // 4 % 2:n_ // 4 % 2 + 1, :].to_broadcast([P, 4, 512]), ALU.mult).then_inc(S("kprod"), 1)

            for i in range(TILES):
                mask(i, 0)
                mask(i, 1)
                for lv in range(7):
                    key_group()
                    if lv + 2 < 7:
                        mask(i, lv + 2)
            while kg[0] < 32:
                key_group()
            nc.gpsimd.iota(IOTAI, [[1, 16]], base=0, channel_multiplier=0).then_inc(S("iota"), 1)

            pu, pv = a["peer_u"][0], a["peer_v"][0]

            def ready(sem, value):
                pool.wait_ge(S(sem), value)
                pool.sem_inc(S("pool_pace"), 1)

            def gather(dst, table, idx, sem):
                nc.gpsimd.indirect_dma_start(dst, None, table, bass.IndirectOffsetOnAxis(ap=idx, axis=0)).then_inc(S(sem), 16)

            pool.sem_inc(S("v_used"), 8)
            pool.sem_inc(S("sums_free"), 2)
            job_done(pool, last_job[-1])
            job_done(pool, last_job[-2])
            pool.wait_ge(S("picked"), 1)
            for s_ in range(16):
                if s_ >= 4:
                    pool.wait_ge(S("dots"), s_ - 3)
                gather(UR[:, s_ % 4, :], pu, EIX[:, 0, s_:s_ + 1], f"u_in{s_ % 4}")

            def peer_gathers(h, last):
                for t in range(TILES):
                    n_ = h * 4 + t
                    more = not (last and t == 3)
                    if more:
                        ready("picked", n_ + 2)
                    for s_ in range(16):
                        if more:
                            ready("dots", n_ * 16 + 16 + s_ - 3)
                            gather(UR[:, s_ % 4, :], pu, EIX[:, (t + 1) % 4, s_:s_ + 1], f"u_in{s_ % 4}")
                        ready("v_used", n_ * 16 + s_ + 1)
                        gather(VR[:, s_ % 8, :], pv, EIX[:, t, s_:s_ + 1], f"v_in{s_ % 8}")

            with pool.Fori(0, PH - 1) as h:
                peer_gathers(h, False)
            peer_gathers(PH - 1, True)
            pool.wait_ge(S("sample_ix"), 1)
            for t in range(NB):
                if t < 4:
                    pool.wait_ge(S("dots"), 32 * 16)
                else:
                    pool.wait_ge(S("sample_dots"), t - 3)
                gather(UR[:, t % 4, :], pu, IXT[:, t:t + 1], f"u_in{t % 4}")
            for t in range(NB):
                pool.wait_ge(S("v_used"), 32 * 16 + t + 1)
                gather(VR[:, t, :], pv, IXT[:, t:t + 1], f"v_in{t}")

        @block.sync
        def _(sp):
            def load(dst, src, sem, **k):
                sp.dma_start(dst, src, **k).then_inc(S(sem), 16)

            stored = {}

            def store(dst, src, sem):
                sp.dma_start(dst, src, allow_slow_non_contiguous=src.shape[-1] == 1).then_inc(S(sem), 16)
                stored[sem] = stored.get(sem, 0) + 16

            load(C9[0:1, :], a["c_prompt"], "c_in")
            load(C9[1:9, :], a["c_sample"], "c_in")
            load(CWN, a["conv_w"][0].rearrange("j (b c) -> (j b) c", c=P), "conv_w_in")

            def chunk(n):
                name, src = chunks[n]
                if before[n] is not None:
                    job_done(sp, last_job[before[n]])
                load(slot(name), src, f"ring{slot_of[n]}_loaded")

            def bmod(j):
                if j >= 2:
                    sp.wait_ge(S("mod_row"), j - 1)
                load(BMR[0:9, j % 2, :], a["b_mod"][:, j * 512:(j + 1) * 512].to_broadcast([9, 512]), f"bmod{j % 2}")

            def mod_store(j):
                sp.wait_ge(S("mod_row"), j + 1)
                store(mod_d[:, j * 512:(j + 1) * 512], MR[0:9, j % 2, :], f"mod_out{j % 2}")

            def x_load(t):
                if t >= 2:
                    sp.wait_ge(S("h_ready"), t - 1)
                src = a["x_prompt"][0, t * P:(t + 1) * P, :] if t < 4 else a["x_sample"][:, 0, :]
                load(XR[0:(P if t < 4 else NB), t % 2, :], src, f"x_in{t % 2}")

            chunk(0)
            bmod(0)
            bmod(1)
            chunk(1)
            chunk(2)
            load(BIAS[:, 0, :], a["dt_bias"].to_broadcast([P, 8]), "bias_in")
            load(BIAS[:, 1, :], a["fox_fb"].to_broadcast([P, 8]), "bias_in")
            load(BIAS[:, 2, :], a["a_log"].to_broadcast([P, 8]), "bias_in")
            x_load(0)
            x_load(1)
            for j in range(4):
                chunk(j + 3)
                mod_store(j)
                if j + 2 < 4:
                    bmod(j + 2)
            sp.wait_ge(S("mod_out0"), 32)
            sp.wait_ge(S("mod_out1"), 32)
            for i, at in enumerate((0, D_MODEL)):
                load(MV[:, i, :], mod_d[0:1, at:at + D_MODEL].to_broadcast([P, D_MODEL]), "mv_prompt")
            for i, at in enumerate((0, D_MODEL)):
                load(MV[0:NB, 2 + i, :], mod_d[1:9, at:at + D_MODEL], "mv_sample")
            for t in range(2, 5):
                x_load(t)

            def sconv_load(g):
                if g:
                    sp.wait_ge(S("sconv_done"), g)
                load(SST[0:NB, :, :], a["state_conv"][0, :, :, g * 512:(g + 1) * 512], "sconv_in")
                load(SCW[0:NB, :, :], a["conv_w"][:, :, g * 512:(g + 1) * 512].to_broadcast([NB, 4, 512]), "sconv_in")

            for n in range(7, 11):
                chunk(n)
            bmod(4)
            bmod(5)
            for t in range(TILES):
                job_read(sp, ("fv", t))
                store(o["v_prompt"][0, 0, t * P:(t + 1) * P].rearrange("t h d -> t (h d)"), VT[:, t, :], "results_out")
            job_read(sp, ("fv", 4))
            store(o["v_sample"][0, :, 0].rearrange("b h d -> b (h d)"), PS[0:NB, COL_FV:COL_FV + 512], "samples_out")
            for t in range(TILES):
                sp.wait_ge(S("ktok_copied"), t + 1)
                store(o["k_prompt"][0, 0, t * P:(t + 1) * P].rearrange("t h d -> t (h d)"), KO[:, t % 2, :], f"k_out{t % 2}")
            for n in range(11, 13):
                chunk(n)
            job_read(sp, ("fk", 4))
            store(o["k_sample"][0, :, 0].rearrange("b h d -> b (h d)"), PS[0:NB, COL_FK:COL_FK + 512], "samples_out")
            sp.wait_ge(S("sample_raw"), 3)
            sp.wait_ge(S("k_out0"), 32)
            sp.wait_ge(S("k_out1"), 32)
            job_done(sp, ("cvT", 11))
            for g in range(3):
                sconv_load(g)
            store(o["conv_sample"][0, :, 0:2], a["state_conv"][0, :, 1:3], "samples_out")
            store(o["conv_sample"][0, :, 2], PS[0:NB, 0:CONV], "samples_out")
            sp.wait_ge(S("tail_out"), 3)
            store(o["conv_prompt"][0, 0], TAILO[0:3, :], "samples_out")
            sp.wait_ge(S("gates_ready"), 1)
            store(o["logf_prompt"][0, 0].rearrange("(t p) h -> p t h", p=P), LOGF[:, 0:4, :], "results_out")
            store(o["logf_sample"][0, :, 0], LOGF[0:NB, 4, :], "results_out")
            sp.wait_ge(S("sconv_silu"), 1)
            for n in range(3):
                store(samp_d[:, n, :], PSC[0:NB, n * 512:(n + 1) * 512], "samp_out")
            store(samp_d[:, 3, :], PS[0:NB, COL_Z:COL_Z + 512], "samp_out")
            store(samp_d[:, 4, :], PS[0:NB, COL_FQ:COL_FQ + 512], "samp_out")
            store(sgate_d[0], BETA[0:NB, 4, :], "samp_out")
            store(sgate_d[1], G[0:NB, 4, :], "samp_out")
            sp.wait_ge(S("new_score"), 1)
            store(sgate_d[2], SN[0:NB, :], "samp_out")
            sp.wait_ge(S("frows"), 1)
            store(frow_d[0], FR[0:8, :], "frow_out")
            store(frow_d[1], NFR[0:8, :], "frow_out")
            for sem in ("samp_out", "frow_out", "samples_out"):
                sp.wait_ge(S(sem), stored[sem])
            sp.sem_inc(S("psbuf_free"), 1)

            def frow_load(h):
                if h >= 2:
                    job_done(sp, ("sc", 4 * (h - 2) + 3))
                load(FA[1:2, h % 2, :], frow_d[0, h:h + 1, :], f"frow_in{h % 2}")
                load(FB[0:1, h % 2, :], frow_d[1, h:h + 1, :], f"frow_in{h % 2}")

            sp.wait_ge(S("frow_ones"), 2)
            frow_load(0)
            frow_load(1)
            by_head = "b (h d) -> b h d"
            load(SS0[0:64].rearrange("p k v -> p (k v)"), a["state_delta"][0].rearrange("b h k v -> (b h) (k v)"), "srule_in")
            for n in range(4):
                load(SV[0:64, n, :], samp_d[:, n, :].rearrange(by_head, h=8), "srule_in")
            load(SSM[0:64, 0:1], sgate_d[0].rearrange("b (h o) -> b h o", o=1), "srule_in", allow_slow_non_contiguous=True)
            load(SSM[0:64, 1:2], sgate_d[1].rearrange("b (h o) -> b h o", o=1), "srule_in", allow_slow_non_contiguous=True)
            load(NW, a["gdn_norm_w"].to_broadcast([P, HD]), "srule_in")
            load(PTI, a["page_table"].rearrange("b (g o) -> (b g) o", o=1).bitcast(U32), "pages_in", allow_slow_non_contiguous=True)
            load(PTB, a["page_table"].rearrange("(o b) g -> o (b g)", o=1), "table_in")
            load(LNB, o["logf_sample"][0, :, 0].rearrange("(o b) h -> o (b h)", o=1).to_broadcast([P, 64]), "new_in")
            mod_store(4)
            for h in range(2, 8):
                frow_load(h)
                if h % 2 == 1:
                    bmod(4 + (h - 1) // 2 + 1)
                    chunk(12 + (h - 1) // 2)
                    mod_store(4 + (h - 1) // 2)
            sp.wait_ge(S("srule"), 4)
            store(o["delta_sample"][0].rearrange("b h k v -> (b h) (k v)"), SS0[0:64].rearrange("p k v -> p (k v)"), "srule_stored")
            sp.wait_ge(S("srule"), 6)
            store(samp_d[:, 5, :].rearrange(by_head, h=8), SV[0:64, 4, :], "srule_stored")
            sp.wait_ge(S("srule_stored"), 32)
            load(OGS, samp_d[:, 5, :], "ogs_in")

            def cache_group(cache, n, b, q):
                for g in range(4):
                    at = b * PAGES + q * 4 + g
                    page = sp.value_load(PTB[0:1, at:at + 1], min_val=0, max_val=a["cache_k"].shape[1] - 1)
                    load(KG4[n % 2][:, g, :], a[cache][0, bass.ds(page, 1)].rearrange("o p h d -> p (o h d)"), f"kv_in{n % 2}")

            sp.wait_ge(S("table_in"), 16)
            sp.wait_ge(S("scores_cleared"), 1)
            load(SC[0:1, :, :, 16], sgate_d[2:3].rearrange("o b h -> o h b"), "new_in", allow_slow_non_contiguous=True)
            job_done(sp, ("fo", 31))
            for n in range(32):
                b, q = divmod(n, 4)
                if q == 0:
                    if b >= 2:
                        sp.wait_ge(S("kprod"), 4 * (b - 1))
                    load(QB[:, b % 2, :], samp_d[b:b + 1, 4, :].to_broadcast([P, 512]), f"qb_in{b % 2}")
                if n >= 2:
                    sp.wait_ge(S("kred"), n - 1)
                cache_group("cache_k", n, b, q)
                if n % 7 == 2:
                    m = n // 7
                    if m:
                        mod_store(7 + m)
                    if m < 3:
                        bmod(9 + m)
                    chunk(16 + m)
            for n in range(32):
                b, q = divmod(n, 4)
                if n < 2:
                    sp.wait_ge(S("kred"), 31 + n)
                else:
                    sp.wait_ge(S("kv_used"), n - 1)
                cache_group("cache_v", n, b, q)
                if q == 0:
                    if b >= 2:
                        job_done(sp, ("pv", b - 2))
                    load(VNEW[:, (b % 2) * 512:(b % 2) * 512 + 512], o["v_sample"][0, b:b + 1, 0].rearrange("b h d -> b (h d)"), f"vnew_in{b % 2}")
            sp.wait_ge(S("gdn_out"), 4)
            sp.wait_ge(S("state"), 9)
            for r_ in range(2):
                store(o["delta_prompt"][0, 0].rearrange("(j a) d e -> a d j e", a=2)[r_], ST[r_ * HD:r_ * HD + HD, :, r_ * HD:r_ * HD + HD], "results_out")
            job_done(sp, ("dS", 3))
            load(X1[:, 0:4, :], a["x_prompt"][0].rearrange("(t p) d -> p t d", p=P), "x1_in")
            load(X1[0:NB, 4, :], a["x_sample"][:, 0, :], "x1_in")
            load(MV[:, 0, :], mod_d[0:1, 2 * D_MODEL:3 * D_MODEL].to_broadcast([P, D_MODEL]), "g1_in")
            load(MV[0:NB, 1, :], mod_d[1:9, 2 * D_MODEL:3 * D_MODEL], "g1_in")
            job_done(sp, ("oT", 4, 0))
            job_done(sp, ("pv", 7))
            sp.wait_ge(S("mod_out0"), 96)
            sp.wait_ge(S("mod_out1"), 96)
            load(KN, a["peer_subkeys"][0].rearrange("h p n c -> n (h p) c"), "keys_in")
            for i in range(2):
                at = (3 + i) * D_MODEL
                load(MV[:, 2 + i, :], mod_d[0:1, at:at + D_MODEL].to_broadcast([P, D_MODEL]), "mv2_in")
                load(MVS2[0:NB, i, :], mod_d[1:9, at:at + D_MODEL], "mv2_in")
            for n in range(21, 25):
                chunk(n)
            sp.wait_ge(S("x1_part"), 10)
            load(MV[:, 0, :], mod_d[0:1, 5 * D_MODEL:6 * D_MODEL].to_broadcast([P, D_MODEL]), "g2_in")
            load(MV[0:NB, 1, :], mod_d[1:9, 5 * D_MODEL:6 * D_MODEL], "g2_in")
            sp.wait_ge(S("h_ready"), 10)
            load(MV[:, 2, :], a["final_norm_w"].rearrange("(o d) -> o d", o=1).to_broadcast([P, D_MODEL]), "g2_in")
            store(h2s_d, H2[0:NB, 4, :], "h2s_out")
            sp.wait_ge(S("h2s_out"), 16)
            sp.wait_ge(S("sample_picks"), 1)
            for t in range(NB):
                if t >= 2:
                    sp.wait_ge(S("sample_dots"), t - 1)
                load(H2B[:, t % 2, :], h2s_d[t:t + 1, :].to_broadcast([P, D_MODEL]), f"h2b_in{t % 2}")
            for t in range(TILES):
                sp.wait_ge(S("y_ready"), t + 1)
                store(o["y_prompt"][0, t * P:(t + 1) * P, :], ACC[:, t, :], "results_out")
            sp.wait_ge(S("y_ready"), 5)
            store(o["y_sample"][:, 0, :], UR[0:NB, 0, :], "results_out")
            for sem, n in stored.items():
                sp.wait_ge(S(sem), n)


_OUTS = [("y_prompt", (1, SEQ, D_MODEL)), ("y_sample", (NB, 1, D_MODEL)),
         ("k_prompt", (1, 1, SEQ, HEADS, HD)), ("v_prompt", (1, 1, SEQ, HEADS, HD)), ("logf_prompt", (1, 1, SEQ, HEADS)),
         ("conv_prompt", (1, 1, 3, CONV)), ("delta_prompt", (1, 1, HEADS, HD, HD)),
         ("k_sample", (1, NB, 1, HEADS, HD)), ("v_sample", (1, NB, 1, HEADS, HD)), ("logf_sample", (1, NB, 1, HEADS)),
         ("conv_sample", (1, NB, 3, CONV)), ("delta_sample", (1, NB, HEADS, HD, HD))]


def kernel(**inputs):
    import concourse.bacc as _bacc
    import numpy as _np
    from concourse import mybir as _mybir
    from concourse.bass_utils import run_bass_kernel_spmd as _run

    nc = _bacc.Bacc("TRN2", target_bir_lowering=False, num_devices=1)
    arrays, ins, outs = {}, {}, {}
    for name, value in inputs.items():
        v = _np.ascontiguousarray(value)
        arrays["in_" + name] = v
        ins[name] = nc.dram_tensor("in_" + name, v.shape, _mybir.dt.from_np(v.dtype), kind="ExternalInput").ap()
    for name, shape in _OUTS:
        outs[name] = nc.dram_tensor("out_" + name, shape, _mybir.dt.float32, kind="ExternalOutput").ap()
    hybrid_decoder_step(nc, ins, outs)
    r = _run(nc, [arrays], core_ids=[0])
    return tuple(r.results[0]["out_" + name] for name, _ in _OUTS)
```

```python
from contextlib import ExitStack

import concourse.bass as bass
from concourse import mybir

F32 = mybir.dt.float32
U32 = mybir.dt.uint32
I32 = mybir.dt.int32
ALU = mybir.AluOpType
ACT = mybir.ActivationFunctionType
AXX = mybir.AxisListType.X

P = 128
D_MODEL, SEQ, NB = 1024, 512, 8
HEADS, HD = 8, 64
WID = HEADS * HD
PAGES = 16
KT = D_MODEL // P
TILES = SEQ // P
TOK = SEQ + NB
CONV = 3 * WID
TAPS = 4
NEXP, NKEY, TOPK, PH = 16384, 128, 16, 8
NEG = -1.0e30
EPS = 1e-6
SRULE_AT = (10, 13, 18, 24, 29)
EARLY = 8
LAG = 3
NARROW = 10
KEYS_FROM = 9
LOOP_STEPS = 142
COL_Q, COL_K, COL_V, COL_Z, COL_AB, COL_FQ, COL_FK, COL_FV = 0, 512, 1024, 1536, 2048, 2064, 2576, 3088
PROJ = 3608
SLOTW = 528


def hybrid_decoder_step(nc, a, o):
    ctx = ExitStack()
    with ctx:
        sems = {}

        def S(name):
            if name not in sems:
                sems[name] = ctx.enter_context(nc.semaphore(name))
            return sems[name]

        def sb(name, shape, dt=F32):
            return ctx.enter_context(nc.sbuf_tensor(name, shape, dt))

        def dram(name, shape):
            return nc.dram_tensor(name, shape, F32, kind="Internal").ap()

        ident = sb("ident", [P, P])
        ones = sb("ones", [P, P])
        upper = sb("upper", [P, P])
        lower = sb("lower", [P, P])
        hide_q = sb("hide_q", [P, P])
        hide_e = sb("hide_e", [P, P])
        level = sb("level", [P, 7, P])
        small = sb("small", [P, 1024])
        RING = sb("RING", [P, 3, KT * SLOTW])
        HT = sb("HT", [P, KT, TOK])
        MV = sb("MV", [P, 4, D_MODEL])
        RQ64 = sb("RQ64", [P, 328])
        R1 = sb("R1", [P, 14336])
        R2 = sb("R2", [P, 14700])
        banks = [ctx.enter_context(nc.psum_tensor(f"bank{i}", [P, 512], F32)) for i in range(8)]

        def part(_t, _at, _n, /, **dims):
            v = _t[:, _at:_at + _n]
            if not dims:
                return v
            names = list(dims)
            return v.rearrange(f"row ({' '.join(names)}) -> row {' '.join(names)}", **{k: dims[k] for k in names[1:]})

        GT = part(R1, 0, 6144, t=TILES, c=CONV)
        GZ = part(R1, 6144, 2048, t=TILES, c=WID)
        VT = part(R1, 8192, 2048, t=TILES, c=WID)
        FQ = part(R1, 10240, 2048, j=4, t=SEQ)
        FK = part(R1, 12288, 2048, j=4, t=SEQ)

        C9 = R2[:, 0:1024]
        SC9 = R2[:, 1024:2048]
        KO = part(R2, 0, 1024, n=2, c=512)
        XR = part(R2, 2048, 2048, n=2, c=1024)
        HJ = part(R2, 4096, 2048, n=2, c=1024)
        PS = R2[:, 2048:2048 + PROJ]
        RAW = part(R2, 6144, 1032, n=2, c=516)
        CACC = part(R2, 7176, 1024, n=2, c=512)
        CACT = part(R2, 8200, 1024, n=2, c=512)
        ints = R2[:, 7176:7688].bitcast(I32).rearrange("p (n c) -> p n c", n=4)
        SCW = part(R2, 0, 2048, n=4, c=512)
        SST = part(R2, 6144, 1536, n=3, c=512)
        STMP = R2[:, 7680:8192]
        PSC = R2[:, 9224:9224 + CONV]
        TAILO = R2[:, 10760:10760 + CONV]
        HFLAT = HT[:, :, :].rearrange("p k t -> p (k t)")
        PT = part(HFLAT, 1024, 1024, n=2, c=512)
        FA = part(HFLAT, 2048, 1024, n=2, c=512)
        FB = part(HFLAT, 3072, 1024, n=2, c=512)
        SS0 = part(R2, 0, 4096, k=HD, v=HD)
        SSP = part(R2, 4096, 4096, k=HD, v=HD)
        PR = part(R2, 8192, 1024, n=2, c=512)
        SV = part(R2, 12288, 320, n=5, c=HD)
        QGT_, KB_, KBG_, KG_ = (R2[:, i * 512:(i + 1) * 512] for i in range(4))
        SQ = R2[:, 0:1024]
        SQ_FIRST = R2[:, 11264:12288]
        TQ, TK, TKB, TQG = (part(R2, 2048 + i * 512, 512, j=4, c=P) for i in range(4))
        BATCH = [[part(R2, 4096 + b * 3584 + i * 512, 512, m=4, c=P) for i in range(7)] for b in range(2)]
        WT = part(R1, 8192, 512, j=4, c=P)
        VN = part(R2, 11628, 512, h=8, d=HD)
        ST = part(R2, 12652 - 512, 512, j=4, d=P)
        EX = MV[:, 3, 0:512]
        KG4 = [part(R2, 12652, 2048, g=4, c=512), part(R2, 9216, 2048, g=4, c=512),
               MV[:, 0:2, :].rearrange("p n d -> p (n d)").rearrange("p (g c) -> p g c", g=4), part(R1, 12288, 2048, g=4, c=512)]

        def buffer_of(m):
            return m % 2 * 2 if m < NARROW else 3 if m >= 32 and m % 3 == 1 else m % 3

        def pages(m):
            return KG4[buffer_of(m)]

        def pages_ready(eng, m):
            nth = sum(1 for i in range(m + 1) if buffer_of(i) == buffer_of(m))
            eng.wait_ge(S(f"kv_in{buffer_of(m)}"), 64 * nth)

        def group_before(m):
            return next((i for i in range(m - 1, -1, -1) if buffer_of(i) == buffer_of(m)), None)

        SLOT2 = RING[:, 2, :]
        SC = part(SLOT2, 0, 1088, h=HEADS, b=NB, g=17)
        LG = SLOT2[:, 1088:2112]
        LP = part(SLOT2, 2112, 1024, h=HEADS, b=NB, g=PAGES)
        QB = part(SLOT2, 3136, 1024, n=2, c=512)
        VSUM = part(SLOT2, 1088, 3072, n=6, c=512)
        VNEW = HFLAT[0:1, 2048:3072]
        PVA = part(small, 896, 32, b=NB, j=4)
        X1 = part(R2, 0, 5120, t=5, d=D_MODEL)
        TMPX = part(R2, 5120, 1024, n=2, c=512)
        H2 = part(R2, 6144, 5120, t=5, d=D_MODEL)
        QT = part(R1, 0, 16 * TOK, b=16, t=TOK)
        KEYT = part(R1, 8320, 2048, b=16, n=P)
        G1 = [part(R1, 512, 1024), part(R1, 2048, 1024)[0:NB]]
        MVP2 = [part(R1, 3584, 1024), part(R1, 5120, 1024)]
        MVS2 = part(R1, 12288, 2048, n=2, d=D_MODEL)
        SCS = R1[:, 12288:14336]
        KN = part(SLOT2, 0, 2048, b=16, c=P)
        FLAT = RING[:, :, :].rearrange("p s n -> p (s n)")
        UR = part(FLAT, 0, 4096, n=4, d=D_MODEL)
        VR = part(FLAT, 4096, 8192, n=8, d=D_MODEL)
        ACC = part(HFLAT, 0, 4096, t=TILES, d=D_MODEL)
        SX = part(R1, 10368, 256, p=2, n=P)
        CAND = R1[:, 10624:10880]
        V16 = part(R1, 10880, 32, p=2, n=16)
        I16 = R1[:, 10912:10944].bitcast(U32).rearrange("q (p n) -> q p n", p=2)
        IF = part(R1, 10944, 32, p=2, n=16)
        FI = R1[:, 10976:10992].bitcast(U32)
        IJ = R1[:, 10992:11024].bitcast(U32).rearrange("q (p n) -> q p n", p=2)
        IJF = part(R1, 11024, 32, p=2, n=16)
        R01 = part(R1, 11056, 32, p=2, n=16)
        OH = part(R1, 11088, 512, p=2, k=16, n=16)
        FVT = R1[:, 11600:11616]
        EIX = R2[:, 11264:11328].bitcast(U32).rearrange("q (t n) -> q t n", t=4)
        FVS = part(R2, 11328, 64, t=4, n=16)
        DOT = part(R2, 11392, 64, t=4, n=16)
        AG = part(R2, 11456, 64, t=4, n=16)
        GAT = part(R2, 11520, 64, t=4, n=16)
        SUMG = R2[:, 11584:11588]
        NMX = R2[:, 11588:11592]
        DG = part(R2, 11628, 512, n=4, c=P)
        EISF = R2[:, 12652:12780]
        FVSS = R2[:, 12780:12908]
        IXT = R2[:, 12908:12916].bitcast(U32)
        GTT = R2[:, 12916:12924]
        DOTS = R2[:, 12924:12932]
        AM = R2[:, 12932:12996]
        H2B = part(R1, 12288, 2048, n=2, d=D_MODEL)
        IOTA16 = small[:, 847:863]
        IOTAI = small[:, 863:879].bitcast(I32)

        def BMR(nth):
            return (part(R2, 12652, 1024, n=2, c=512) if nth < 4 else part(MV[:, 2, :], 0, 1024, n=2, c=512))[0:9, nth % 2, :]

        def MR(nth):
            return (part(R2, 13676, 1024, n=2, c=512) if nth < 4 else part(HFLAT, 0, 1024, n=2, c=512))[0:9, nth % 2, :]

        CT = part(small, 0, 72, k=KT, n=9)
        CW = part(small, 72, 48, j=TAPS, b=12)
        BIAS = part(small, 120, 24, n=3, h=8)
        GATE = part(small, 144, 120, t=5, n=24)
        TAILI = part(small, 264, 36, b=12, n=3)
        BETA = part(small, 300, 40, t=5, h=8)
        G = part(small, 340, 40, t=5, h=8)
        LOGF = part(small, 380, 40, t=5, h=8)
        GW = part(small, 420, 120, t=5, n=24)
        SS = small[:, 540:560]
        FR = MV[:, 2, 0:512]
        NFR = MV[:, 2, 512:1024]
        RS = small[:, 562:594]
        NM = small[:, 594:626]
        RI = small[:, 626:658]
        GC = part(small, 658, 32, t=4, h=8)
        EG = part(small, 690, 32, t=4, h=8)
        GL = part(small, 722, 32, t=4, h=8)
        EKG = part(small, 754, 32, t=4, h=8)
        NBG = part(small, 786, 32, t=4, h=8)
        RQ = small[:, 818:834]
        RQO = small[:, 847:855]
        TDG = small[:, 896:960]
        SRCP = small[:, 960:1024]
        SMX = small[:, 846:847]
        PTI = small[:, 834:835].bitcast(U32)
        SSM = small[:, 836:846]
        LNB = RQ64[:, 0:64]
        M64 = RQ64[:, 64:128]
        SN = RQ64[:, 128:136]
        OGS = MV[0:NB, 3, 512:1024]
        NW = RQ64[:, 136:200]
        PTB = RQ64[0:1, 200:328].bitcast(I32)
        CWN = small[0:48, 896:1024]
        EPSB = small[:, 561:562]

        def SRAW(g):
            return PS[0:NB, g * 512:(g + 1) * 512]

        def SCONV(g):
            return PSC[0:NB, g * 512:(g + 1) * 512]

        def wide(v, n):
            return v.rearrange("p (m o) -> p m o", o=1).to_broadcast([v.shape[0], v.shape[1], n])

        def FOUR(m):
            return m[:, :].rearrange("p (o c) -> p o c", o=1).to_broadcast([P, 4, P])

        def fox_out(j):
            return (EX if j == 0 else FQ[:, j - 1, :]).rearrange("p (t c) -> p t c", t=TILES)

        samp_d = dram("samp_d", [NB, 6, 512])
        sgate_d = dram("sgate_d", [3, NB, 8])
        frow_d = dram("frow_d", [2, 8, SEQ])
        h2s_d = dram("h2s_d", [NB, D_MODEL])
        mod_d = dram("mod_d", [9, 6 * D_MODEL])

        pools = {"A": [0, 1, 2, 3], "D": [4, 5, 6, 7]}
        taken = {"A": 0, "D": 0}
        job_of = {}
        newest = [None]
        last_job = []

        def take_bank(job, pool):
            n = taken[pool]
            taken[pool] += 1
            b = pools[pool][n % 4]
            if n >= 4:
                nc.tensor.wait_ge(S(f"bank{b}_free"), n // 4)
            job_of[job] = (b, n // 4 + 1)
            newest[0] = job
            return banks[b]

        def full_bank(eng, job):
            b, use = job_of[job]
            eng.wait_ge(S(f"bank{b}_full"), use)
            return banks[b]

        def job_done(eng, job):
            b, use = job_of[job]
            eng.wait_ge(S(f"bank{b}_full"), use)

        def job_read(eng, job):
            b, use = job_of[job]
            eng.wait_ge(S(f"bank{b}_free"), use)

        def full(job):
            return S(f"bank{job_of[job][0]}_full")

        def free(job):
            return S(f"bank{job_of[job][0]}_free")

        w_mod = a["w_mod"][0].rearrange("(k p) n -> p k n", p=P)
        w_in = a["w_in"][0].rearrange("(k p) n -> p k n", p=P)
        w_out = a["w_out"][0].rearrange("(k p) n -> p k n", p=P)
        wq = a["peer_wq"][0].rearrange("(k p) n -> p k n", p=P)
        chunks = [(f"mod{j}", w_mod[:, :, j * 512:(j + 1) * 512]) for j in range(4)]
        chunks += [("fv", w_in[:, :, COL_FV:PROJ]), ("gz", w_in[:, :, COL_Z:COL_FQ]),
                   ("fq", w_in[:, :, COL_FQ:COL_FK]), ("fk", w_in[:, :, COL_FK:COL_FV]),
                   ("gq", w_in[:, :, 0:512]), ("gk", w_in[:, :, 512:1024]), ("gv", w_in[:, :, 1024:1536])]
        chunks += [(f"mod{j}", w_mod[:, :, j * 512:(j + 1) * 512]) for j in range(4, 12)]
        chunks += [(f"wo{j}", w_out[:, :, j * 512:(j + 1) * 512]) for j in range(2)]
        chunks += [(f"wq{j}", wq[:, :, j * 512:(j + 1) * 512]) for j in range(4)]
        slot_of = [n % 3 if n < 11 else (n - 9) % 2 for n in range(len(chunks))]
        before = [next((m for m in range(n - 1, -1, -1) if slot_of[m] == slot_of[n]), None) for n in range(len(chunks))]
        chunk_at = {name: n for n, (name, _) in enumerate(chunks)}

        def slot(name):
            n = chunk_at[name]
            w = chunks[n][1].shape[2]
            return RING[:, slot_of[n], 0:KT * w].rearrange("p (k n) -> p k n", k=KT)

        def ring_ready(eng, name):
            n = chunk_at[name]
            eng.wait_ge(S(f"ring{slot_of[n]}_loaded"), 16 * (slot_of[:n].count(slot_of[n]) + 1))
            return slot(name)

        def key_groups(u):
            done = lambda x: NARROW + (x - KEYS_FROM) * (32 - NARROW) // (34 - KEYS_FROM) if x >= KEYS_FROM else \
                min(NARROW, EARLY + max(0, x - 1) // 2)
            return range(done(u), done(u + 1))

        def value_groups(level_):
            done = lambda x: max(0, (x - 6) * 32 // 22)
            return range(done(level_), done(level_ + 1))

        block = ctx.enter_context(nc.Block())

        @block.tensor
        def _(pe):
            def mm(out, lhsT, rhs, start=True, stop=True, sem=None, **k):
                i = nc.tensor.matmul(out, lhsT, rhs, start=start, stop=stop, **k)
                if sem is not None:
                    i.then_inc(sem, 1)
                return i

            def tr(out, in_, sem=None):
                n = in_.shape[0]
                i = nc.tensor.transpose(out, in_, ident[0:n, 0:n])
                if sem is not None:
                    i.then_inc(sem, 1)

            def project(job, pool, lhs, rhs, cols=0):
                b = take_bank(job, pool)
                l0, r0 = lhs(0), rhs(0)
                m, n = l0.shape[1], r0.shape[1]
                for k in range(KT):
                    mm(b[0:m, cols:cols + n], lhs(k), rhs(k), k == 0, k == KT - 1, full(job) if k == KT - 1 else None)

            pe.wait_ge(S("ident_ready"), 1)
            pe.wait_ge(S("silu_c"), 1)
            b = take_bank("cT", "A")
            for k in range(KT):
                tr(b[:, k * 9:k * 9 + 9], SC9[0:9, k * P:(k + 1) * P], full("cT") if k == KT - 1 else None)
            b = take_bank("cwT", "A")
            pe.wait_ge(S("conv_w_in"), 16)
            tr(b[:, 0:48], CWN, full("cwT"))

            def mod_chunk(j):
                w = ring_ready(pe, f"mod{j}")
                project(("mod", j), "D", lambda k: CT[:, k, :], lambda k: w[:, k, :])
                last_job.append(newest[0])

            pe.wait_ge(S("cT_ready"), 1)
            for j in range(4):
                mod_chunk(j)
            for t in range(5):
                n = P if t < 4 else NB
                pe.wait_ge(S("h_ready"), t + 1)
                for half in range(2):
                    b = take_bank(("hT", t, half), "A")
                    for k in range(4):
                        kk = half * 4 + k
                        tr(b[:, k * n:(k + 1) * n], HJ[0:n, t % 2, kk * P:(kk + 1) * P], full(("hT", t, half)) if k == 3 else None)

            def tokens_out(name, cols, w):
                for t in range(5):
                    n = P if t < 4 else NB
                    pe.wait_ge(S("hT_ready"), 2 * t + 2)
                    project((name, t), "A", lambda k: HT[:, k, t * P:t * P + n], lambda k: w[:, k, cols])

            def narrow_out(name, w, cols, n_cols):
                b = take_bank(name, "D")
                for t in range(5):
                    n = P if t < 4 else NB
                    for k in range(KT):
                        last = t == 4 and k == KT - 1
                        mm(b[0:n, t * n_cols:(t + 1) * n_cols], HT[:, k, t * P:t * P + n], w[:, k, cols],
                           k == 0, k == KT - 1, full(name) if last else None)

            w = ring_ready(pe, "fv")
            tokens_out("fv", slice(0, 512), w)
            narrow_out("ff", w, slice(512, 520), 8)
            last_job.append(newest[0])
            w = ring_ready(pe, "gz")
            tokens_out("gz", slice(0, 512), w)
            narrow_out("gab", w, slice(512, 528), 16)
            last_job.append(newest[0])
            for name in ("fq", "fk"):
                w = ring_ready(pe, name)
                for j in range(4):
                    project((name, j), "A", lambda k: w[:, k, j * P:(j + 1) * P], lambda k: HT[:, k, 0:SEQ])
                project((name, 4), "A", lambda k: HT[:, k, SEQ:TOK], lambda k: w[:, k, :])
                last_job.append(newest[0])
            pe.wait_ge(S("fk_ready"), 4)
            for t in range(TILES):
                b = take_bank(("ktok", t), "D")
                for j in range(4):
                    tr(b[:, j * P:(j + 1) * P], FK[:, j, t * P:(t + 1) * P], full(("ktok", t)) if j == 3 else None)
            pe.wait_ge(S("gates_ready"), 1)
            b = take_bank("frow", "D")
            for i in range(TILES):
                for j in range(i + 1):
                    mm(b[0:8, i * P:(i + 1) * P], LOGF[:, j, :], upper[:, :] if j == i else ones[:, :], j == 0, j == i,
                       full("frow") if i == j == TILES - 1 else None)
            b = take_bank("gsum", "D")
            g32 = small[:, 340:372]
            mm(b[:, 0:32], upper[:, :], g32)
            mm(b[:, 32:64], ones[:, :], g32, sem=full("gsum"))

            def conv_back(cb):
                pe.wait_ge(S("conv_act"), cb + 1)
                b = take_bank(("cvT", cb), "D")
                for t in range(TILES):
                    tr(b[:, t * P:(t + 1) * P], CACT[:, cb % 2, t * P:(t + 1) * P], full(("cvT", cb)) if t == 3 else None)

            for g, name in enumerate(("gq", "gk", "gv")):
                w = ring_ready(pe, name)
                for j in range(4):
                    cb = g * 4 + j
                    project(("cv", cb), "A", lambda k: w[:, k, j * P:(j + 1) * P], lambda k: HT[:, k, 0:SEQ])
                    if cb >= 2:
                        conv_back(cb - 2)
                project((name, 4), "A", lambda k: HT[:, k, SEQ:TOK], lambda k: w[:, k, :])
                last_job.append(newest[0])
            conv_back(10)
            conv_back(11)
            pe.wait_ge(S("tails"), 12)
            for q in range(3):
                b = take_bank(("tail", q), "D")
                for j in range(4):
                    tr(b[0:3, j * P:(j + 1) * P], TAILI[:, q * 4 + j, :], full(("tail", q)) if j == 3 else None)
            def forget_turns():
                pe.wait_ge(S("logf_pages"), 16)
                for half in range(2):
                    b = take_bank(("lp", half), "D")
                    for m in range(4):
                        h = half * 4 + m
                        tr(b[:, m * P:(m + 1) * P], LG.rearrange("p (n h) -> p h n", h=HEADS)[:, h, :], full(("lp", half)) if m == 3 else None)

            forget_turns()

            def head_of(h):
                return slice((h % 2) * HD, (h % 2) * HD + HD), h // 2

            def fox_scores(u):
                h, i = divmod(u, 4)
                r, j = head_of(h)
                if i == 0:
                    pe.wait_ge(S(f"frow_in{h % 2}"), 32 * (h // 2 + 1))
                b = take_bank(("sc", u), "A")
                w = P * (i + 1)
                mm(b[:, 0:w], FQ[r, j, i * P:(i + 1) * P], FK[r, j, 0:w], True, False)
                mm(b[:, 0:w], FA[0:2, h % 2, i * P:(i + 1) * P], FB[0:2, h % 2, 0:w], False, False)
                mm(b[:, i * P:w], ident[:, :], hide_q[:, :], False, True, full(("sc", u)))

            def fox_turn(u):
                i = u % 4
                job_read(pe, ("sc", u))
                b = take_bank(("pT", u), "D")
                for k in range(i + 1):
                    tr(b[:, k * P:(k + 1) * P], PR[:, u % 2, k * P:(k + 1) * P], full(("pT", u)) if k == i else None)

            def fox_values(u):
                h, i = divmod(u, 4)
                job_read(pe, ("pT", u))
                b = take_bank(("fo", u), "D")
                for k in range(i + 1):
                    mm(b[:, 0:HD], PT[:, u % 2, k * P:(k + 1) * P], VT[:, k, h * HD:(h + 1) * HD], k == 0, k == i,
                       full(("fo", u)) if k == i else None)

            def forget_sums():
                job_read(pe, ("lp", 0))
                job_read(pe, ("lp", 1))
                for half in range(2):
                    rhs = SLOT2[:, 2112 + half * 512:2112 + half * 512 + 512]
                    b = take_bank(("lsum", half), "D")
                    mm(b[:, :], lower[:, :], rhs, sem=full(("lsum", half)))
                    b = take_bank(("ltot", half), "D")
                    mm(b[:, :], ones[:, :], rhs, sem=full(("ltot", half)))

            def sample_max_turn():
                pe.wait_ge(S("smax"), 1)
                b = take_bank("smT", "D")
                tr(b[0:64, 0:P], M64, full("smT"))

            def sample_max_spread():
                pe.wait_ge(S("smax"), 2)
                b = take_bank("smB", "D")
                mm(b[:, 0:64], ones[0:64, :], TDG[0:64, :], sem=full("smB"))

            def sample_sums():
                pe.wait_ge(S("ssums"), 1)
                b = take_bank("ssum", "D")
                mm(b[:, 0:64], ones[:, :], M64, sem=full("ssum"))

            def sample_values(n):
                bb, q = divmod(n, 4)
                pe.wait_ge(S("kred"), 32 + n + 1)
                if q == 3:
                    pe.wait_ge(S(f"vnew_in{bb % 2}"), 16 * (bb // 2 + 1))
                b = take_bank(("pv", n), "D")
                for j in range(4):
                    mm(b[:, j:j + 1], VSUM[:, n % 6, j * P:(j + 1) * P], ones[:, 0:1], sem=full(("pv", n)) if j == 3 and q < 3 else None)
                if q == 3:
                    for j in range(4):
                        mm(b[:, 4 + 2 * j:6 + 2 * j], VNEW[:, (bb % 2) * 512 + j * P:(bb % 2) * 512 + (j + 1) * P],
                           SC[0:1, 2 * j:2 * j + 2, bb, 16], sem=full(("pv", n)) if j == 3 else None)

            steps = {1: sample_max_turn, 2: sample_max_spread, 4: sample_sums}

            for u in range(34):
                if u < 32:
                    fox_scores(u)
                if 1 <= u < 33:
                    fox_turn(u - 1)
                if u >= 2:
                    fox_values(u - 2)
                if u in (6, 14, 22, 30):
                    mod_chunk(4 + (u - 6) // 8)
                if u == 1:
                    forget_sums()

            def pair_turns(i):
                pe.wait_ge(S("gdn_tokens"), i + 1)
                for name, src in (("q", GT[:, i, 0:512]), ("k", GT[:, i, 512:1024]), ("kb", KB_), ("qG", QGT_)):
                    b = take_bank(("t" + name, i), "A")
                    for j in range(4):
                        tr(b[:, j * P:(j + 1) * P], src[:, j * P:(j + 1) * P], full(("t" + name, i)) if j == 3 else None)

            def products(i, hb):
                heads = range(hb, HEADS, 2)
                b = take_bank(("dec", i, hb), "D")
                for m, h in enumerate(heads):
                    mm(b[:, m * P:(m + 1) * P], G[:, i, h:h + 1].to_broadcast([P, P]), upper[:, :],
                       sem=full(("dec", i, hb)) if m == 3 else None)
                job_read(pe, ("tk", i))
                job_read(pe, ("tkb", i))
                for name, rhs in (("kk", TKB), ("kq", TQ)):
                    b = take_bank((name, i, hb), "D")
                    for m, h in enumerate(heads):
                        r, j = head_of(h)
                        mm(b[:, m * P:(m + 1) * P], TK[r, j, :], rhs[r, j, :], sem=full((name, i, hb)) if m == 3 else None)

            def solve(i, hb, lv):
                _, AT, AQ, X, Y, M0, M1 = BATCH[hb]
                T = BATCH[hb][0]
                M = (M0, M1)[lv % 2]
                pe.wait_ge(S(f"level{hb}"), 7 * i + lv + 1)
                if lv == 1:
                    pe.wait_ge(S("eye"), 2 * i + hb + 1)
                elif lv:
                    job_read(pe, ("Y", i, hb, lv - 1))
                    job_read(pe, ("X", i, hb, lv - 1))
                b = take_bank(("T", i, hb, lv), "A")
                for m in range(4):
                    mm(b[:, m * P:(m + 1) * P], M[:, m, :], X[:, m, :] if lv else ident[:, :], sem=full(("T", i, hb, lv)) if m == 3 else None)

            def solve2(i, hb, lv):
                _, AT, AQ, X, Y, M0, M1 = BATCH[hb]
                T = BATCH[hb][0]
                job_read(pe, ("T", i, hb, lv))
                for name, l, r in (("X", Y, T), ("Y", T, Y)):
                    if lv == 6 and name == "X":
                        continue
                    b = take_bank((name, i, hb, lv), "D")
                    for m in range(4):
                        mm(b[:, m * P:(m + 1) * P], l[:, m, :], r[:, m, :], sem=full((name, i, hb, lv)) if m == 3 else None)

            def state(i):
                YH = lambda h: BATCH[h % 2][4][:, h // 2, :]
                AQH = lambda h: BATCH[h % 2][2][:, h // 2, :]
                job_read(pe, ("Y", i, 0, 6))
                job_read(pe, ("Y", i, 1, 6))
                b = take_bank(("wt", i), "A")
                for h in range(HEADS):
                    r, j = head_of(h)
                    mm(b[r, j * P:(j + 1) * P], KBG_[:, h * HD:(h + 1) * HD], YH(h), sem=full(("wt", i)) if h == 7 else None)
                job_read(pe, ("wt", i))
                pe.wait_ge(S("state"), 2 * i + 1)
                b = take_bank(("vn", i), "A")
                for h in range(HEADS):
                    if h % 2 == 0:
                        mm(b[:, h * HD:(h + 2) * HD], WT[:, h // 2, :], ST[:, h // 2, :], True, False)
                    mm(b[:, h * HD:(h + 1) * HD], YH(h), GT[:, i, 1024 + h * HD:1024 + (h + 1) * HD], False, h % 2 == 1,
                       full(("vn", i)) if h == 7 else None)
                job_read(pe, ("vn", i))
                b = take_bank(("o", i), "D")
                for h in range(HEADS):
                    if h % 2 == 0:
                        mm(b[:, h * HD:(h + 2) * HD], TQG[:, h // 2, :], ST[:, h // 2, :], True, False)
                    mm(b[:, h * HD:(h + 1) * HD], AQH(h), VN[:, h, :], False, h % 2 == 1, full(("o", i)) if h == 7 else None)
                b = take_bank(("dS", i), "D")
                for j in range(4):
                    mm(b[:, j * P:(j + 1) * P], KG_[:, j * P:(j + 1) * P], VN[:, 2 * j:2 * j + 2, :].rearrange("p h d -> p (h d)"),
                       sem=full(("dS", i)) if j == 3 else None)

            for i in range(TILES):
                pair_turns(i)
                products(i, 0)
                products(i, 1)
                for lv in range(7):
                    solve(i, 0, lv)
                    solve(i, 1, lv)
                    for n in value_groups(7 * i + lv - LAG):
                        sample_values(n)
                    if lv:
                        solve2(i, 0, lv)
                        solve2(i, 1, lv)
                    if 7 * i + lv in steps:
                        steps[7 * i + lv]()
                state(i)
                mod_chunk(8 + i)
            for n in range(value_groups(28 - LAG).start, 32):
                sample_values(n)

            for i in range(5):
                n = P if i < 4 else NB
                if i < 4:
                    pe.wait_ge(S("gdn_out"), i + 1)
                else:
                    pe.wait_ge(S("ogs_in"), 16)
                for half in range(2 if i < 4 else 1):
                    job = ("oT", i, half)
                    b = take_bank(job, "A")
                    for j in range(4):
                        src = fox_out(j)[:, i, :] if half else (GT[:, i, j * P:(j + 1) * P] if i < 4 else OGS[:, j * P:(j + 1) * P])
                        tr(b[:, j * n:(j + 1) * n], src, full(job) if j == 3 else None)
            job_read(pe, ("oT", 4, 0))
            job_read(pe, ("oT", 3, 0))
            job_read(pe, ("oT", 3, 1))
            job_read(pe, ("oT", 2, 1))
            pe.wait_ge(S("sample_attention"), 1)
            def second_turn(t):
                n = P if t < 4 else NB
                pe.wait_ge(S("h_ready"), 5 + t + 1)
                for half in range(2):
                    job = ("h2T", t, half)
                    b = take_bank(job, "A")
                    for k in range(4):
                        tr(b[:, k * n:(k + 1) * n], H2[0:n, t, (half * 4 + k) * P:(half * 4 + k + 1) * P], full(job) if k == 3 else None)

            for c in range(2):
                w = ring_ready(pe, f"wo{c}")
                for t in range(5):
                    n = P if t < 4 else NB
                    project(("wo", c, t), "D", lambda k: HT[:, k, t * P:t * P + n], lambda k: w[:, k, :])
                    if c == 1 and t >= 2:
                        second_turn(t - 2)
                last_job.append(("wo", c, 4))
                if c == 0:
                    pe.wait_ge(S("keys_in"), 16)
                    for q in range(4):
                        b = take_bank(("key", q), "A")
                        for j in range(4):
                            tr(b[:, j * P:(j + 1) * P], KN[:, q * 4 + j, :], full(("key", q)) if j == 3 else None)
            second_turn(3)
            second_turn(4)
            for t in range(5):
                job_read(pe, ("h2T", t, 0))
                job_read(pe, ("h2T", t, 1))
            for c in range(4):
                w = ring_ready(pe, f"wq{c}")
                for j in range(4):
                    project(("qT", c * 4 + j), "A", lambda k: w[:, k, j * P:(j + 1) * P], lambda k: HT[:, k, 0:SEQ])
                b = take_bank(("qTs", c), "A")
                for j in range(4):
                    for k in range(KT):
                        mm(b[:, j * NB:(j + 1) * NB], w[:, k, j * P:(j + 1) * P], HT[:, k, SEQ:TOK], k == 0, k == KT - 1,
                           full(("qTs", c)) if j == 3 and k == KT - 1 else None)
                last_job.append(newest[0])
            for t in range(5):
                n = P if t < 4 else NB
                for q in range(4):
                    if t == 0:
                        for j in range(4):
                            job_read(pe, ("qT", q * 4 + j))
                        job_read(pe, ("key", q))
                        job_read(pe, ("qTs", q))
                    b = take_bank(("score", t, q), "A")
                    for j in range(4):
                        mm(b[0:n, j * P:(j + 1) * P], QT[:, q * 4 + j, t * P:t * P + n], KEYT[:, q * 4 + j, :],
                           sem=full(("score", t, q)) if j == 3 else None)

            for t in range(5):
                for q in range(4):
                    job_read(pe, ("score", t, q))

            def peer_values(h, t):
                n_ = h * 4 + t
                lo, hi = banks[(t % 2) * 2], banks[(t % 2) * 2 + 1]
                pe.wait_ge(S("sums_free"), n_ + 1)
                for s_ in range(16):
                    pe.wait_ge(S(f"v_in{s_ % 8}"), n_ * 32 + 16 * (s_ // 8 + 1))
                    pe.wait_ge(S("diagonal"), n_ * 16 + s_ + 1)
                    mm(lo[:, :], DG[:, s_ % 4, :], VR[:, s_ % 8, 0:512], s_ == 0, s_ == 15)
                    mm(hi[:, :], DG[:, s_ % 4, :], VR[:, s_ % 8, 512:1024], s_ == 0, s_ == 15, S("v_used"))

            with pe.Fori(0, PH - 1) as h:
                for t in range(TILES):
                    peer_values(h, t)
            for t in range(TILES):
                if t == 3:
                    pe.wait_ge(S("sample_picks"), 1)
                    b = take_bank("ixT", "D")
                    tr(b[:, 0:8], EISF[0:NB, :])
                    pe.wait_ge(S("sample_picks"), 2)
                    tr(b[:, 8:16], FVSS[0:NB, :], full("ixT"))
                peer_values(PH - 1, t)
            pe.wait_ge(S("sums_free"), 34)
            pe.wait_ge(S("sample_gates"), 1)
            for t in range(NB):
                pe.wait_ge(S(f"v_in{t}"), 16 * (64 + 1))
                for half in range(2):
                    mm(banks[half][0:NB, :], AM[:, t * 8:t * 8 + 8], VR[:, t, half * 512:(half + 1) * 512], t == 0, t == NB - 1,
                       S("v_used") if half else None)

        @block.scalar
        def _(act):
            A = nc.scalar.activation
            act.wait_ge(S("c_in"), 32)
            A(SC9[0:9, :], C9[0:9, :], ACT.Silu).then_inc(S("silu_c"), 1)
            b = full_bank(act, "cT")
            A(small[:, 0:72], b[:, 0:72], ACT.Copy).then_inc(S("cT_ready"), 1)
            act.wait_ge(S("cT_ready"), 1)
            nc.scalar.sem_inc(free("cT"), 1)
            b = full_bank(act, "cwT")
            A(small[:, 72:120], b[:, 0:48], ACT.Copy).then_inc(free("cwT"), 1)
            for t in range(5):
                n = P if t < 4 else NB
                act.wait_ge(S("sumsq"), t + 1)
                A(SS[0:n, 5 + t:6 + t], SS[0:n, t:t + 1], ACT.Sqrt, scale=1.0 / D_MODEL, bias=EPSB[0:n, :]).then_inc(S("root"), 1)
                for half in range(2):
                    b = full_bank(act, ("hT", t, half))
                    A(HT[:, half * 4:half * 4 + 4, t * P:t * P + n], b[:, 0:4 * n].rearrange("p (k n) -> p k n", k=4),
                      ACT.Copy).then_inc(S("hT_ready"), 1)
                    act.wait_ge(S("hT_ready"), 2 * t + half + 1)
                    act.sem_inc(free(("hT", t, half)), 1)
            for t in range(4):
                b = full_bank(act, ("fv", t))
                A(VT[:, t, :], b[:, :], ACT.Copy).then_inc(free(("fv", t)), 1)
            b = full_bank(act, ("fv", 4))
            A(PS[0:NB, COL_FV:COL_FV + 512], b[0:NB, :], ACT.Copy).then_inc(free(("fv", 4)), 1)
            for t in range(4):
                b = full_bank(act, ("gz", t))
                A(GZ[:, t, :], b[:, :], ACT.Silu).then_inc(free(("gz", t)), 1)
            b = full_bank(act, ("gz", 4))
            A(PS[0:NB, COL_Z:COL_Z + 512], b[0:NB, :], ACT.Silu).then_inc(free(("gz", 4)), 1)
            act.wait_ge(S("gate_abs"), 1)
            for t0, n, tt in ((0, P, 4), (4, NB, 1)):
                v = GW[0:n, t0:t0 + tt, :]
                A(v, v, ACT.Exp, scale=-1.0).then_inc(S("gate_exp"), 1)
            act.wait_ge(S("gate_exp"), 2)
            for t0, n, tt in ((0, P, 4), (4, NB, 1)):
                v = GW[0:n, t0:t0 + tt, 0:16]
                A(v, v, ACT.Ln, bias=1.0).then_inc(S("gate_ln"), 1)
            A(BIAS[:, 2, :], BIAS[:, 2, :], ACT.Exp).then_inc(S("gate_ln"), 1)
            for name, dst, scale, col in (("fq", FQ, HD ** -0.5, COL_FQ), ("fk", FK, 1.0, COL_FK)):
                for j in range(4):
                    b = full_bank(act, (name, j))
                    A(dst[:, j, :], b[:, :], ACT.Copy, scale=scale).then_inc(S(name + "_ready"), 1)
                    act.wait_ge(S(name + "_ready"), j + 1)
                    act.sem_inc(free((name, j)), 1)
                b = full_bank(act, (name, 4))
                A(PS[0:NB, col:col + 512], b[0:NB, :], ACT.Copy, scale=scale).then_inc(free((name, 4)), 1)

            def conv_silu(cb):
                act.wait_ge(S("conv_sum"), cb + 1)
                if cb >= 2:
                    job_done(act, ("cvT", cb - 2))
                A(CACT[:, cb % 2, :], CACC[:, cb % 2, :], ACT.Silu).then_inc(S("conv_act"), 1)

            act.wait_ge(S("gsums"), 1)
            A(small[:, 690:722], small[:, 658:690], ACT.Exp).then_inc(S("decays"), 1)
            A(small[:, 754:786], small[:, 754:786], ACT.Exp).then_inc(S("decays"), 1)
            A(small[:, 722:754], small[:, 722:754], ACT.Exp).then_inc(S("decays"), 1)
            act.wait_ge(S("raw_zero"), 1)
            for g, name in enumerate(("gq", "gk", "gv")):
                for j in range(4):
                    cb = g * 4 + j
                    b = full_bank(act, ("cv", cb))
                    if cb >= 2:
                        act.wait_ge(S("tails"), cb - 1)
                    A(RAW[:, cb % 2, 3:515], b[:, :], ACT.Copy).then_inc(S("raw_ready"), 1)
                    act.wait_ge(S("raw_ready"), cb + 1)
                    act.sem_inc(free(("cv", cb)), 1)
                    if cb >= 1:
                        conv_silu(cb - 1)
                b = full_bank(act, (name, 4))
                A(PS[0:NB, g * 512:(g + 1) * 512], b[0:NB, :], ACT.Copy).then_inc(S("sample_raw"), 1)
                act.wait_ge(S("sample_raw"), g + 1)
                act.sem_inc(free((name, 4)), 1)
            conv_silu(11)
            act.sem_inc(S("sample_ready"), 1)
            job_done(act, ("cvT", 11))
            def squares(i):
                act.wait_ge(S("sq_free"), i + 1)
                A(SQ if i else SQ_FIRST, GT[:, i, 0:1024], ACT.Square).then_inc(S("gdn_sq"), 1)

            def roots(i):
                act.wait_ge(S("gdn_ss"), i + 1)
                A(RQ, RQ, ACT.Sqrt, bias=EPSB).then_inc(S("gdn_root"), 1)

            for u in range(32):
                w = P * (u % 4 + 1)
                b = full_bank(act, ("sc", u))
                act.wait_ge(S("fox_max"), u + 1)
                if u >= 2:
                    job_done(act, ("pT", u - 2))
                A(PR[:, u % 2, 0:w], b[:, 0:w], ACT.Exp, bias=NM[:, u:u + 1], accum_out=RS[:, u:u + 1]).then_inc(free(("sc", u)), 1)
                if u == 6:
                    act.wait_ge(S("sconv_done"), 3)
                    A(PSC[0:NB, :], PSC[0:NB, :], ACT.Silu).then_inc(S("sconv_silu"), 1)
                if u == 28:
                    squares(0)
                if u == 31:
                    roots(0)
                if u == SRULE_AT[0] + 2:
                    act.wait_ge(S("srule"), 1)
                    A(SSM[0:64, 4:6], SSM[0:64, 2:4], ACT.Sqrt, bias=EPSB[0:64, :]).then_inc(S("srule_act"), 1)
                    A(SSM[0:64, 6:7], SSM[0:64, 1:2], ACT.Exp).then_inc(S("srule_act"), 1)
            act.wait_ge(S("srule"), 5)
            A(SSM[0:64, 4:5], SSM[0:64, 2:3], ACT.Sqrt, scale=1.0 / HD, bias=EPSB[0:64, :]).then_inc(S("srule_act"), 1)

            def out_roots(i):
                act.wait_ge(S("o_ss"), i + 1)
                A(RQO, RQO, ACT.Sqrt, scale=1.0 / HD, bias=EPSB).then_inc(S("o_root"), 1)

            for i in range(TILES):
                for name, dst in (("q", TQ), ("k", TK), ("kb", TKB), ("qG", TQG)):
                    b = full_bank(act, ("t" + name, i))
                    A(dst, b[:, :].rearrange("p (j c) -> p j c", j=4), ACT.Copy).then_inc(free(("t" + name, i)), 1)
                for hb in range(2):
                    act.wait_ge(S("exponents"), 2 * i + hb + 1)
                    A(BATCH[hb][0], BATCH[hb][0], ACT.Exp).then_inc(S("decay_matrix"), 1)
                for lv in range(1, 7):
                    for hb in range(2):
                        b = full_bank(act, ("T", i, hb, lv))
                        if lv == 1:
                            act.wait_ge(S("decay_used"), 2 * i + hb + 1)
                        A(BATCH[hb][0], b[:, :].rearrange("p (m c) -> p m c", m=4), ACT.Copy).then_inc(free(("T", i, hb, lv)), 1)
                    if i == 0 and lv == 3:
                        act.wait_ge(S("sshift"), 1)
                        A(SLOT2[:, 0:1088], SLOT2[:, 0:1088], ACT.Exp).then_inc(S("sexp"), 1)
                    if lv == 1 and i:
                        out_roots(i - 1)
                    if lv == 2 and i + 1 < TILES:
                        squares(i + 1)
                    if lv == 4 and i + 1 < TILES:
                        roots(i + 1)
                b = full_bank(act, ("wt", i))
                A(WT, b[:, :].rearrange("p (j c) -> p j c", j=4), ACT.Copy).then_inc(free(("wt", i)), 1)
                b = full_bank(act, ("vn", i))
                A(VN, b[:, :].rearrange("p (h d) -> p h d", h=8), ACT.Copy).then_inc(free(("vn", i)), 1)
            out_roots(TILES - 1)
            for m in range(2):
                act.wait_ge(S(f"mod_out{m}"), 96)
            job_done(act, ("fo", 31))
            for i in range(5):
                n = P if i < 4 else NB
                for half in range(2 if i < 4 else 1):
                    b = full_bank(act, ("oT", i, half))
                    A(HT[:, half * 4:half * 4 + 4, i * P:i * P + n], b[:, 0:4 * n].rearrange("p (k n) -> p k n", k=4),
                      ACT.Copy).then_inc(free(("oT", i, half)), 1)
            for q in range(4):
                b = full_bank(act, ("key", q))
                A(KEYT[:, q * 4:q * 4 + 4, :], b[:, :].rearrange("p (b n) -> p b n", b=4), ACT.Copy).then_inc(free(("key", q)), 1)
            for t in range(5):
                n = P if t < 4 else NB
                act.wait_ge(S("sumsq"), 5 + t + 1)
                A(SS[0:n, 5 + t:6 + t], SS[0:n, t:t + 1], ACT.Sqrt, scale=1.0 / D_MODEL, bias=EPSB[0:n, :]).then_inc(S("root"), 1)
                for half in range(2):
                    b = full_bank(act, ("h2T", t, half))
                    job_done(act, ("wo", 1, t))
                    A(HT[:, half * 4:half * 4 + 4, t * P:t * P + n], b[:, 0:4 * n].rearrange("p (k n) -> p k n", k=4),
                      ACT.Copy).then_inc(free(("h2T", t, half)), 1)
            for c in range(4):
                for j in range(4):
                    b = full_bank(act, ("qT", c * 4 + j))
                    A(QT[:, c * 4 + j, 0:SEQ], b[:, :], ACT.Copy).then_inc(free(("qT", c * 4 + j)), 1)
                b = full_bank(act, ("qTs", c))
                A(QT[:, c * 4:c * 4 + 4, SEQ:TOK], b[:, 0:32].rearrange("p (b n) -> p b n", b=4), ACT.Copy).then_inc(free(("qTs", c)), 1)
            for t in range(5):
                n = P if t < 4 else NB
                for q in range(4):
                    b = full_bank(act, ("score", t, q))
                    dst = QT[:, q * 4:q * 4 + 4, t * P:(t + 1) * P] if t < 4 else SCS[0:NB, q * 512:(q + 1) * 512].rearrange("p (b n) -> p b n", b=4)
                    A(dst, b[0:n, :].rearrange("p (b n) -> p b n", b=4), ACT.Copy).then_inc(free(("score", t, q)), 1)

            def gates(n_, t):
                act.wait_ge(S("picked"), n_ + 1)
                A(GAT[:, t, :], FVS[:, t, :], ACT.Exp, bias=NMX[:, t:t + 1], accum_out=SUMG[:, t:t + 1]).then_inc(S("gate_raw"), 1)

            def gelu(n_, t):
                act.wait_ge(S("dots"), n_ * 16 + 16)
                A(AG[:, t, :], DOT[:, t, :], ACT.Gelu).then_inc(S("gelu"), 1)

            def peer_scalar(h, last):
                for t in range(TILES):
                    n_ = h * 4 + t
                    if last and t == 2:
                        act.wait_ge(S("sample_shift"), 1)
                        A(FVSS[0:NB, :], FVSS[0:NB, :], ACT.Exp).then_inc(S("sample_exp"), 1)
                    act.wait_ge(S("weights"), n_ + 1)
                    for s_ in range(16):
                        act.wait_ge(S("v_used"), n_ * 16 + s_ + 5)
                        A(DG[:, s_ % 4, :], ident[:, :], ACT.Copy, scale=AG[:, t, s_:s_ + 1]).then_inc(S("diagonal"), 1)
                        if s_ == 8 and not (last and t >= 2):
                            gates(n_ + 2, (t + 2) % 4)
                    if not (last and t == 3):
                        gelu(n_ + 1, (t + 1) % 4)

            gates(0, 0)
            gates(1, 1)
            gelu(0, 0)
            with act.Fori(0, PH - 1) as h:
                peer_scalar(h, False)
            peer_scalar(PH - 1, True)
            for t in range(5):
                n = P if t < 4 else NB
                if t == 2:
                    act.wait_ge(S("sample_dots"), NB)
                    A(DOTS, DOTS, ACT.Gelu).then_inc(S("sample_gelu"), 1)
                act.wait_ge(S("sumsq"), 10 + t + 1)
                A(SS[0:n, 5 + t:6 + t], SS[0:n, t:t + 1], ACT.Sqrt, scale=1.0 / D_MODEL, bias=EPSB[0:n, :]).then_inc(S("root"), 1)

        @block.vector
        def _(dve):
            V = nc.vector
            count = [0]

            def step(ins):
                count[0] += 1
                ins.then_inc(S("dve_steps"), 1)

            def settle():
                dve.wait_ge(S("dve_steps"), count[0])

            step(V.memset(ones[:, :], 1.0))
            step(V.memset(EPSB[:, :], EPS))
            V.memset(RAW[:, :, 0:3], 0.0).then_inc(S("raw_zero"), 1)
            dve.wait_ge(S("iota"), 2)
            E, C = ints[:, 0, :], ints[:, 1, :]
            V.tensor_tensor(ident[:, :], E, C, ALU.is_equal).then_inc(S("ident_ready"), 1)
            step(V.tensor_tensor(upper[:, :], E, C, ALU.is_le))
            step(V.tensor_tensor(lower[:, :], E, C, ALU.is_gt))
            settle()
            step(V.tensor_scalar(hide_e[:, :], lower[:, :], NEG, None, ALU.mult))
            step(V.tensor_tensor(hide_q[:, :], E, C, ALU.is_lt))
            settle()
            step(V.tensor_scalar(hide_q[:, :], hide_q[:, :], NEG, None, ALU.mult))
            for s in range(7):
                step(V.tensor_scalar(ints[:, 2, :], C, s, 1, ALU.logical_shift_right, ALU.bitwise_xor))
                step(V.tensor_scalar(ints[:, 3, :], E, s, 0, ALU.logical_shift_right, ALU.bitwise_or))
                settle()
                step(V.tensor_tensor(level[:, s, :], ints[:, 2, :], ints[:, 3, :], ALU.is_equal))
                settle()
                step(V.tensor_tensor(level[:, s, :], level[:, s, :], upper[:, :], ALU.mult))
                settle()

            def mod_row(j, nth):
                b = full_bank(dve, ("mod", j))
                dve.wait_ge(S(f"bmod{nth % 2}"), 16 * (nth // 2 + 1))
                if nth >= 2:
                    dve.wait_ge(S(f"mod_out{nth % 2}"), 16 * (nth // 2))
                plus = 1.0 if j in (2, 3, 8, 9) else 0.0
                V.scalar_tensor_tensor(MR(nth), b[0:9, :], plus, BMR(nth), ALU.add, ALU.add)\
                    .then_inc(S("mod_row"), 1)
                dve.wait_ge(S("mod_row"), nth + 1)
                dve.sem_inc(free(("mod", j)), 1)

            def norm_sum(x, out, ss):
                V.scalar_tensor_tensor(out, x, 1.0, x, ALU.mult, ALU.mult, accum_out=ss[0]).then_inc(S("sumsq"), 1)

            def norm_apply(nth, x, out, sh, sc, ss):
                dve.wait_ge(S("sumsq"), nth + 1)
                dve.wait_ge(S("root"), nth + 1)
                step(V.reciprocal(ss[1], ss[1]))
                settle()
                step(V.scalar_tensor_tensor(out, x, ss[1], sc, ALU.mult, ALU.mult))
                settle()
                V.tensor_tensor(out, out, sh, ALU.add).then_inc(S("h_ready"), 1)

            def squares_of(t, n):
                return SS[0:n, t:t + 1], SS[0:n, 5 + t:6 + t]

            def first_sum(t):
                n = P if t < 4 else NB
                dve.wait_ge(S(f"x_in{t % 2}"), 16 * (t // 2 + 1))
                if t >= 2:
                    full_bank(dve, ("hT", t - 2, 1))
                norm_sum(XR[0:n, t % 2, :], HJ[0:n, t % 2, :], squares_of(t, n))

            def first_apply(t):
                n, mv = (P, 0) if t < 4 else (NB, 2)
                if t == 0:
                    dve.wait_ge(S("mv_prompt"), 32)
                if t == 4:
                    dve.wait_ge(S("mv_sample"), 32)
                norm_apply(t, XR[0:n, t % 2, :], HJ[0:n, t % 2, :], MV[0:n, mv, :], MV[0:n, mv + 1, :], squares_of(t, n))

            first_sum(0)
            first_sum(1)
            for j in range(4):
                mod_row(j, j)
            for t in range(5):
                first_apply(t)
                if t in (1, 2, 3):
                    first_sum(t + 1)
            b = full_bank(dve, "ff")
            step(V.tensor_copy(GATE[:, 0:4, 16:24], b[:, 0:32].rearrange("p (t h) -> p t h", h=8)))
            V.tensor_copy(GATE[0:NB, 4, 16:24], b[0:NB, 32:40]).then_inc(free("ff"), 1)
            b = full_bank(dve, "gab")
            step(V.tensor_copy(GATE[:, 0:4, 0:16], b[:, 0:64].rearrange("p (t h) -> p t h", h=16)))
            V.tensor_copy(GATE[0:NB, 4, 0:16], b[0:NB, 64:80]).then_inc(free("gab"), 1)
            job_read(dve, "gab")
            dve.wait_ge(S("bias_in"), 48)
            settle()
            both = ((0, P, 4), (4, NB, 1))
            for t0, n, tt in both:
                step(V.tensor_tensor(GATE[0:n, t0:t0 + tt, 0:8], GATE[0:n, t0:t0 + tt, 0:8],
                                     BIAS[0:n, 0:1, :].to_broadcast([n, tt, 8]), ALU.add))
                step(V.tensor_tensor(GATE[0:n, t0:t0 + tt, 16:24], GATE[0:n, t0:t0 + tt, 16:24],
                                     BIAS[0:n, 1:2, :].to_broadcast([n, tt, 8]), ALU.add))
            settle()
            for t0, n, tt in both:
                for at, frm in ((0, 0), (8, 16)):
                    v = GATE[0:n, t0:t0 + tt, frm:frm + 8]
                    step(V.scalar_tensor_tensor(GW[0:n, t0:t0 + tt, at:at + 8], v, -1.0, v, ALU.mult, ALU.max))
                step(V.tensor_copy(GW[0:n, t0:t0 + tt, 16:24], GATE[0:n, t0:t0 + tt, 8:16]))
            settle()
            dve.sem_inc(S("gate_abs"), 1)
            dve.wait_ge(S("gate_ln"), 3)
            for t0, n, tt in both:
                step(V.tensor_scalar_add(BETA[0:n, t0:t0 + tt, :], GW[0:n, t0:t0 + tt, 16:24], 1.0))
                step(V.scalar_tensor_tensor(G[0:n, t0:t0 + tt, :], GATE[0:n, t0:t0 + tt, 0:8], 0.0,
                                            GW[0:n, t0:t0 + tt, 0:8], ALU.max, ALU.add))
                step(V.scalar_tensor_tensor(LOGF[0:n, t0:t0 + tt, :], GATE[0:n, t0:t0 + tt, 16:24], 0.0,
                                            GW[0:n, t0:t0 + tt, 8:16], ALU.min, ALU.subtract))
            settle()
            for t0, n, tt in both:
                step(V.reciprocal(BETA[0:n, t0:t0 + tt, :], BETA[0:n, t0:t0 + tt, :]))
                step(V.scalar_tensor_tensor(G[0:n, t0:t0 + tt, :], G[0:n, t0:t0 + tt, :], -1.0,
                                            BIAS[0:n, 2:3, :].to_broadcast([n, tt, 8]), ALU.mult, ALU.mult))
            settle()
            dve.sem_inc(S("gates_ready"), 1)
            for t in range(TILES):
                b = full_bank(dve, ("ktok", t))
                if t >= 2:
                    dve.wait_ge(S(f"k_out{t % 2}"), 16 * (t // 2))
                V.tensor_copy(KO[:, t % 2, :], b[:, :]).then_inc(S("ktok_copied"), 1)
                dve.wait_ge(S("ktok_copied"), t + 1)
                dve.sem_inc(free(("ktok", t)), 1)

            b = full_bank(dve, "frow")
            step(V.tensor_copy(FR[0:8, :], b[0:8, :]))
            V.tensor_scalar(NFR[0:8, :], b[0:8, :], -1.0, None, ALU.mult).then_inc(free("frow"), 1)
            b = full_bank(dve, "gsum")
            step(V.tensor_copy(small[:, 658:690], b[:, 0:32]))
            V.tensor_copy(small[:, 722:754], b[:, 32:64]).then_inc(free("gsum"), 1)
            job_read(dve, "gsum")
            job_read(dve, "frow")
            settle()
            dve.sem_inc(S("frows"), 1)
            step(V.tensor_tensor(small[:, 754:786], small[:, 722:754], small[:, 658:690], ALU.subtract))
            settle()
            dve.sem_inc(S("gsums"), 1)
            dve.wait_ge(S("decays"), 3)
            step(V.scalar_tensor_tensor(small[:, 786:818], small[:, 300:332], -1.0, small[:, 690:722], ALU.mult, ALU.mult))

            flat = lambda v: v.rearrange("p h b g -> p (h b) g")
            TP = LG.rearrange("p (h b g) -> p h b g", h=HEADS, b=NB)

            def key_group(n):
                dve.wait_ge(S("kprod"), n + 1)
                V.tensor_reduce(SC[:, :, n // 4, (n % 4) * 4:(n % 4) * 4 + 4].rearrange("p h g -> p g h"),
                                pages(n).rearrange("p g (h d) -> p g h d", d=HD), AXX, ALU.add).then_inc(S("kred"), 1)

            def conv_block(cb):
                dve.wait_ge(S("raw_ready"), cb + 1)
                r, acc = RAW[:, cb % 2, :], CACC[:, cb % 2, :]
                if cb >= 2:
                    dve.wait_ge(S("conv_act"), cb - 1)
                V.tensor_copy(TAILI[:, cb, :], r[:, 512:515]).then_inc(S("tails_early"), 1)
                step(V.tensor_scalar(acc, r[:, 0:512], CW[:, 0, cb:cb + 1], None, ALU.mult))
                for j in range(1, 3):
                    settle()
                    step(V.scalar_tensor_tensor(acc, r[:, j:j + 512], CW[:, j, cb:cb + 1], acc, ALU.mult, ALU.add))
                settle()
                V.scalar_tensor_tensor(acc, r[:, 3:515], CW[:, 3, cb:cb + 1], acc, ALU.mult, ALU.add)\
                    .then_inc(S("conv_sum"), 1)
                dve.wait_ge(S("conv_sum"), cb + 1)
                dve.wait_ge(S("tails_early"), cb + 1)
                dve.sem_inc(S("tails"), 1)

            def conv_tokens(cb):
                b = full_bank(dve, ("cvT", cb))
                V.tensor_copy(GT[:, :, cb * P:(cb + 1) * P], b[:, :].rearrange("p (t c) -> p t c", t=TILES))\
                    .then_inc(free(("cvT", cb)), 1)

            dve.wait_ge(S("raw_zero"), 1)
            for cb in range(12):
                conv_block(cb)
                if cb >= 2:
                    conv_tokens(cb - 2)
                if cb == 11 - EARLY:
                    job_done(dve, last_job[8])
                    V.memset(SC[:, :, :, 16], NEG).then_inc(S("scores_cleared"), 1)
                if cb > 11 - EARLY:
                    key_group(cb - 12 + EARLY)
            conv_tokens(10)
            conv_tokens(11)
            for q in range(3):
                b = full_bank(dve, ("tail", q))
                V.tensor_copy(TAILO[0:3, q * 512:(q + 1) * 512], b[0:3, :]).then_inc(S("tail_out"), 1)
                dve.wait_ge(S("tail_out"), q + 1)
                dve.sem_inc(free(("tail", q)), 1)
            dve.wait_ge(S("sample_ready"), 1)
            T8 = MV[0:NB, 3, 0:512]
            step(V.tensor_tensor(T8, PS[0:NB, COL_FQ:COL_FQ + 512], PS[0:NB, COL_FK:COL_FK + 512], ALU.mult))
            settle()
            V.tensor_reduce(SN[0:NB, :], T8.rearrange("p (h d) -> p h d", h=8), AXX, ALU.add).then_inc(S("new_score"), 1)
            def fox_max(u):
                w = P * (u % 4 + 1)
                job_done(dve, ("sc", u))
                V.tensor_reduce(NM[:, u:u + 1], banks[job_of[("sc", u)][0]][:, 0:w], AXX, ALU.max, negate=True)\
                    .then_inc(S("fox_max"), 1)

            def fox_turned(u):
                w = P * (u % 4 + 1)
                b = full_bank(dve, ("pT", u))
                if u >= 2:
                    job_done(dve, ("fo", u - 2))
                V.tensor_copy(PT[:, u % 2, 0:w], b[:, 0:w]).then_inc(free(("pT", u)), 1)

            def fox_norm(u):
                h, i = divmod(u, 4)
                job_read(dve, ("sc", u))
                step(V.reciprocal(RI[:, u:u + 1], RS[:, u:u + 1]))
                b = full_bank(dve, ("fo", u))
                settle()
                V.tensor_scalar(fox_out(h // 2)[:, i, (h % 2) * HD:(h % 2) * HD + HD], b[:, 0:HD], RI[:, u:u + 1], None,
                                ALU.mult).then_inc(free(("fo", u)), 1)

            SR = slice(0, 64)

            def srule_norms():
                dve.wait_ge(S("srule_in"), 128)
                t = SSP[SR].rearrange("p k v -> p (k v)")[:, 0:128].rearrange("p (n d) -> p n d", n=2)
                step(V.tensor_tensor(t, SV[SR, 0:2, :], SV[SR, 0:2, :], ALU.mult))
                settle()
                V.tensor_reduce(SSM[SR, 2:4], t, AXX, ALU.add).then_inc(S("srule"), 1)

            def srule_scale():
                dve.wait_ge(S("srule_act"), 2)
                step(V.reciprocal(SSM[SR, 4:6], SSM[SR, 4:6]))
                step(V.scalar_tensor_tensor(SSM[SR, 7:8], SSM[SR, 0:1], -1.0, SSM[SR, 6:7], ALU.mult, ALU.mult))
                step(V.tensor_scalar(SV[SR, 2, :], SV[SR, 2, :], SSM[SR, 0:1], None, ALU.mult))
                settle()
                step(V.tensor_scalar(SV[SR, 0, :], SV[SR, 0, :], SSM[SR, 4:5], HD ** -0.5, ALU.mult, ALU.mult))
                step(V.tensor_scalar(SV[SR, 1, :], SV[SR, 1, :], SSM[SR, 5:6], None, ALU.mult))
                settle()
                dve.sem_inc(S("srule"), 1)

            def srule_new():
                dve.wait_ge(S("srule_pool"), 1)
                step(V.tensor_reduce(SV[SR, 4, :], SSP[SR].rearrange("p k v -> p v k"), AXX, ALU.add))
                settle()
                V.scalar_tensor_tensor(SV[SR, 2, :], SV[SR, 4, :], SSM[SR, 7:8], SV[SR, 2, :], ALU.mult, ALU.add)\
                    .then_inc(S("srule"), 1)

            def srule_state():
                dve.wait_ge(S("srule_pool"), 2)
                V.scalar_tensor_tensor(SS0[SR], SS0[SR], SSM[SR, 6:7], SSP[SR], ALU.mult, ALU.add).then_inc(S("srule"), 1)

            def srule_out():
                dve.wait_ge(S("srule_pool"), 3)
                o_ = SV[SR, 4, :]
                t = SSP[SR, 0, :]
                step(V.tensor_reduce(o_, SSP[SR].rearrange("p k v -> p v k"), AXX, ALU.add))
                settle()
                step(V.tensor_tensor(t, o_, o_, ALU.mult))
                settle()
                V.tensor_reduce(SSM[SR, 2:3], t, AXX, ALU.add).then_inc(S("srule"), 1)

            def srule_gate():
                dve.wait_ge(S("srule_act"), 3)
                o_ = SV[SR, 4, :]
                step(V.reciprocal(SSM[SR, 4:5], SSM[SR, 4:5]))
                settle()
                step(V.scalar_tensor_tensor(o_, o_, SSM[SR, 4:5], NW[SR, :], ALU.mult, ALU.mult))
                settle()
                V.tensor_tensor(o_, o_, SV[SR, 3, :], ALU.mult).then_inc(S("srule"), 1)

            def forget_turned():
                for half in range(2):
                    b = full_bank(dve, ("lp", half))
                    V.tensor_copy(SLOT2[:, 2112 + half * 512:2624 + half * 512], b[:, :]).then_inc(free(("lp", half)), 1)

            def forget_after():
                for half in range(2):
                    b = full_bank(dve, ("lsum", half))
                    at = slice(2112 + half * 512, 2624 + half * 512)
                    job_done(dve, ("ltot", half))
                    V.tensor_copy(SLOT2[:, at], b[:, :]).then_inc(free(("lsum", half)), 1)
                    b = full_bank(dve, ("ltot", half))
                    V.tensor_copy(LG[:, half * 512:(half + 1) * 512], b[:, :]).then_inc(free(("ltot", half)), 1)
                for half in range(2):
                    job_read(dve, ("lsum", half))
                    job_read(dve, ("ltot", half))
                for g in range(14, -1, -1):
                    step(V.tensor_tensor(TP[:, :, :, g], TP[:, :, :, g], TP[:, :, :, g + 1], ALU.add))
                    settle()
                step(V.tensor_tensor(flat(LP[:, :, :, 0:15]), flat(LP[:, :, :, 0:15]), flat(TP[:, :, :, 1:16]), ALU.add))

            def sample_scores():
                dve.wait_ge(S("kred"), 32)
                dve.wait_ge(S("new_in"), 32)
                settle()
                step(V.tensor_tensor(flat(SC[:, :, :, 0:16]), flat(SC[:, :, :, 0:16]), flat(LP), ALU.add))
                settle()
                step(V.tensor_tensor(SC[:, :, :, 0:16], SC[:, :, :, 0:16],
                                     LNB.rearrange("p (b h o) -> p h b o", h=8, o=1).to_broadcast([P, 8, 8, 16]), ALU.add))
                settle()
                V.tensor_reduce(M64, flat(SC), AXX, ALU.max).then_inc(S("smax"), 1)

            def sample_max():
                b = full_bank(dve, "smT")
                V.tensor_reduce(SMX[0:64, :], b[0:64, 0:P], AXX, ALU.max).then_inc(free("smT"), 1)
                job_read(dve, "smT")
                V.tensor_scalar(TDG[0:64, :], ident[0:64, 0:64], SMX[0:64, :], None, ALU.mult).then_inc(S("smax"), 1)

            def sample_shift():
                b = full_bank(dve, "smB")
                V.tensor_tensor(flat(SC), flat(SC), wide(b[:, 0:64], 17), ALU.subtract).then_inc(free("smB"), 1)
                job_read(dve, "smB")
                dve.sem_inc(S("sshift"), 1)

            def sample_exp_sums():
                dve.wait_ge(S("sexp"), 1)
                V.tensor_reduce(M64, flat(SC), AXX, ALU.add).then_inc(S("ssums"), 1)

            def sample_probs():
                b = full_bank(dve, "ssum")
                V.reciprocal(SRCP, b[:, 0:64]).then_inc(free("ssum"), 1)
                job_read(dve, "ssum")
                V.tensor_tensor(flat(SC), flat(SC), wide(SRCP, 17), ALU.mult).then_inc(S("probs"), 1)

            def value_sum(n):
                dve.wait_ge(S("kprod"), 32 + n + 1)
                if n >= 6:
                    job_done(dve, ("pv", n - 6))
                V.tensor_reduce(VSUM[:, n % 6, :], pages(32 + n).rearrange("p g c -> p c g"), AXX, ALU.add).then_inc(S("kred"), 1)

            def sample_values(n):
                bb, q = divmod(n, 4)
                b = full_bank(dve, ("pv", n))
                if n:
                    job_read(dve, ("pv", n - 1))
                if q == 0:
                    V.tensor_copy(PVA[:, bb, :], b[:, 0:4]).then_inc(free(("pv", n)), 1)
                elif q < 3:
                    V.tensor_tensor(PVA[:, bb, :], PVA[:, bb, :], b[:, 0:4], ALU.add).then_inc(free(("pv", n)), 1)
                else:
                    step(V.tensor_tensor(PVA[:, bb, :], PVA[:, bb, :], b[:, 0:4], ALU.add))
                    settle()
                    step(V.tensor_tensor(PVA[0:64, bb, :], PVA[0:64, bb, :], b[0:64, 4:12:2], ALU.add))
                    V.tensor_tensor(PVA[64:128, bb, :], PVA[64:128, bb, :], b[64:128, 5:12:2], ALU.add).then_inc(free(("pv", n)), 1)

            steps = {0: sample_scores, 1: sample_max, 2: sample_shift, 3: sample_exp_sums, 4: sample_probs}
            three = lambda v: v.rearrange("p (h d) -> p h d", h=8)

            def token_heads(i):
                return [three(GT[:, i, n * 512:(n + 1) * 512]) for n in range(3)]

            def norm_sums(i):
                v8 = token_heads(i)[2]
                dve.wait_ge(S("gdn_sq"), i + 1)
                V.tensor_reduce(RQ, (SQ if i else SQ_FIRST).rearrange("p (n d) -> p n d", d=HD), AXX, ALU.add).then_inc(S("gdn_ss"), 1)
                step(V.tensor_tensor(v8, v8, wide(BETA[:, i, :], HD), ALU.mult))

            def norm_scale(i):
                q8, k8, _ = token_heads(i)
                dve.wait_ge(S("gdn_root"), i + 1)
                step(V.reciprocal(RQ, RQ))
                settle()
                step(V.tensor_scalar(RQ[:, 0:8], RQ[:, 0:8], HD ** -0.5, None, ALU.mult))
                step(V.tensor_tensor(k8, k8, wide(RQ[:, 8:16], HD), ALU.mult))
                settle()
                step(V.tensor_tensor(q8, q8, wide(RQ[:, 0:8], HD), ALU.mult))
                settle()

            def first_squares():
                dve.wait_ge(S("psbuf_free"), 1)
                dve.sem_inc(S("sq_free"), 1)

            between = {1: forget_after, 26: first_squares, 30: lambda: norm_sums(0), 31: srule_gate, 33: lambda: norm_scale(0)}
            between.update(zip(SRULE_AT, (srule_norms, srule_scale, srule_new, srule_state, srule_out)))
            forget_turned()
            for u in range(34):
                if u < 32:
                    fox_max(u)
                if 1 <= u < 33:
                    fox_turned(u - 1)
                if u >= 2:
                    fox_norm(u - 2)
                if u in (6, 14, 22, 30):
                    mod_row(4 + (u - 6) // 8, 4 + (u - 6) // 8)
                if u in between:
                    between[u]()
                for n in key_groups(u):
                    key_group(n)
            dve.wait_ge(S("srule"), 6)
            dve.wait_ge(S("srule_stored"), 32)
            step(V.memset(ST, 0.0))
            settle()
            dve.sem_inc(S("state"), 1)
            def out_sums(i):
                O8, t8 = token_heads(i)[0], three(SQ[:, 0:512])
                job_read(dve, ("o", i))
                if i + 1 < TILES:
                    job_done(dve, ("tqG", i + 1))
                step(V.tensor_tensor(t8, O8, O8, ALU.mult))
                step(V.tensor_tensor(three(GZ[:, i, :]), three(GZ[:, i, :]), NW.rearrange("p (o d) -> p o d", o=1).to_broadcast([P, 8, HD]), ALU.mult))
                settle()
                V.tensor_reduce(RQO, t8, AXX, ALU.add).then_inc(S("o_ss"), 1)
                step(V.tensor_tensor(O8, O8, three(GZ[:, i, :]), ALU.mult))

            def out_scale(i):
                O8 = token_heads(i)[0]
                dve.wait_ge(S("o_root"), i + 1)
                step(V.reciprocal(RQO, RQO))
                settle()
                step(V.tensor_tensor(O8, O8, wide(RQO, HD), ALU.mult))
                settle()
                dve.sem_inc(S("gdn_out"), 1)

            for i in range(TILES):
                q8, k8, v8 = token_heads(i)
                step(V.tensor_tensor(three(KB_), k8, wide(BETA[:, i, :], HD), ALU.mult))
                step(V.tensor_tensor(three(KBG_), k8, wide(NBG[:, i, :], HD), ALU.mult))
                step(V.tensor_tensor(three(KG_), k8, wide(EKG[:, i, :], HD), ALU.mult))
                settle()
                V.tensor_tensor(three(QGT_), q8, wide(EG[:, i, :], HD), ALU.mult).then_inc(S("gdn_tokens"), 1)
                if i:
                    mod_row(7 + i, 7 + i)
                for hb in range(2):
                    D, AT, AQ, X, Y, M0, M1 = BATCH[hb]
                    b = full_bank(dve, ("dec", i, hb))
                    V.tensor_tensor(D, b[:, :].rearrange("p (m c) -> p m c", m=4), wide(GC[:, i, hb:8:2], P),
                                    ALU.subtract).then_inc(free(("dec", i, hb)), 1)
                    job_read(dve, ("dec", i, hb))
                    V.tensor_tensor(D, D, FOUR(hide_e), ALU.min).then_inc(S("exponents"), 1)
                    dve.wait_ge(S("decay_matrix"), 2 * i + hb + 1)
                    for name, dst in (("kk", AT), ("kq", AQ)):
                        b = full_bank(dve, (name, i, hb))
                        V.tensor_tensor(dst, b[:, :].rearrange("p (m c) -> p m c", m=4), D, ALU.mult)\
                            .then_inc(free((name, i, hb)), 1)
                    job_read(dve, ("kq", i, hb))
                    job_read(dve, ("kk", i, hb))
                    dve.sem_inc(S("decay_used"), 1)
                for lv in range(7):
                    for n in value_groups(7 * i + lv - LAG):
                        sample_values(n)
                    for hb in range(2):
                        D, AT, AQ, X, Y, M0, M1 = BATCH[hb]
                        if lv == 0:
                            b = full_bank(dve, ("T", i, hb, 0))
                            V.tensor_tensor(X, FOUR(ident), b[:, :].rearrange("p (m c) -> p m c", m=4), ALU.subtract)\
                                .then_inc(free(("T", i, hb, 0)), 1)
                            dve.wait_ge(S(f"level{hb}"), 7 * i + 1)
                            step(V.tensor_tensor(Y, FOUR(ident), M0, ALU.subtract))
                            settle()
                            job_read(dve, ("T", i, hb, 0))
                            dve.sem_inc(S("eye"), 1)
                        for name, dst in (("X", X), ("Y", Y)):
                            if lv == 0 or lv == 6 and name == "X":
                                continue
                            b = full_bank(dve, (name, i, hb, lv))
                            V.tensor_tensor(dst, dst, b[:, :].rearrange("p (m c) -> p m c", m=4), ALU.subtract)\
                                .then_inc(free((name, i, hb, lv)), 1)
                    if 7 * i + lv in steps:
                        steps[7 * i + lv]()
                    if lv == 0 and i:
                        out_sums(i - 1)
                    if lv == 1:
                        if i:
                            out_scale(i - 1)
                        if i + 1 < TILES:
                            job_done(dve, ("tqG", i))
                            dve.sem_inc(S("sq_free"), 1)
                    if lv == 3 and i + 1 < TILES:
                        norm_sums(i + 1)
                    if lv == 5 and i + 1 < TILES:
                        norm_scale(i + 1)
                    for n in value_groups(7 * i + lv):
                        value_sum(n)
                dve.wait_ge(S("decays"), 3)
                b = full_bank(dve, ("o", i))
                V.tensor_copy(q8, b[:, :].rearrange("p (h d) -> p h d", h=8)).then_inc(free(("o", i)), 1)
                b = full_bank(dve, ("dS", i))
                for a_ in range(2):
                    r_ = slice(a_ * HD, a_ * HD + HD)
                    own = ST[r_, :, r_]
                    step(V.tensor_tensor(own, own, wide(GL[:, i, :].rearrange("p (j a) -> p a j", a=2)[r_, a_, :], HD), ALU.mult))
                settle()
                for a_ in range(2):
                    r_ = slice(a_ * HD, a_ * HD + HD)
                    ins = V.tensor_tensor(ST[r_, :, r_], ST[r_, :, r_], b[:, :].rearrange("p (j c) -> p j c", j=4)[r_, :, r_], ALU.add)
                    ins.then_inc(free(("dS", i)), 1) if a_ else step(ins)
                settle()
                job_read(dve, ("dS", i))
                dve.sem_inc(S("state"), 2)
            mod_row(11, 11)
            for n in range(value_groups(28 - LAG).start, 32):
                sample_values(n)
            out_sums(TILES - 1)
            out_scale(TILES - 1)
            settle()
            job_read(dve, ("pv", 31))
            V.tensor_copy(HT[:, 4:8, SEQ:TOK], PVA.rearrange("p b j -> p j b")).then_inc(S("sample_attention"), 1)
            def second_apply(t):
                n = P if t < 4 else NB
                if t == 0:
                    dve.wait_ge(S("mv2_in"), 64)
                norm_apply(5 + t, X1[0:n, t, :], H2[0:n, t, :], (MVP2[0] if t < 4 else MVS2[:, 0, :])[0:n],
                           (MVP2[1] if t < 4 else MVS2[:, 1, :])[0:n], squares_of(t, n))

            dve.wait_ge(S("x1_in"), 32)
            dve.wait_ge(S("g1_in"), 32)
            nth = 0
            for c in range(2):
                for t in range(5):
                    n = P if t < 4 else NB
                    cs = slice(c * 512, (c + 1) * 512)
                    b = full_bank(dve, ("wo", c, t))
                    tmp = TMPX[0:n, nth % 2, :]
                    V.tensor_tensor(tmp, b[0:n, :], (G1[0] if t < 4 else G1[1])[0:n, cs], ALU.mult).then_inc(free(("wo", c, t)), 1)
                    job_read(dve, ("wo", c, t))
                    if nth >= 2:
                        dve.wait_ge(S("x1_part"), nth - 1)
                    V.tensor_tensor(X1[0:n, t, cs], X1[0:n, t, cs], tmp, ALU.add).then_inc(S("x1_part"), 1)
                    nth += 1
                    if c == 1:
                        dve.wait_ge(S("x1_part"), nth)
                        norm_sum(X1[0:n, t, :], H2[0:n, t, :], squares_of(t, n))
                        if t:
                            second_apply(t - 1)
            second_apply(4)
            dve.wait_ge(S("h_ready"), 10)
            dve.wait_ge(S("iota"), 3)
            step(V.tensor_copy(IOTA16, IOTAI))
            job_done(dve, ("qTs", 3))
            step(V.memset(ACC, 0.0))
            settle()
            base = count[0]
            clock = [lambda: count[0]]

            def calm(plain=False):
                dve.wait_ge(S("dve_steps"), clock[0]())
                if plain:
                    dve.sem_inc(S("dve_pace"), 1)

            def top16(rows, n_parts, val, vals16, idx16):
                for rnd in range(2):
                    for p_ in range(n_parts):
                        step(V.max(vals16(p_)[rows, rnd * 8:rnd * 8 + 8], val(p_)[rows]))
                    calm(True)
                    for p_ in range(n_parts):
                        step(V.max_index(idx16(p_)[rows, rnd * 8:rnd * 8 + 8], vals16(p_)[rows, rnd * 8:rnd * 8 + 8], val(p_)[rows]))
                    if rnd == 0:
                        calm(True)
                        for p_ in range(n_parts):
                            step(V.match_replace(val(p_)[rows], vals16(p_)[rows, 0:8], val(p_)[rows], NEG))
                        calm(True)

            def pick_sums(n, src):
                rows = slice(0, n)
                step(V.tensor_copy(SX[rows], src))
                calm(True)
                top16(rows, 2, lambda p_: SX[:, p_, :], lambda p_: V16[:, p_, :], lambda p_: I16[:, p_, :])
                calm()
                step(V.tensor_copy(IF[rows], I16[rows]))
                step(V.tensor_tensor(CAND[rows].rearrange("p (i j) -> p i j", i=16), wide(V16[rows, 0, :], 16),
                                     V16[rows, 1:2, :].to_broadcast([n, 16, 16]), ALU.add))

            def pick_experts(n, fv, eix):
                rows = slice(0, n)
                calm(True)
                top16(rows, 1, lambda p_: CAND, lambda p_: fv, lambda p_: FI)
                calm()
                step(V.tensor_scalar(IJ[rows, 0, :], FI[rows], 4, 0, ALU.logical_shift_right, ALU.bitwise_or))
                step(V.tensor_scalar(IJ[rows, 1, :], FI[rows], 15, 0, ALU.bitwise_and, ALU.bitwise_or))
                calm()
                step(V.tensor_copy(IJF[rows], IJ[rows]))
                calm()
                iota = IOTA16[rows].rearrange("p (a b n) -> p a b n", a=1, b=1).to_broadcast([n, 2, 16, 16])
                step(V.tensor_tensor(OH[rows], iota, IJF[rows].rearrange("q p (n o) -> q p n o", o=1).to_broadcast([n, 2, 16, 16]), ALU.is_equal))
                calm()
                step(V.tensor_tensor(OH[rows], OH[rows], IF[rows].rearrange("q p (o n) -> q p o n", o=1).to_broadcast([n, 2, 16, 16]), ALU.mult))
                calm()
                step(V.tensor_reduce(R01[rows], OH[rows], AXX, ALU.add))
                calm()
                step(V.scalar_tensor_tensor(eix, R01[rows, 0, :], float(NKEY), R01[rows, 1, :], ALU.mult, ALU.add))

            def prompt_sums(h, t):
                pick_sums(P, QT[:, bass.ds(2 * h, 2), t * P:(t + 1) * P])

            def prompt_experts(t):
                pick_experts(P, FVS[:, t, :], EIX[:, t, :])
                step(V.tensor_scalar(NMX[:, t:t + 1], FVS[:, t, 0:1], -1.0, None, ALU.mult))
                calm()
                dve.sem_inc(S("picked"), 1)

            def sample_sums(h):
                pick_sums(NB, SCS[0:NB, bass.ds(h * 256, 256)].rearrange("p (a n) -> p a n", a=2))

            def sample_experts(h):
                pick_experts(NB, FVT, EISF[0:NB, bass.ds(h * 16, 16)])
                step(V.tensor_copy(FVSS[0:NB, bass.ds(h * 16, 16)], FVT[0:NB, :]))

            def dots(n_, t, s0, s1):
                for s_ in range(s0, s1):
                    dve.wait_ge(S(f"u_in{s_ % 4}"), n_ * 64 + 16 * (s_ // 4 + 1))
                    g = UR[:, s_ % 4, :]
                    V.scalar_tensor_tensor(g, g, 1.0, H2[:, t, :], ALU.mult, ALU.mult, accum_out=DOT[:, t, s_:s_ + 1]).then_inc(S("dots"), 1)

            def weigh(n_, t):
                dve.wait_ge(S("gate_raw"), n_ + 1)
                step(V.reciprocal(SUMG[:, t:t + 1], SUMG[:, t:t + 1]))
                dve.wait_ge(S("gelu"), n_ + 1)
                calm()
                V.scalar_tensor_tensor(AG[:, t, :], AG[:, t, :], SUMG[:, t:t + 1], GAT[:, t, :], ALU.mult, ALU.mult).then_inc(S("weights"), 1)

            def gather_sums(n_, t):
                dve.wait_ge(S("v_used"), n_ * 16 + 16 + 8)
                for half in range(2):
                    b = banks[(t % 2) * 2 + half]
                    v = ACC[:, t, half * 512:(half + 1) * 512]
                    step(V.tensor_tensor(v, v, b[:, :], ALU.add))
                calm()
                dve.sem_inc(S("sums_free"), 1)

            def sample_gates():
                settle()
                f3 = FVSS[0:NB, :].rearrange("p (h k) -> p h k", h=PH)
                dve.sem_inc(S("sample_picks"), 1)
                step(V.tensor_copy(OH[0:NB, 0, 0, 0:8], f3[:, :, 0]))
                settle()
                V.tensor_tensor(f3, f3, wide(OH[0:NB, 0, 0, 0:8], 16), ALU.subtract).then_inc(S("sample_shift"), 1)
                dve.wait_ge(S("sample_exp"), 1)
                step(V.tensor_reduce(OH[0:NB, 0, 0, 0:8], f3, AXX, ALU.add))
                settle()
                step(V.reciprocal(OH[0:NB, 0, 0, 0:8], OH[0:NB, 0, 0, 0:8]))
                settle()
                V.tensor_tensor(f3, f3, wide(OH[0:NB, 0, 0, 0:8], 16), ALU.mult).then_inc(S("sample_picks"), 1)

            def sample_indices():
                b = full_bank(dve, "ixT")
                V.tensor_copy(IXT, b[:, 0:8]).then_inc(S("sample_ix"), 1)
                V.tensor_copy(GTT, b[:, 8:16]).then_inc(free("ixT"), 1)
            def sample_dot(t):
                dve.wait_ge(S(f"u_in{t % 4}"), 16 * (128 + t // 4 + 1))
                dve.wait_ge(S(f"h2b_in{t % 2}"), 16 * (t // 2 + 1))
                g = UR[:, t % 4, :]
                V.scalar_tensor_tensor(g, g, 1.0, H2B[:, t % 2, :], ALU.mult, ALU.mult, accum_out=DOTS[:, t:t + 1]).then_inc(S("sample_dots"), 1)

            def peer_vector(h, last):
                for t in range(TILES):
                    n_ = h * 4 + t
                    picks, more = not (last and t >= 2), not (last and t == 3)
                    if more:
                        dots(n_ + 1, (t + 1) % 4, 0, 4)
                    if picks:
                        prompt_sums(h + (1 if t >= 2 else 0), (t + 2) % 4)
                    if more:
                        dots(n_ + 1, (t + 1) % 4, 4, 8)
                    if picks:
                        prompt_experts((t + 2) % 4)
                    if more:
                        dots(n_ + 1, (t + 1) % 4, 8, 12)
                    if t == 1:
                        sample_sums(h)
                    if more:
                        dots(n_ + 1, (t + 1) % 4, 12, 16)
                        weigh(n_ + 1, (t + 1) % 4)
                    if t == 1:
                        sample_experts(h)
                    if last and t == 3:
                        sample_indices()
                        for t2 in range(4):
                            sample_dot(t2)
                    gather_sums(n_, t)
                    if last and t == 1:
                        sample_gates()

            def scores_ready(t):
                for q in range(4):
                    job_read(dve, ("score", t, q))

            scores_ready(0)
            prompt_sums(0, 0)
            prompt_experts(0)
            scores_ready(1)
            prompt_sums(0, 1)
            prompt_experts(1)
            for t in range(2, 5):
                scores_ready(t)
            dots(0, 0, 0, 16)
            weigh(0, 0)
            base = count[0]
            with dve.Fori(0, PH - 1) as h:
                clock[0] = lambda: h * LOOP_STEPS + count[0]
                peer_vector(h, False)
                assert count[0] - base == LOOP_STEPS, (count[0] - base)
            count[0] += (PH - 2) * LOOP_STEPS
            clock[0] = lambda: count[0]
            peer_vector(PH - 1, True)
            dve.wait_ge(S("g2_in"), 48)

            def finish(t, n, y):
                settle()
                step(V.tensor_tensor(y, y, X1[0:n, t, :], ALU.add))
                settle()
                V.scalar_tensor_tensor(H2[0:n, t, :], y, 1.0, y, ALU.mult, ALU.mult, accum_out=SS[0:n, t:t + 1]).then_inc(S("sumsq"), 1)
                dve.wait_ge(S("root"), 10 + t + 1)
                step(V.reciprocal(SS[0:n, 5 + t:6 + t], SS[0:n, 5 + t:6 + t]))
                settle()
                V.scalar_tensor_tensor(y, y, SS[0:n, 5 + t:6 + t], MV[0:n, 2, :], ALU.mult, ALU.mult).then_inc(S("y_ready"), 1)

            def finish_tile(t):
                step(V.tensor_tensor(ACC[:, t, :], ACC[:, t, :], MV[:, 0, :], ALU.mult))
                finish(t, P, ACC[:, t, :])

            step(V.memset(AM, 0.0))
            for t in range(NB):
                if t % 4 == 0:
                    finish_tile(t // 4)
                if t >= 4:
                    sample_dot(t)
            dve.wait_ge(S("sample_gelu"), 1)
            job_read(dve, "ixT")
            settle()
            V.tensor_tensor(AM[:, 0:64:9], DOTS, GTT, ALU.mult).then_inc(S("sample_gates"), 1)
            finish_tile(2)
            finish_tile(3)
            dve.wait_ge(S("v_used"), 32 * 16 + 8 + NB)
            ys = UR[0:NB, 0, :]
            for half in range(2):
                c = slice(half * 512, (half + 1) * 512)
                step(V.tensor_tensor(ys[:, c], banks[half][0:NB, :], MV[0:NB, 1, c], ALU.mult))
            finish(4, NB, ys)

        @block.gpsimd
        def _(pool):
            nc.gpsimd.iota(ints[:, 0, :], [[0, P]], base=0, channel_multiplier=1).then_inc(S("iota"), 1)
            nc.gpsimd.iota(ints[:, 1, :], [[1, P]], base=0, channel_multiplier=0).then_inc(S("iota"), 1)
            T = nc.gpsimd.tensor_tensor
            n = [0]

            def step(ins):
                n[0] += 1
                ins.then_inc(S("pool_steps"), 1)
                pool.wait_ge(S("pool_steps"), n[0])

            pool.wait_ge(S("pages_in"), 16)
            job_done(pool, last_job[8])
            nc.gpsimd.indirect_dma_start(LG, None, a["cache_logf"][0].rearrange("n p h -> n (p h)"),
                                         bass.IndirectOffsetOnAxis(ap=PTI, axis=0)).then_inc(S("logf_pages"), 16)
            def key_product(n):
                pages_ready(pool, n)
                pool.wait_ge(S(f"qb_in{n // 4 % 2}"), 16 * (n // 8 + 1))
                k = pages(n)
                T(k, k, QB[:, n // 4 % 2:n // 4 % 2 + 1, :].to_broadcast([P, 4, 512]), ALU.mult).then_inc(S("kprod"), 1)

            for n_ in range(EARLY):
                key_product(n_)
            job_done(pool, ("gv", 4))
            nc.gpsimd.memset(FA[0:2, :, :], 1.0).then_inc(S("frow_ones"), 1)
            nc.gpsimd.memset(FB[0:2, :, :], 1.0).then_inc(S("frow_ones"), 1)
            for g in range(3):
                if g:
                    key_product(EARLY + g - 1)
                pool.wait_ge(S("sconv_in"), 32 * (g + 1))
                pool.wait_ge(S("sample_raw"), g + 1)
                x = SRAW(g)
                step(T(SCONV(g), x, SCW[0:NB, 3, :], ALU.mult))
                for j in range(3):
                    step(T(STMP[0:NB, :], SST[0:NB, j, :], SCW[0:NB, j, :], ALU.mult))
                    step(T(SCONV(g), SCONV(g), STMP[0:NB, :], ALU.add))
                pool.sem_inc(S("sconv_done"), 1)
            SR = slice(0, 64)
            over_v = lambda v: wide(v, HD)
            over_k = lambda v: v.rearrange("p (o d) -> p o d", o=1).to_broadcast([64, HD, HD])
            for u in range(34):
                for n_ in key_groups(u):
                    if n_ >= NARROW:
                        key_product(n_)
                if u == SRULE_AT[1]:
                    pool.wait_ge(S("srule"), 2)
                    T(SSP[SR], SS0[SR], over_v(SV[SR, 1, :]), ALU.mult).then_inc(S("srule_pool"), 1)
                if u == SRULE_AT[2]:
                    pool.wait_ge(S("srule"), 3)
                    T(SSP[SR], over_v(SV[SR, 1, :]), over_k(SV[SR, 2, :]), ALU.mult).then_inc(S("srule_pool"), 1)
                if u == SRULE_AT[3]:
                    pool.wait_ge(S("srule"), 4)
                    T(SSP[SR], SS0[SR], over_v(SV[SR, 0, :]), ALU.mult).then_inc(S("srule_pool"), 1)

            def mask(i, lv):
                for hb in range(2):
                    AT, M = BATCH[hb][1], BATCH[hb][5 + lv % 2]
                    if lv == 0:
                        pool.wait_ge(S("decay_used"), 2 * i + hb + 1)
                        if i:
                            job_done(pool, ("T", i - 1, hb, 6))
                    elif lv >= 2:
                        job_done(pool, ("T", i, hb, lv - 2))
                        if lv == 2:
                            pool.wait_ge(S("eye"), 2 * i + hb + 1)
                    T(M, AT, level[:, lv:lv + 1, :].to_broadcast([P, 4, P]), ALU.mult).then_inc(S(f"level{hb}"), 1)

            def value_product(n):
                bb, q = divmod(n, 4)
                pool.wait_ge(S("probs"), 1)
                pages_ready(pool, 32 + n)
                v = pages(32 + n).rearrange("p g (h d) -> p g h d", d=HD)
                w = SC[:, :, bb, q * 4:q * 4 + 4].rearrange("p h (g o) -> p g h o", o=1).to_broadcast([P, 4, HEADS, HD])
                T(v, v, w, ALU.mult).then_inc(S("kprod"), 1)

            for i in range(TILES):
                mask(i, 0)
                mask(i, 1)
                for lv in range(7):
                    for n_ in value_groups(7 * i + lv):
                        value_product(n_)
                    if lv + 2 < 7:
                        mask(i, lv + 2)
            nc.gpsimd.iota(IOTAI, [[1, 16]], base=0, channel_multiplier=0).then_inc(S("iota"), 1)

            pu, pv = a["peer_u"][0], a["peer_v"][0]

            def ready(sem, value):
                pool.wait_ge(S(sem), value)
                pool.sem_inc(S("pool_pace"), 1)

            def gather(dst, table, idx, sem):
                nc.gpsimd.indirect_dma_start(dst, None, table, bass.IndirectOffsetOnAxis(ap=idx, axis=0)).then_inc(S(sem), 16)

            pool.sem_inc(S("v_used"), 8)
            pool.sem_inc(S("sums_free"), 2)
            job_done(pool, last_job[-1])
            job_done(pool, last_job[-2])
            pool.wait_ge(S("picked"), 1)
            for s_ in range(16):
                if s_ >= 4:
                    pool.wait_ge(S("dots"), s_ - 3)
                gather(UR[:, s_ % 4, :], pu, EIX[:, 0, s_:s_ + 1], f"u_in{s_ % 4}")

            def peer_gathers(h, last):
                for t in range(TILES):
                    n_ = h * 4 + t
                    more = not (last and t == 3)
                    if more:
                        ready("picked", n_ + 2)
                    for s_ in range(16):
                        if more:
                            ready("dots", n_ * 16 + 16 + s_ - 3)
                            gather(UR[:, s_ % 4, :], pu, EIX[:, (t + 1) % 4, s_:s_ + 1], f"u_in{s_ % 4}")
                        ready("v_used", n_ * 16 + s_ + 1)
                        gather(VR[:, s_ % 8, :], pv, EIX[:, t, s_:s_ + 1], f"v_in{s_ % 8}")
                        if not more and s_ == 8:
                            pool.wait_ge(S("sample_ix"), 1)
                            pool.wait_ge(S("dots"), 32 * 16)
                            for t2 in range(4):
                                gather(UR[:, t2, :], pu, IXT[:, t2:t2 + 1], f"u_in{t2}")

            with pool.Fori(0, PH - 1) as h:
                peer_gathers(h, False)
            peer_gathers(PH - 1, True)
            for t in range(4, NB):
                pool.wait_ge(S("sample_dots"), t - 3)
                gather(UR[:, t % 4, :], pu, IXT[:, t:t + 1], f"u_in{t % 4}")
            for t in range(NB):
                pool.wait_ge(S("v_used"), 32 * 16 + t + 1)
                gather(VR[:, t, :], pv, IXT[:, t:t + 1], f"v_in{t}")

        @block.sync
        def _(sp):
            def load(dst, src, sem, **k):
                sp.dma_start(dst, src, **k).then_inc(S(sem), 16)

            stored = {}

            def store(dst, src, sem):
                sp.dma_start(dst, src, allow_slow_non_contiguous=src.shape[-1] == 1).then_inc(S(sem), 16)
                stored[sem] = stored.get(sem, 0) + 16

            load(C9[0:1, :], a["c_prompt"], "c_in")
            load(C9[1:9, :], a["c_sample"], "c_in")
            load(CWN, a["conv_w"][0].rearrange("j (b c) -> (j b) c", c=P), "conv_w_in")

            def chunk(n):
                name, src = chunks[n]
                if before[n] is not None:
                    job_done(sp, last_job[before[n]])
                load(slot(name), src, f"ring{slot_of[n]}_loaded")

            def bmod(j):
                if j >= 2:
                    sp.wait_ge(S("mod_row"), j - 1)
                load(BMR(j), a["b_mod"][:, j * 512:(j + 1) * 512].to_broadcast([9, 512]), f"bmod{j % 2}")

            def mod_store(j):
                sp.wait_ge(S("mod_row"), j + 1)
                store(mod_d[:, j * 512:(j + 1) * 512], MR(j), f"mod_out{j % 2}")

            def x_load(t):
                if t >= 2:
                    sp.wait_ge(S("h_ready"), t - 1)
                src = a["x_prompt"][0, t * P:(t + 1) * P, :] if t < 4 else a["x_sample"][:, 0, :]
                load(XR[0:(P if t < 4 else NB), t % 2, :], src, f"x_in{t % 2}")

            chunk(0)
            bmod(0)
            bmod(1)
            chunk(1)
            chunk(2)
            load(BIAS[:, 0, :], a["dt_bias"].to_broadcast([P, 8]), "bias_in")
            load(BIAS[:, 1, :], a["fox_fb"].to_broadcast([P, 8]), "bias_in")
            load(BIAS[:, 2, :], a["a_log"].to_broadcast([P, 8]), "bias_in")
            load(PTI, a["page_table"].rearrange("b (g o) -> (b g) o", o=1).bitcast(U32), "pages_in", allow_slow_non_contiguous=True)
            load(PTB, a["page_table"].rearrange("(o b) g -> o (b g)", o=1), "table_in")
            x_load(0)
            x_load(1)
            for j in range(4):
                chunk(j + 3)
                mod_store(j)
                if j + 2 < 4:
                    bmod(j + 2)
            sp.wait_ge(S("mod_out0"), 32)
            sp.wait_ge(S("mod_out1"), 32)
            for i, at in enumerate((0, D_MODEL)):
                load(MV[:, i, :], mod_d[0:1, at:at + D_MODEL].to_broadcast([P, D_MODEL]), "mv_prompt")
            for i, at in enumerate((0, D_MODEL)):
                load(MV[0:NB, 2 + i, :], mod_d[1:9, at:at + D_MODEL], "mv_sample")
            for t in range(2, 5):
                x_load(t)

            def frow_load(h):
                if h >= 2:
                    job_done(sp, ("sc", 4 * (h - 2) + 3))
                load(FA[1:2, h % 2, :], frow_d[0, h:h + 1, :], f"frow_in{h % 2}")
                load(FB[0:1, h % 2, :], frow_d[1, h:h + 1, :], f"frow_in{h % 2}")

            def page_numbers(n):
                return [sp.value_load(PTB[0:1, 4 * n + g:4 * n + g + 1], min_val=0, max_val=a["cache_k"].shape[1] - 1) for g in range(4)]

            def cache_group(cache, m, numbers):
                for g in range(4):
                    load(pages(m)[:, g, :], a[cache][0, bass.ds(numbers[g], 1)].rearrange("o p h d -> p (o h d)"), f"kv_in{buffer_of(m)}")

            def key_pages(n):
                numbers = page_numbers(n)
                b, q = divmod(n, 4)
                if q == 0:
                    if b >= 2:
                        sp.wait_ge(S("kprod"), 4 * (b - 1))
                    load(QB[:, b % 2, :], samp_d[b:b + 1, 4, :].to_broadcast([P, 512]), f"qb_in{b % 2}")
                if group_before(n) is not None:
                    sp.wait_ge(S("kred"), group_before(n) + 1)
                cache_group("cache_k", n, numbers)

            def sconv_load(g):
                if g:
                    sp.wait_ge(S("sconv_done"), g)
                load(SST[0:NB, :, :], a["state_conv"][0, :, :, g * 512:(g + 1) * 512], "sconv_in")
                load(SCW[0:NB, :, :], a["conv_w"][:, :, g * 512:(g + 1) * 512].to_broadcast([NB, 4, 512]), "sconv_in")

            for n in range(7, 11):
                chunk(n)
            for t in range(TILES):
                job_read(sp, ("fv", t))
                store(o["v_prompt"][0, 0, t * P:(t + 1) * P].rearrange("t h d -> t (h d)"), VT[:, t, :], "results_out")
            job_read(sp, ("fv", 4))
            store(o["v_sample"][0, :, 0].rearrange("b h d -> b (h d)"), PS[0:NB, COL_FV:COL_FV + 512], "samples_out")
            for t in range(TILES):
                sp.wait_ge(S("ktok_copied"), t + 1)
                store(o["k_prompt"][0, 0, t * P:(t + 1) * P].rearrange("t h d -> t (h d)"), KO[:, t % 2, :], f"k_out{t % 2}")
            sp.wait_ge(S("gates_ready"), 1)
            store(o["logf_prompt"][0, 0].rearrange("(t p) h -> p t h", p=P), LOGF[:, 0:4, :], "results_out")
            store(o["logf_sample"][0, :, 0], LOGF[0:NB, 4, :], "results_out")
            sp.wait_ge(S("frows"), 1)
            store(frow_d[0], FR[0:8, :], "frow_out")
            store(frow_d[1], NFR[0:8, :], "frow_out")
            job_read(sp, ("fq", 4))
            store(samp_d[:, 4, :], PS[0:NB, COL_FQ:COL_FQ + 512], "samp_out")
            sp.wait_ge(S("samp_out"), 16)
            sp.wait_ge(S("table_in"), 16)
            job_done(sp, last_job[8])
            for n in range(EARLY):
                if n == 4:
                    chunk(11)
                key_pages(n)
            chunk(12)
            job_read(sp, ("fk", 4))
            store(o["k_sample"][0, :, 0].rearrange("b h d -> b (h d)"), PS[0:NB, COL_FK:COL_FK + 512], "samples_out")
            sp.wait_ge(S("frow_out"), 32)
            sp.wait_ge(S("frow_ones"), 2)
            frow_load(0)
            frow_load(1)
            sp.wait_ge(S("sample_raw"), 3)
            sp.wait_ge(S("k_out0"), 32)
            sp.wait_ge(S("k_out1"), 32)
            job_done(sp, ("cvT", 11))
            sconv_load(0)
            bmod(4)
            bmod(5)
            key_pages(EARLY)
            sconv_load(1)
            key_pages(EARLY + 1)
            sconv_load(2)
            frow_load(2)
            store(o["conv_sample"][0, :, 0:2], a["state_conv"][0, :, 1:3], "samples_out")
            store(o["conv_sample"][0, :, 2], PS[0:NB, 0:CONV], "samples_out")
            sp.wait_ge(S("tail_out"), 3)
            store(o["conv_prompt"][0, 0], TAILO[0:3, :], "samples_out")
            sp.wait_ge(S("sconv_silu"), 1)
            for n in range(3):
                store(samp_d[:, n, :], PSC[0:NB, n * 512:(n + 1) * 512], "samp_out")
            store(samp_d[:, 3, :], PS[0:NB, COL_Z:COL_Z + 512], "samp_out")
            store(sgate_d[0], BETA[0:NB, 4, :], "samp_out")
            store(sgate_d[1], G[0:NB, 4, :], "samp_out")
            sp.wait_ge(S("new_score"), 1)
            store(sgate_d[2], SN[0:NB, :], "samp_out")
            for sem in ("samp_out", "frow_out", "samples_out"):
                sp.wait_ge(S(sem), stored[sem])
            sp.sem_inc(S("psbuf_free"), 1)

            by_head = "b (h d) -> b h d"
            load(SS0[0:64].rearrange("p k v -> p (k v)"), a["state_delta"][0].rearrange("b h k v -> (b h) (k v)"), "srule_in")
            for n in range(4):
                load(SV[0:64, n, :], samp_d[:, n, :].rearrange(by_head, h=8), "srule_in")
            load(SSM[0:64, 0:1], sgate_d[0].rearrange("b (h o) -> b h o", o=1), "srule_in", allow_slow_non_contiguous=True)
            load(SSM[0:64, 1:2], sgate_d[1].rearrange("b (h o) -> b h o", o=1), "srule_in", allow_slow_non_contiguous=True)
            load(NW, a["gdn_norm_w"].to_broadcast([P, HD]), "srule_in")
            load(LNB, o["logf_sample"][0, :, 0].rearrange("(o b) h -> o (b h)", o=1).to_broadcast([P, 64]), "new_in")
            load(SC[0:1, :, :, 16], sgate_d[2:3].rearrange("o b h -> o h b"), "new_in", allow_slow_non_contiguous=True)

            def next_mod(m):
                mod_store(m)
                if m + 2 < 12:
                    bmod(m + 2)
                chunk(m + 9)

            mods, turns = 4, [3, False]
            unit_of = {n: u for u in range(34) for n in key_groups(u)}
            for n in range(NARROW, 32):
                past = unit_of[n - 4] if n >= NARROW + 4 else 0
                while turns[0] < 8 and past >= 4 * turns[0] - 5:
                    frow_load(turns[0])
                    turns[0] += 1
                if mods < 7 and past > 6 + 8 * (mods - 4):
                    next_mod(mods)
                    mods += 1
                if past > SRULE_AT[3] and not turns[1]:
                    turns[1] = True
                    sp.wait_ge(S("srule"), 4)
                    store(o["delta_sample"][0].rearrange("b h k v -> (b h) (k v)"), SS0[0:64].rearrange("p k v -> p (k v)"), "srule_stored")
                key_pages(n)
            next_mod(mods)
            mods += 1
            sp.wait_ge(S("srule"), 6)
            store(samp_d[:, 5, :].rearrange(by_head, h=8), SV[0:64, 4, :], "srule_stored")
            sp.wait_ge(S("srule_stored"), 32)
            load(OGS, samp_d[:, 5, :], "ogs_in")
            level_of = {n: at for at in range(28) for n in value_groups(at)}
            for n in range(32):
                b, q = divmod(n, 4)
                numbers = page_numbers(n)
                if n == 0:
                    job_done(sp, ("fo", 31))
                last = group_before(32 + n)
                while last is not None and last >= 32 and mods < 12 and level_of[last - 32] > 7 * (mods - 8) + 6:
                    next_mod(mods)
                    mods += 1
                if last is not None:
                    sp.wait_ge(S("kred"), last + 1)
                cache_group("cache_v", 32 + n, numbers)
                if q == 0:
                    if b >= 2:
                        job_done(sp, ("pv", 4 * b - 5))
                    load(VNEW[:, (b % 2) * 512:(b % 2) * 512 + 512], o["v_sample"][0, b:b + 1, 0].rearrange("b h d -> b (h d)"), f"vnew_in{b % 2}")
            for m in range(mods, 12):
                next_mod(m)
            sp.wait_ge(S("gdn_out"), 4)
            sp.wait_ge(S("state"), 9)
            for r_ in range(2):
                store(o["delta_prompt"][0, 0].rearrange("(j a) d e -> a d j e", a=2)[r_], ST[r_ * HD:r_ * HD + HD, :, r_ * HD:r_ * HD + HD], "results_out")
            job_done(sp, ("dS", 3))
            load(X1[:, 0:4, :], a["x_prompt"][0].rearrange("(t p) d -> p t d", p=P), "x1_in")
            load(X1[0:NB, 4, :], a["x_sample"][:, 0, :], "x1_in")
            load(G1[0], mod_d[0:1, 2 * D_MODEL:3 * D_MODEL].to_broadcast([P, D_MODEL]), "g1_in")
            load(G1[1], mod_d[1:9, 2 * D_MODEL:3 * D_MODEL], "g1_in")
            sp.wait_ge(S("mod_out0"), 96)
            sp.wait_ge(S("mod_out1"), 96)
            job_done(sp, ("pv", 31))
            load(KN, a["peer_subkeys"][0].rearrange("h p n c -> n (h p) c"), "keys_in")
            for i in range(2):
                at = (3 + i) * D_MODEL
                load(MVP2[i], mod_d[0:1, at:at + D_MODEL].to_broadcast([P, D_MODEL]), "mv2_in")
                load(MVS2[0:NB, i, :], mod_d[1:9, at:at + D_MODEL], "mv2_in")
            for n in range(21, 25):
                chunk(n)
            sp.wait_ge(S("x1_part"), 10)
            load(MV[:, 0, :], mod_d[0:1, 5 * D_MODEL:6 * D_MODEL].to_broadcast([P, D_MODEL]), "g2_in")
            load(MV[0:NB, 1, :], mod_d[1:9, 5 * D_MODEL:6 * D_MODEL], "g2_in")
            sp.wait_ge(S("h_ready"), 10)
            load(MV[:, 2, :], a["final_norm_w"].rearrange("(o d) -> o d", o=1).to_broadcast([P, D_MODEL]), "g2_in")
            store(h2s_d, H2[0:NB, 4, :], "h2s_out")
            sp.wait_ge(S("h2s_out"), 16)
            sp.wait_ge(S("sample_picks"), 1)
            for t in range(NB):
                if t >= 2:
                    sp.wait_ge(S("sample_dots"), t - 1)
                load(H2B[:, t % 2, :], h2s_d[t:t + 1, :].to_broadcast([P, D_MODEL]), f"h2b_in{t % 2}")
            for t in range(TILES):
                sp.wait_ge(S("y_ready"), t + 1)
                store(o["y_prompt"][0, t * P:(t + 1) * P, :], ACC[:, t, :], "results_out")
            sp.wait_ge(S("y_ready"), 5)
            store(o["y_sample"][:, 0, :], UR[0:NB, 0, :], "results_out")
            for sem, n in stored.items():
                sp.wait_ge(S(sem), n)


_OUTS = [("y_prompt", (1, SEQ, D_MODEL)), ("y_sample", (NB, 1, D_MODEL)),
         ("k_prompt", (1, 1, SEQ, HEADS, HD)), ("v_prompt", (1, 1, SEQ, HEADS, HD)), ("logf_prompt", (1, 1, SEQ, HEADS)),
         ("conv_prompt", (1, 1, 3, CONV)), ("delta_prompt", (1, 1, HEADS, HD, HD)),
         ("k_sample", (1, NB, 1, HEADS, HD)), ("v_sample", (1, NB, 1, HEADS, HD)), ("logf_sample", (1, NB, 1, HEADS)),
         ("conv_sample", (1, NB, 3, CONV)), ("delta_sample", (1, NB, HEADS, HD, HD))]


def kernel(**inputs):
    import concourse.bacc as _bacc
    import numpy as _np
    from concourse import mybir as _mybir
    from concourse.bass_utils import run_bass_kernel_spmd as _run

    nc = _bacc.Bacc("TRN2", target_bir_lowering=False, num_devices=1)
    arrays, ins, outs = {}, {}, {}
    for name, value in inputs.items():
        v = _np.ascontiguousarray(value)
        arrays["in_" + name] = v
        ins[name] = nc.dram_tensor("in_" + name, v.shape, _mybir.dt.from_np(v.dtype), kind="ExternalInput").ap()
    for name, shape in _OUTS:
        outs[name] = nc.dram_tensor("out_" + name, shape, _mybir.dt.float32, kind="ExternalOutput").ap()
    hybrid_decoder_step(nc, ins, outs)
    r = _run(nc, [arrays], core_ids=[0])
    return tuple(r.results[0]["out_" + name] for name, _ in _OUTS)
```
